# Optimizing a Trainium2 kernel written in Bass

```python
import math
import jax, jax.numpy as jnp
from jax import lax
import numpy as np

D_MODEL = 1024
BATCH = 1
SEQ = 512
DEPTH = 1

MEM_LEN = 256
EPS = 1e-6
CONV_K = 4
GDN_HEADS = 8
GDN_DK = 128
GDN_DV = 128
GDN_DIM = GDN_HEADS * GDN_DV
GDN_CHUNK = 64
GDN_COLS = 4 * GDN_DIM + 2 * GDN_HEADS
SSM_DIM = D_MODEL
SSM_HEADDIM = 64
SSM_HEADS = SSM_DIM // SSM_HEADDIM
SSM_GROUPS = 2
SSM_HPG = SSM_HEADS // SSM_GROUPS
SSM_STATE = 128
SSM_CHUNK = 128
SSM_BC = SSM_GROUPS * SSM_STATE
SSM_COLS = 2 * SSM_DIM + 2 * SSM_BC + SSM_HEADS
MIX_DIM = GDN_DIM + SSM_DIM
IN_COLS = GDN_COLS + SSM_COLS
MEM_HEADS = 4
MEM_HEADDIM = D_MODEL // MEM_HEADS
D_FF = 4 * D_MODEL

kernel_name = "hybrid_gdn_ssd_parallel_heads_memxattn"

def rmsnorm(x, w):
    xf = x.astype(jnp.float32)
    y = xf * lax.rsqrt(jnp.mean(xf * xf, axis=-1, keepdims=True) + EPS)
    return (y * w.astype(jnp.float32)).astype(x.dtype)

def l2norm(x):
    return x * lax.rsqrt(jnp.sum(x * x, axis=-1, keepdims=True) + EPS)

def causal_depthwise_conv(x, w, b=None):
    K, C = w.shape
    xp = jnp.pad(x, ((0, 0), (K - 1, 0), (0, 0)))
    y = lax.conv_general_dilated(xp, w[:, None, :].astype(x.dtype), window_strides=(1,),
                                 padding='VALID', dimension_numbers=('NWC', 'WIO', 'NWC'),
                                 feature_group_count=C)
    if b is not None:
        y = y + b.astype(x.dtype)
    return y

def gated_delta_rule_chunked(q, k, v, g, beta):
    Bsz, T, H, Dk = q.shape
    Dv = v.shape[-1]
    C = GDN_CHUNK
    N = T // C
    q = l2norm(q) * (Dk ** -0.5)
    k = l2norm(k)

    def chunks(t):
        return t.reshape(Bsz, N, C, H, -1).transpose(0, 3, 1, 2, 4)

    q, k, v = chunks(q), chunks(k), chunks(v)
    g = g.reshape(Bsz, N, C, H).transpose(0, 3, 1, 2)
    beta = beta.reshape(Bsz, N, C, H).transpose(0, 3, 1, 2)
    g_cs = jnp.cumsum(g, axis=-1)
    causal = jnp.tril(jnp.ones((C, C), dtype=bool))
    strict = jnp.tril(jnp.ones((C, C), dtype=bool), -1)
    decay = jnp.exp(jnp.where(causal, g_cs[..., :, None] - g_cs[..., None, :], -jnp.inf))
    k_beta = k * beta[..., None]
    v_beta = v * beta[..., None]
    Lmat = jnp.where(strict, jnp.einsum('bhncd,bhnsd->bhncs', k_beta, k) * decay, 0.0)
    Amat = Lmat + jnp.eye(C, dtype=jnp.float32)
    rhs = jnp.concatenate([v_beta, k_beta * jnp.exp(g_cs)[..., None]], axis=-1)
    sol = lax.linalg.triangular_solve(Amat, rhs, left_side=True, lower=True, unit_diagonal=True)
    u = sol[..., :Dv]
    w = sol[..., Dv:]
    attn_intra = jnp.einsum('bhncd,bhnsd->bhncs', q, k) * decay
    q_dec = q * jnp.exp(g_cs)[..., None]
    k_dec = k * jnp.exp(g_cs[..., -1:] - g_cs)[..., None]
    chunk_decay = jnp.exp(g_cs[..., -1])

    def step(S, inp):
        qd, kd, u_c, w_c, a_c, cd = inp
        v_new = u_c - jnp.einsum('bhcd,bhde->bhce', w_c, S)
        o = jnp.einsum('bhcd,bhde->bhce', qd, S) + jnp.einsum('bhcs,bhse->bhce', a_c, v_new)
        S = S * cd[..., None, None] + jnp.einsum('bhcd,bhce->bhde', kd, v_new)
        return S, o

    mv = lambda t: jnp.moveaxis(t, 2, 0)
    S0 = jnp.zeros((Bsz, H, Dk, Dv), jnp.float32)
    _, o = lax.scan(step, S0, (mv(q_dec), mv(k_dec), mv(u), mv(w), mv(attn_intra), mv(chunk_decay)))
    return o.transpose(1, 0, 3, 2, 4).reshape(Bsz, T, H, Dv)

def gdn_mixer(p, conv_w, a_log, dt_bias, norm_w):
    Bsz, T, _ = p.shape
    qkv = jax.nn.silu(causal_depthwise_conv(p[..., :3 * GDN_DIM], conv_w))
    z = p[..., 3 * GDN_DIM:4 * GDN_DIM]
    b_raw = p[..., 4 * GDN_DIM:4 * GDN_DIM + GDN_HEADS].astype(jnp.float32)
    a_raw = p[..., 4 * GDN_DIM + GDN_HEADS:].astype(jnp.float32)
    qkv = qkv.astype(jnp.float32)
    q = qkv[..., :GDN_DIM].reshape(Bsz, T, GDN_HEADS, GDN_DK)
    k = qkv[..., GDN_DIM:2 * GDN_DIM].reshape(Bsz, T, GDN_HEADS, GDN_DK)
    v = qkv[..., 2 * GDN_DIM:].reshape(Bsz, T, GDN_HEADS, GDN_DV)
    beta = jax.nn.sigmoid(b_raw)
    g = -jnp.exp(a_log.astype(jnp.float32)) * jax.nn.softplus(a_raw + dt_bias.astype(jnp.float32))
    o = gated_delta_rule_chunked(q, k, v, g, beta)
    zf = z.astype(jnp.float32).reshape(Bsz, T, GDN_HEADS, GDN_DV)
    o = rmsnorm(o, norm_w) * jax.nn.silu(zf)
    return o.reshape(Bsz, T, GDN_DIM).astype(p.dtype)

def ssd_chunked(x, dt, A, Bm, Cm):
    Bsz, T, H, P = x.shape
    L = SSD_L = SSM_CHUNK
    Nc = T // L
    G, J, N = SSM_GROUPS, SSM_HPG, SSM_STATE
    xdt = (x * dt[..., None]).reshape(Bsz, Nc, L, G, J, P)
    a = (dt * A).reshape(Bsz, Nc, L, H).transpose(0, 3, 1, 2)
    Bc = Bm.reshape(Bsz, Nc, L, G, N)
    Cc = Cm.reshape(Bsz, Nc, L, G, N)
    a_cs = jnp.cumsum(a, axis=-1)
    causal = jnp.tril(jnp.ones((L, L), dtype=bool))
    seg = jnp.exp(jnp.where(causal, a_cs[..., :, None] - a_cs[..., None, :], -jnp.inf))
    CB = jnp.einsum('bclgn,bcsgn->bgcls', Cc, Bc)
    scores = seg.reshape(Bsz, G, J, Nc, L, L) * CB[:, :, None]
    y_diag = jnp.einsum('bgjcls,bcsgjp->bclgjp', scores, xdt)
    decay_states = jnp.exp(a_cs[..., -1:] - a_cs).reshape(Bsz, G, J, Nc, L)
    states = jnp.einsum('bclgn,bgjcl,bclgjp->bcgjpn', Bc, decay_states, xdt)
    chunk_decay = jnp.exp(a_cs[..., -1]).reshape(Bsz, G, J, Nc)

    def step(h, inp):
        st, dec = inp
        return h * dec[..., None, None] + st, h

    h0 = jnp.zeros((Bsz, G, J, P, N), jnp.float32)
    _, prev = lax.scan(step, h0, (jnp.moveaxis(states, 1, 0), jnp.moveaxis(chunk_decay, 3, 0)))
    prev = jnp.moveaxis(prev, 0, 1)
    y_off = jnp.einsum('bclgn,bcgjpn,bgjcl->bclgjp', Cc, prev,
                       jnp.exp(a_cs).reshape(Bsz, G, J, Nc, L))
    return (y_diag + y_off).reshape(Bsz, T, H, P)

def ssd_mixer(p, conv_w, conv_b, a_log, dt_bias, d_skip, norm_w):
    Bsz, T, _ = p.shape
    z = p[..., :SSM_DIM]
    xbc = jax.nn.silu(causal_depthwise_conv(p[..., SSM_DIM:2 * SSM_DIM + 2 * SSM_BC], conv_w, conv_b))
    dt_raw = p[..., 2 * SSM_DIM + 2 * SSM_BC:].astype(jnp.float32)
    xbc = xbc.astype(jnp.float32)
    xs = xbc[..., :SSM_DIM].reshape(Bsz, T, SSM_HEADS, SSM_HEADDIM)
    Bm = xbc[..., SSM_DIM:SSM_DIM + SSM_BC].reshape(Bsz, T, SSM_GROUPS, SSM_STATE)
    Cm = xbc[..., SSM_DIM + SSM_BC:].reshape(Bsz, T, SSM_GROUPS, SSM_STATE)
    dt = jax.nn.softplus(dt_raw + dt_bias.astype(jnp.float32))
    A = -jnp.exp(a_log.astype(jnp.float32))
    y = ssd_chunked(xs, dt, A, Bm, Cm) + xs * d_skip.astype(jnp.float32)[:, None]
    yg = (y.reshape(Bsz, T, SSM_DIM) * jax.nn.silu(z.astype(jnp.float32)))
    yg = yg.reshape(Bsz, T, SSM_GROUPS, SSM_DIM // SSM_GROUPS)
    yg = yg * lax.rsqrt(jnp.mean(yg * yg, axis=-1, keepdims=True) + EPS)
    yg = yg.reshape(Bsz, T, SSM_DIM) * norm_w.astype(jnp.float32)
    return yg.astype(p.dtype)

def memory_cross_attention(h, m, wq, wk, wv, wo):
    Bsz, T, _ = h.shape
    M = m.shape[1]
    q = (h @ wq).reshape(Bsz, T, MEM_HEADS, MEM_HEADDIM)
    k = (m @ wk).reshape(Bsz, M, MEM_HEADS, MEM_HEADDIM)
    v = (m @ wv).reshape(Bsz, M, MEM_HEADS, MEM_HEADDIM)
    s = jnp.einsum('bthd,bmhd->bhtm', q, k).astype(jnp.float32) * (MEM_HEADDIM ** -0.5)
    pr = jax.nn.softmax(s, axis=-1).astype(v.dtype)
    o = jnp.einsum('bhtm,bmhd->bthd', pr, v).reshape(Bsz, T, D_MODEL)
    return o @ wo

def _inv_softplus_dt(key, n):
    dt = jnp.exp(jax.random.uniform(key, (n,), minval=math.log(1e-3), maxval=math.log(1e-1)))
    return dt + jnp.log(-jnp.expm1(-dt))

def setup_inputs(seed: int = 0) -> dict:
    key = jax.random.key(seed)
    ks = jax.random.split(key, 26)
    nrm = lambda k, shape, s: jax.random.normal(k, shape, jnp.float32) * s
    gain = lambda k, n: 1.0 + 0.02 * jax.random.normal(k, (n,), jnp.float32)
    return {
        "x": nrm(ks[0], (BATCH, SEQ, D_MODEL), 1.0),
        "mem": nrm(ks[1], (BATCH, MEM_LEN, D_MODEL), 1.0),
        "norm1_w": gain(ks[2], D_MODEL),
        "w_in": nrm(ks[3], (D_MODEL, IN_COLS), D_MODEL ** -0.5),
        "gdn_conv_w": nrm(ks[4], (CONV_K, 3 * GDN_DIM), CONV_K ** -0.5),
        "gdn_a_log": jnp.log(jax.random.uniform(ks[5], (GDN_HEADS,), minval=1.0, maxval=16.0)),
        "gdn_dt_bias": _inv_softplus_dt(ks[6], GDN_HEADS),
        "gdn_norm_w": gain(ks[7], GDN_DV),
        "ssm_conv_w": nrm(ks[8], (CONV_K, SSM_DIM + 2 * SSM_BC), CONV_K ** -0.5),
        "ssm_conv_b": nrm(ks[9], (SSM_DIM + 2 * SSM_BC,), 0.02),
        "ssm_a_log": jnp.log(jax.random.uniform(ks[10], (SSM_HEADS,), minval=1.0, maxval=16.0)),
        "ssm_dt_bias": _inv_softplus_dt(ks[11], SSM_HEADS),
        "ssm_d": gain(ks[12], SSM_HEADS),
        "ssm_norm_w": gain(ks[13], SSM_DIM),
        "w_out": nrm(ks[14], (MIX_DIM, D_MODEL), MIX_DIM ** -0.5),
        "norm2_w": gain(ks[15], D_MODEL),
        "mem_norm_w": gain(ks[16], D_MODEL),
        "wq_mem": nrm(ks[17], (D_MODEL, D_MODEL), D_MODEL ** -0.5),
        "wk_mem": nrm(ks[18], (D_MODEL, D_MODEL), D_MODEL ** -0.5),
        "wv_mem": nrm(ks[19], (D_MODEL, D_MODEL), D_MODEL ** -0.5),
        "wo_mem": nrm(ks[20], (D_MODEL, D_MODEL), D_MODEL ** -0.5),
        "norm3_w": gain(ks[21], D_MODEL),
        "w_up": nrm(ks[22], (D_MODEL, D_FF), D_MODEL ** -0.5),
        "w_down": nrm(ks[23], (D_FF, D_MODEL), D_FF ** -0.5),
        "final_norm_w": gain(ks[24], D_MODEL),
    }

def reference(x, mem, norm1_w, w_in, gdn_conv_w, gdn_a_log, gdn_dt_bias, gdn_norm_w,
              ssm_conv_w, ssm_conv_b, ssm_a_log, ssm_dt_bias, ssm_d, ssm_norm_w, w_out,
              norm2_w, mem_norm_w, wq_mem, wk_mem, wv_mem, wo_mem, norm3_w, w_up, w_down,
              final_norm_w):
    m = rmsnorm(mem, mem_norm_w)
    for _ in range(DEPTH):
        h = rmsnorm(x, norm1_w)
        p = h @ w_in
        o_a = gdn_mixer(p[..., :GDN_COLS], gdn_conv_w, gdn_a_log, gdn_dt_bias, gdn_norm_w)
        o_b = ssd_mixer(p[..., GDN_COLS:], ssm_conv_w, ssm_conv_b, ssm_a_log, ssm_dt_bias,
                        ssm_d, ssm_norm_w)
        x = x + jnp.concatenate([o_a, o_b], axis=-1) @ w_out
        x = x + memory_cross_attention(rmsnorm(x, norm2_w), m, wq_mem, wk_mem, wv_mem, wo_mem)
        u = jax.nn.relu(rmsnorm(x, norm3_w) @ w_up)
        x = x + (u * u) @ w_down
    return rmsnorm(x, final_norm_w)


_drawn_inputs = setup_inputs


def setup_inputs(seed=0):
    import zlib

    import numpy as np

    out = dict(_drawn_inputs(seed))
    spreads = {}
    factors = {'gdn_norm_w': 8.0,
     'ssm_conv_b': 3.402,
     'ssm_d': 7.774,
     'ssm_norm_w': 4.547,
     'norm2_w': 8.0,
     'mem_norm_w': 8.0,
     'norm3_w': 9.615,
     'final_norm_w': 8.214}
    for name, (base, spread) in spreads.items():
        noise = np.random.default_rng([zlib.crc32(name.encode()), seed]).standard_normal(out[name].shape)
        drawn = base * np.exp(spread * noise) if base else spread * noise
        out[name] = __import__('jax').numpy.asarray(drawn.astype(out[name].dtype))
    for name, factor in factors.items():
        out[name] = (out[name] * factor).astype(out[name].dtype)
    return out
```

```python
from contextlib import ExitStack

import concourse.bass as bass
import numpy as np
from concourse import mybir

F32 = mybir.dt.float32
F32R = mybir.dt.float32r
BF16 = mybir.dt.bfloat16
ALU = mybir.AluOpType
ACT = mybir.ActivationFunctionType
AX = mybir.AxisListType

P = 128
D = 1024
T = 512
M = 256
KT = D // P
TT = T // P
MT = M // P
HALF = 512
EPS = 1e-6
TAPS = 4
HG = 8
GDN = HG * P
GDN_COLS = 4 * GDN + 2 * HG
HS = 16
HP = 64
XT = D // P
GROUPS = 2
BC = GROUPS * P
HEADS = HG + HS
MIX = (GDN + D) // P
FF = 4 * D
FT = FF // P
AH = 4
HD = D // AH
LEVELS = 7
SLOTS = 4
RAW_SLOTS = 2
SLAB = 1024

S_GDN = 0
S_BC = S_GDN + 4 * HG
S_XZ = S_BC + 4
S_OUT = S_XZ + 2 * XT
S_WK = S_OUT + MIX
S_WV = S_WK + KT
S_WQ = S_WV + KT
S_WO = S_WQ + KT
S_UP = S_WO + KT
S_DOWN = S_UP + FT
S_END = S_DOWN + FT

C_ID, C_TRI, C_ONES, C_VEC, C_MASK = 0, 1, 2, 3, 4
NCONST = C_MASK + LEVELS
V_CB, V_NW, V_GN, VROWS = 0, 12, 20, 21
G_G, G_NEG, G_NEXP, G_DEC, G_CD, G_BETA, KINDS = 0, 1, 2, 3, 4, 5, 6


def constants():
    c = np.zeros((P, NCONST, P), np.float32)
    s, t = np.arange(P)[:, None], np.arange(P)[None, :]
    c[:, C_ID] = s == t
    c[:, C_TRI] = s <= t
    c[:, C_ONES] = 1.0
    c[:, C_VEC, 0] = 1.0 / P
    c[:, C_VEC, 1] = EPS * P
    c[:, C_VEC, 2] = 1.0
    for l in range(LEVELS):
        c[:, C_MASK + l] = ((s >> (l + 1)) == (t >> (l + 1))) & ((s >> l) + 1 == (t >> l))
    return c


def neg_mask():
    m = np.zeros((P, 1 + TT, P), np.float32)
    s, t = np.arange(P)[:, None], np.arange(P)[None, :]
    m[:, 0] = s == t
    m[:, 1:] = np.where(s > t, -1e30, 0.0)[:, None, :]
    return m


def need(eng, sem, n):
    if isinstance(n, int) and n <= 0:
        return
    eng.wait_ge(sem, n)


def layer(nc, a, out):
    with ExitStack() as ctx:
        def sb(name, shape, dt=F32):
            return ctx.enter_context(nc.sbuf_tensor(name, shape, dt))

        def sem(name):
            return ctx.enter_context(nc.semaphore(name))

        B = [ctx.enter_context(nc.psum_tensor(f"bank{i}", [P, HALF], F32)) for i in range(8)]

        raw = sb("raw", [P, RAW_SLOTS, SLAB])
        w_hi = sb("w_hi", [P, SLOTS, SLAB], F32R)
        w_lo = sb("w_lo", [P, SLOTS, SLAB], F32R)
        x_res = sb("x_res", [P, TT, D])
        h_hi = sb("h_hi", [P, KT, T], F32R)
        h_lo = sb("h_lo", [P, KT, T], F32R)
        cst = sb("cst", [P, NCONST, P])
        negm = sb("negm", [P, 1 + TT, P], BF16)
        a_hi = sb("a_hi", [P, 2, T], F32R)
        a_lo = sb("a_lo", [P, 2, T], F32R)
        nrow = sb("nrow", [P, D])
        xn = sb("xn", [P, D])
        stat = sb("stat", [P, 6, TT])
        ident, tri, ones = cst[:, C_ID, :], cst[:, C_TRI, :], cst[:, C_ONES, :]

        def mb(name, shape, dt=F32, where=ctx):
            return where.enter_context(nc.sbuf_tensor(name, shape, dt))

        mixing = ExitStack()
        mix = mb("mix", [P, MIX, T], where=mixing)
        vec = mb("vec", [P, VROWS], where=mixing)
        inner = ExitStack()
        cw_g = mb("cw_g", [P, TAPS * 24], where=inner)
        cw_s = mb("cw_s", [P, TAPS * 12], where=inner)
        dcol = mb("dcol", [P, XT], where=inner)
        gates = mb("gates", [P, HEADS, KINDS, TT], where=inner)
        cacc = mb("cacc", [P, 2, T], where=inner)

        start = ExitStack()
        rows_g = mb("rows_g", [96, P], where=start)
        rows_s = mb("rows_s", [48, P], where=start)
        rows_v = mb("rows_v", [VROWS, P], where=start)
        wsm = mb("wsm", [P, KT, 32], where=start)
        wsm_hi = mb("wsm_hi", [P, KT, 32], F32R, start)
        wsm_lo = mb("wsm_lo", [P, KT, 32], F32R, start)
        brow = mb("brow", [P, HEADS], where=start)
        arow = mb("arow", [P, HEADS], where=start)
        gr = mb("gr", [P, TT, 32], where=start)
        gt = mb("gt", [P, 10, TT, HEADS], where=start)
        start.close()

        gdn = ExitStack()
        qA = mb("qA", [P, T], where=gdn)
        kA = mb("kA", [P, T], where=gdn)
        vA = mb("vA", [P, T], where=gdn)
        cwB = mb("cwB", [P, 2, 12], where=gdn)
        colB = mb("colB", [P, 2, KINDS, TT], where=gdn)
        br2B = mb("br2B", [P, 2, 2, TT], where=gdn)
        ssA = mb("ssA", [P, 3, TT], where=gdn)
        kB = mb("kB", [P, 2, T], where=gdn)
        qdB = mb("qdB", [P, 2, T], where=gdn)
        q_sqB = mb("q_sqB", [P, 2, T], where=gdn)
        vB = mb("vB", [P, 2, T], where=gdn)
        kdB = mb("kdB", [P, 2, T], where=gdn)
        atB = mb("atB", [P, 2, T], where=gdn)
        nB = mb("nB", [P, 2, T], where=gdn)
        eg = mb("eg", [P, T], where=gdn)
        dt_ = mb("dt_", [P, T], where=gdn)
        u_neg = mb("u_neg", [P, T], where=gdn)
        u_off = mb("u_off", [P, 2, T], where=gdn)
        nW = mb("nW", [P, T], where=gdn)
        mW = mb("mW", [P, T], where=gdn)
        xW = mb("xW", [P, T], where=gdn)
        stS = mb("stS", [P, P], where=gdn)
        rR = mb("rR", [P, P], where=gdn)
        vN = mb("vN", [P, P], where=gdn)
        sqW = mb("sqW", [P, T], where=gdn)
        oz = mb("oz", [P, T], where=gdn)
        fW = mb("fW", [P, 3, TT], where=gdn)
        gdn.close()

        ssd = ExitStack()
        bcA = mb("bcA", [P, 4, T], where=ssd)
        b_tok = mb("b_tok", [P, GROUPS, T], where=ssd)
        cb = mb("cb", [P, GROUPS, T], where=ssd)
        b_cur = mb("b_cur", [P, T], where=ssd)
        colS = mb("colS", [P, 2, KINDS, TT], where=ssd)
        cwS = mb("cwS", [P, 2, 6], where=ssd)
        xA = mb("xA", [P, 2, T], where=ssd)
        egS = mb("egS", [P, 2, T], where=ssd)
        dtS = mb("dtS", [P, 2, T], where=ssd)
        cdS = mb("cdS", [P, 2, T], where=ssd)
        scS = mb("scS", [P, 2, T], where=ssd)
        xdt = mb("xdt", [P, T], where=ssd)
        xdd = mb("xdd", [P, T], where=ssd)
        hst = mb("hst", [P, 3, P], where=ssd)
        y1 = mb("y1", [P, T], where=ssd)
        y_sq = mb("y_sq", [P, 4, T], where=ssd)
        y_root = mb("y_root", [P, 2, T], where=ssd)
        ssd.close()
        inner.close()

        mem = ExitStack()
        mx = mb("mx", [P, MT, D], where=mem)
        m_hi = mb("m_hi", [P, KT, M], F32R, mem)
        m_lo = mb("m_lo", [P, KT, M], F32R, mem)
        mem.close()
        mixing.close()

        att = ExitStack()
        kmT = mb("kmT", [P, KT, M], where=att)
        v_m = mb("v_m", [P, MT, D], where=att)
        pr = mb("pr", [P, 2, TT, M], where=att)
        prT = mb("prT", [P, 2, MT, T], where=att)
        qmT = mb("qmT", [P, KT, T], where=att)
        oT = mb("oT", [P, KT, T], where=att)
        sm = mb("sm", [P, 2, 4, TT], where=att)
        att.close()

        uT = mb("uT", [P, FT, T])
        ur = mb("ur", [P, 2, T])

        names = """
        par_in cst_in x_in n_row mem_in out_done
        slab_hi slab_ready slab_used
        n_sq n_add n_mean n_root n_rstd n_xn n_tr n_hi n_lo
        rows_tr rows_cp wsm_hi_ok wsm_lo_ok gate_mm gate_raw gate_dve gate_act gate_cs gates_ok
        d_cols d_cw d_sse d_rec d_br d_nb d_kb d_qd d_kd d_u d_at d_v d_off d_n d_r d_s d_oz d_fe d_fr mix_done
        d_tap a_tap a_silu z_done
        pe_ss pe_g pe_gm pe_kk pe_kq pe_kt pe_vt pe_mt pe_x pe_n pe_ks pe_v pe_s pe_o pe_f pe_fb
        a_eg a_dt a_q2 a_rinv a_x a_m a_v a_o2 a_k2 a_rf
        as_tap ds_tap as_silu zs_done pb_tr pb_cb ab_tok db_cb
        ds_cw ds_cols ds_bcur ds_xdt ds_xdd ds_cd ds_sc ds_h ds_y1 ds_mix
        ps_g ps_m ps_x ps_st ps_y as_eg as_dt
        gn_sq gn_sum gn_mean gn_root gn_rec gn_mix
        cut_hi cut_lo x_add km_ok vm_ok qm_ok
        at_s at_max at_neg at_exp at_rec at_pn at_tr at_prt at_pv at_o
        up_relu up_sq fin_y
        """.split()
        S = {n: sem(n) for n in names}
        raw_in = [sem(f"raw_in{j}") for j in range(RAW_SLOTS)]
        block = ctx.enter_context(nc.Block())

        N1, NM, N2, N3, NF = (0, 0, TT), (1, TT, MT), (2, TT + MT, TT), (3, 2 * TT + MT, TT), (4, 3 * TT + MT, TT)

        def chunk(ap, c):
            return ap[:, c * P:(c + 1) * P]

        def bcast(ap, n):
            return ap.unsqueeze(2).to_broadcast([P, ap.shape[1], n])

        @block.sync
        def _(sp):
            w_in_v = a["w_in"].rearrange("(k p) n -> p k n", p=P)

            def slab(s, j, src):
                need(sp, S["slab_ready"], s - RAW_SLOTS + 1)
                dst = raw[:, j % RAW_SLOTS, :]
                if len(src.shape) == 3:
                    dst = dst.rearrange("p (k n) -> p k n", k=KT)
                sp.dma_start(dst, src).then_inc(raw_in[j % RAW_SLOTS], 16)

            def cols(w, c0):
                return w[:, :, bass.ds(c0, P)]

            def rows(w, r0):
                return w[bass.ds(r0, P), :]

            def gdn_slabs(h):
                for j in range(4):
                    slab(S_GDN + 4 * h + j, j, cols(w_in_v, j * GDN + h * P))

            gdn_slabs(0)
            with sp.Fori(1, HG) as h:
                gdn_slabs(h)
            for n in range(4):
                slab(S_BC + n, n, cols(w_in_v, GDN_COLS + 2 * D + n * P))

            def xz_slabs(i):
                for u in range(2):
                    slab(S_XZ + 4 * i + 2 * u, 2 * u, cols(w_in_v, GDN_COLS + D + (2 * i + u) * P))
                    slab(S_XZ + 4 * i + 2 * u + 1, 2 * u + 1, cols(w_in_v, GDN_COLS + (2 * i + u) * P))

            with sp.Fori(0, XT // 2) as i:
                xz_slabs(i)

            def row_slabs(w, s0, n):
                with sp.Fori(0, n // 4) as i:
                    for j in range(4):
                        slab(s0 + 4 * i + j, j, rows(w, (4 * i + j) * P))

            def col_slabs(w, s0, n):
                wv = w.rearrange("(k p) n -> p k n", p=P)
                with sp.Fori(0, n // 4) as i:
                    for j in range(4):
                        slab(s0 + 4 * i + j, j, cols(wv, (4 * i + j) * P))

            row_slabs(a["w_out"], S_OUT, MIX)
            col_slabs(a["wk_mem"], S_WK, KT)
            row_slabs(a["wv_mem"], S_WV, KT)
            col_slabs(a["wq_mem"], S_WQ, KT)
            row_slabs(a["wo_mem"], S_WO, KT)
            col_slabs(a["w_up"], S_UP, FT)
            row_slabs(a["w_down"], S_DOWN, FT)
            for t in range(TT):
                sp.wait_ge(S["fin_y"], t + 1)
                sp.dma_start(out[0, t * P:(t + 1) * P, :], x_res[:, t, :]).then_inc(S["out_done"], 16)
            sp.wait_ge(S["out_done"], 16 * TT)

        @block.gpsimd
        def _(pool):
            def cut(i, j):
                s = 4 * i + j
                pool.wait_ge(S["slab_hi"], s + 1)
                nc.gpsimd.tensor_tensor(w_lo[:, j, :], raw[:, j % RAW_SLOTS, :], w_hi[:, j, :].bitcast(F32),
                                        ALU.subtract).then_inc(S["slab_ready"], 1)

            for j in range(SLOTS):
                cut(0, j)
            with pool.Fori(1, N_SLABS // SLOTS) as i:
                for j in range(SLOTS):
                    cut(i, j)

        @block.tensor
        def _(pe):
            mm = nc.tensor.matmul

            def dense_k(s, j, bank, k, r_hi=h_hi, r_lo=h_lo, n=T):
                if k == 0:
                    pe.wait_ge(S["slab_ready"], s + 1)
                wh, wl = w_hi[:, j, k * P:(k + 1) * P], w_lo[:, j, k * P:(k + 1) * P]
                mm(bank[:, 0:n], wh, r_hi[:, k, :], start=(k == 0), stop=False)
                mm(bank[:, 0:n], wh, r_lo[:, k, :], start=False, stop=False)
                m = mm(bank[:, 0:n], wl, r_hi[:, k, :], start=False, stop=(k == KT - 1))
                if k == KT - 1:
                    m.then_inc(S["slab_used"], 1)

            def norm_tile(batch, i):
                g = batch[1] + i
                pe.wait_ge(S["n_xn"], g + 1)
                for f in range(2):
                    bank = B[2 + (2 * g + f) % 4]
                    need(pe, S["n_lo"], 2 * g + f - 3)
                    for q in range(4):
                        m = nc.tensor.transpose(chunk(bank, q), xn[:, (4 * f + q) * P:(4 * f + q + 1) * P], ident)
                    m.then_inc(S["n_tr"], 1)

            def row_k(s, j, k, first, last, lhs_hi, lhs_lo, tiles, banks):
                pe.wait_ge(S["slab_ready"], s + 1)
                for t in range(tiles):
                    lh, ll = lhs_hi(k, t), lhs_lo(k, t)
                    for f in range(2):
                        bank = banks[2 * t + f]
                        fs = slice(f * HALF, (f + 1) * HALF)
                        mm(bank[:], lh, w_hi[:, j, fs], start=first, stop=False)
                        mm(bank[:], lh, w_lo[:, j, fs], start=False, stop=False)
                    for f in range(2):
                        fs = slice(f * HALF, (f + 1) * HALF)
                        m = mm(banks[2 * t + f][:], ll, w_hi[:, j, fs], start=False, stop=last)
                m.then_inc(S["slab_used"], 1)

            def row_product(s0, c0, nk):
                def step(i, j, first, last):
                    k = 4 * i + j
                    pe.wait_ge(S["cut_lo"], c0 + k + 1)
                    row_k(s0 + k, j, k, first, last, lambda k, t: chunk(a_hi[:, j % 2, :], t),
                          lambda k, t: chunk(a_lo[:, j % 2, :], t), TT, B)
                n = nk // 4
                for j in range(4):
                    step(0, j, j == 0, False)
                if n > 2:
                    with pe.Fori(1, n - 1) as i:
                        for j in range(4):
                            step(i, j, False, False)
                for j in range(4):
                    step(n - 1, j, False, j == 3)

            pe.wait_ge(S["par_in"], PAR_DMAS * 16)
            pe.wait_ge(S["cst_in"], 32)
            nc.tensor.transpose(B[0][:, 0:96], rows_g[:], cst[0:96, C_ID, 0:96])
            nc.tensor.transpose(B[0][:, 96:144], rows_s[:], cst[0:48, C_ID, 0:48])
            nc.tensor.transpose(B[0][:, 144:144 + VROWS], rows_v[:],
                                cst[0:VROWS, C_ID, 0:VROWS]).then_inc(S["rows_tr"], 1)
            for i in range(TT):
                norm_tile(N1, i)
            pe.wait_ge(S["n_lo"], 2 * TT)
            pe.wait_ge(S["wsm_lo_ok"], 1)
            for t in range(TT):
                o = B[1][:, t * 32:(t + 1) * 32]
                for k in range(KT):
                    lh, ll = chunk(h_hi[:, k, :], t), chunk(h_lo[:, k, :], t)
                    mm(o, lh, wsm_hi[:, k, :], start=(k == 0), stop=False)
                    mm(o, lh, wsm_lo[:, k, :], start=False, stop=False)
                    m = mm(o, ll, wsm_hi[:, k, :], start=False, stop=(k == KT - 1))
            m.then_inc(S["gate_mm"], 1)
            pe.wait_ge(S["gate_cs"], 1)
            gsrc = gt[:, 5].rearrange("p c h -> p (c h)")
            mm(B[2][:, 0:TT * HEADS], tri, gsrc, start=True, stop=True)
            mm(B[3][:, 0:TT * HEADS], ones, gsrc, start=True, stop=True).then_inc(S["gate_mm"], 1)

            def gdn_iter(h, a_, b, par, dense, inv, chain):
                pa, pb = 1 - par, par
                steps = iter(range(32))

                def D(n):
                    if not dense:
                        return
                    for _ in range(n):
                        x = next(steps)
                        j, k = x // 8, x % 8
                        if k == 0:
                            if j < 2:
                                need(pe, S["d_tap" if j == 0 else "z_done"], 9 * h if j == 0 else h)
                            else:
                                need(pe, S["d_tap"], 9 * h + 3 * (j - 1))
                        dense_k(4 * h + j, j, B[j % 2], k)

                def ss():
                    pe.wait_ge(S["a_k2"], a_ + 1)
                    need(pe, S["mix_done"], a_ - 1)
                    for c in range(TT):
                        m = mm(B[5][:, c:c + 1], chunk(sqW, c), ones[:, 0:1], start=True, stop=True)
                    m.then_inc(S["pe_ss"], 1)

                def gsum():
                    pe.wait_ge(S["d_cols"], a_ + 1)
                    need(pe, S["d_v"], a_)
                    for c in range(TT):
                        m = mm(chunk(B[7], c), colB[:, pa, G_G, c:c + 1].to_broadcast([P, P]), tri,
                               start=(c == 0), stop=False, skip_group_check=True)
                    m.then_inc(S["pe_g"], 1)

                def mask():
                    pe.wait_ge(S["a_eg"], a_ + 1)
                    mm(B[7][:], negm[:, 0, :], negm[:, 1:, :].rearrange("p c t -> p (c t)"), start=False,
                       stop=True, skip_group_check=True).then_inc(S["pe_gm"], 1)

                def kk():
                    need(pe, S["a_x"], 6 * a_)
                    pe.wait_ge(S["a_silu"], 3 * a_ + 2)
                    for c in range(TT):
                        m = mm(chunk(B[2], c), chunk(kA, c), chunk(kA, c), start=True, stop=True)
                    m.then_inc(S["pe_kk"], 1)

                def kq():
                    need(pe, S["d_n"], 7 * a_)
                    for c in range(TT):
                        m = mm(chunk(B[3], c), chunk(kA, c), chunk(qA, c), start=True, stop=True)
                    m.then_inc(S["pe_kq"], 1)

                def kt():
                    need(pe, S["a_m"], 6 * a_)
                    for c in range(TT):
                        m = nc.tensor.transpose(chunk(B[4], c), chunk(kA, c), ident)
                    m.then_inc(S["pe_kt"], 1)

                def vt():
                    pe.wait_ge(S["a_dt"], a_ + 1)
                    pe.wait_ge(S["a_silu"], 3 * a_ + 3)
                    for c in range(TT):
                        m = nc.tensor.transpose(chunk(B[7], c), chunk(vA, c), ident)
                    m.then_inc(S["pe_vt"], 1)

                def mt(l):
                    pe.wait_ge(S["d_n"], 7 * a_ + l + 1)
                    if l == 0:
                        pe.wait_ge(S["d_kd"], a_ + 1)
                    else:
                        pe.wait_ge(S["a_m"], 6 * a_ + l)
                    for c in range(TT):
                        m = nc.tensor.transpose(chunk(B[4], c), chunk(nW, c), ident)
                    m.then_inc(S["pe_mt"], 1)

                def xm(l):
                    pe.wait_ge(S["a_m"], 6 * a_ + l)
                    pe.wait_ge(S["d_off"], 7 * a_ + l + 1)
                    if l == 1:
                        pe.wait_ge(S["d_u"], a_ + 1)
                    else:
                        pe.wait_ge(S["a_x"], 6 * a_ + l - 1)
                    for c in range(TT):
                        m = mm(chunk(B[2], c), chunk(u_off[:, l % 2, :], c), chunk(mW, c), start=True, stop=True)
                    m.then_inc(S["pe_x"], 1)

                def nn(l):
                    pe.wait_ge(S["a_x"], 6 * a_ + l)
                    pe.wait_ge(S["d_n"], 7 * a_ + l)
                    if l == 1:
                        pe.wait_ge(S["d_at"], a_ + 1)
                    for c in range(TT):
                        m = mm(chunk(B[3], c), chunk(xW, c), chunk(nW, c), start=True, stop=True)
                    m.then_inc(S["pe_n"], 1)

                def ks(c):
                    pe.wait_ge(S["d_s"], 3 * b + c)
                    mm(B[5][:, 0:P], chunk(kB[:, pb, :], c), stS[:], start=True, stop=True).then_inc(S["pe_ks"], 1)

                def vv(c):
                    if c == 0:
                        pe.wait_ge(S["d_n"], 7 * b + 7)
                        pe.wait_ge(S["d_v"], b + 1)
                        if inv:
                            pe.wait_ge(S["d_sse"], a_ + 1)
                        else:
                            need(pe, S["mix_done"], b)
                        rhs = chunk(vB[:, pb, :], 0)
                    else:
                        pe.wait_ge(S["d_r"], 3 * b + c)
                        rhs = rR[:]
                    mm(B[5][:, 0:P], chunk(nB[:, pb, :], c), rhs, start=True, stop=True).then_inc(S["pe_v"], 1)

                def oo(c):
                    if c == 0:
                        need(pe, S["d_oz"], b)
                        pe.wait_ge(S["d_at"], b + 1)
                    else:
                        mm(chunk(B[6], c), stS[:], chunk(qdB[:, pb, :], c), start=True, stop=False)
                    pe.wait_ge(S["a_v"], 4 * b + c + 1)
                    m = mm(chunk(B[6], c), vN[:], chunk(atB[:, pb, :], c), start=(c == 0), stop=True)
                    if c < TT - 1:
                        mm(B[5][:, 0:P], chunk(kdB[:, pb, :], c), vN[:], start=True, stop=True).then_inc(S["pe_s"], 1)
                    else:
                        m.then_inc(S["pe_o"], 1)

                def fsum():
                    pe.wait_ge(S["a_o2"], b + 1)
                    for c in range(TT):
                        mm(B[5][:, c:c + 1], chunk(sqW, c), cst[:, C_VEC, 0:1], start=True, stop=False)
                        m = mm(B[5][:, c:c + 1], chunk(q_sqB[:, pb, :], c), cst[:, C_VEC, 1:2], start=False, stop=True)
                    m.then_inc(S["pe_f"], 1)

                def fb():
                    pe.wait_ge(S["d_fr"], b + 1)
                    for c in range(TT):
                        m = mm(chunk(B[5], c), fW[:, 2, c:c + 1].to_broadcast([P, P]), ident, start=True, stop=True)
                    m.then_inc(S["pe_fb"], 1)

                I = lambda f, *x: f(*x) if inv else None
                C = lambda f, *x: f(*x) if chain else None
                I(ss); I(gsum); I(kk); D(1)
                I(kq); I(kt); C(vv, 0); D(1)
                I(mask); C(oo, 0); D(1)
                C(ks, 1); D(2)
                I(vt); C(vv, 1); D(1)
                I(mt, 0); C(oo, 1); D(1)
                I(xm, 1); C(ks, 2); D(1)
                I(nn, 1); C(vv, 2); D(1)
                I(mt, 1); C(oo, 2); D(2)
                I(xm, 2); C(ks, 3); D(1)
                I(nn, 2); C(vv, 3); D(1)
                I(mt, 2); C(oo, 3); D(2)
                I(xm, 3); C(fsum); D(1)
                I(nn, 3); D(2)
                I(mt, 3); C(fb); D(1)
                I(xm, 4); D(2)
                I(nn, 4); D(1)
                I(mt, 4); D(2)
                I(xm, 5); D(2)
                I(nn, 5); D(1)
                I(mt, 5); D(2)
                I(xm, 6); D(1)
                I(nn, 6); D(2)

            gdn_iter(0, None, None, 0, True, False, False)
            gdn_iter(1, 0, None, 1, True, True, False)
            gdn_iter(2, 1, 0, 0, True, True, True)
            gdn_iter(3, 2, 1, 1, True, True, True)
            with pe.Fori(2, HG // 2) as i:
                gdn_iter(2 * i, 2 * i - 1, 2 * i - 2, 0, True, True, True)
                gdn_iter(2 * i + 1, 2 * i, 2 * i - 1, 1, True, True, True)
            gdn_iter(None, HG - 1, HG - 2, 0, False, True, True)
            gdn_iter(None, None, HG - 1, 1, False, False, True)

            for n in range(4):
                if n == 0:
                    pe.wait_ge(S["d_tap"], 9 * HG)
                elif n == 1:
                    pe.wait_ge(S["z_done"], HG)
                else:
                    pe.wait_ge(S["ds_tap"], 3 * (n - 1))
                for k in range(KT):
                    dense_k(S_BC + n, n, B[n % 2], k)

            def ssd_iter(j, i, par, dense, ssd_):
                pi = 1 - par
                steps = iter(range(16))

                def D(n):
                    if not dense:
                        return
                    for _ in range(n):
                        x = next(steps)
                        u, k = x // 8, x % 8
                        if k == 0 and u == 0:
                            pe.wait_ge(S["ds_tap"], 3 * (3 + j))
                        elif k == 0 and isinstance(j, int) and j == 0:
                            pe.wait_ge(S["ds_tap"], 3 * 4)
                        elif k == 0:
                            pe.wait_ge(S["zs_done"], j)
                        dense_k(S_XZ + 2 * j + u, (2 * par + u), B[u], k)

                def gsum(hh):
                    bank = B[7] if hh == 0 else B[2]
                    if hh == 0:
                        pe.wait_ge(S["ds_cols"], i + 1)
                    need(pe, S["as_dt"], 2 * i - 1 + hh)
                    for c in range(TT):
                        m = mm(chunk(bank, c), colS[:, hh, G_G, c:c + 1].to_broadcast([P, P]), tri,
                               start=(c == 0), stop=False, skip_group_check=True)
                    m.then_inc(S["ps_g"], 1)

                def mask(hh):
                    bank = B[7] if hh == 0 else B[2]
                    pe.wait_ge(S["as_eg"], 2 * i + 1 + hh)
                    mm(bank[:], negm[:, 0, :], negm[:, 1:, :].rearrange("p c t -> p (c t)"), start=False,
                       stop=True, skip_group_check=True).then_inc(S["ps_m"], 1)

                def xt():
                    pe.wait_ge(S["as_silu"], i + 5)
                    need(pe, S["ds_xdt"], i)
                    for c in range(TT):
                        m = nc.tensor.transpose(chunk(B[3], c), chunk(xA[:, pi, :], c), ident)
                    m.then_inc(S["ps_x"], 1)

                def st():
                    pe.wait_ge(S["ds_xdd"], i + 1)
                    pe.wait_ge(S["ds_bcur"], i + 1)
                    need(pe, S["ds_h"], 3 * i)
                    for c in range(TT - 1):
                        m = mm(chunk(B[4], c), chunk(b_cur, c), chunk(xdd, c), start=True, stop=True)
                    m.then_inc(S["ps_st"], 1)

                def yy():
                    pe.wait_ge(S["ds_sc"], 2 * i + 2)
                    pe.wait_ge(S["ds_cd"], 2 * i + 2)
                    pe.wait_ge(S["ds_h"], 3 * i + 3)
                    need(pe, S["ds_y1"], i)
                    for c in range(TT):
                        for hh in range(2):
                            o = B[6][hh * HP:(hh + 1) * HP, c * P:(c + 1) * P]
                            hs = slice(c * P + hh * HP, c * P + (hh + 1) * HP)
                            m = mm(o, xdt[:, hs], chunk(scS[:, hh, :], c), start=True, stop=(c == 0))
                            if c:
                                m = mm(o, hst[:, c - 1, hh * HP:(hh + 1) * HP], chunk(cdS[:, hh, :], c),
                                       start=False, stop=True)
                    m.then_inc(S["ps_y"], 1)

                R = lambda f, *x: f(*x) if ssd_ else None
                R(gsum, 0); R(xt); D(2)
                R(gsum, 1); D(2)
                R(mask, 0); D(2)
                R(mask, 1); D(2)
                R(st); D(6)
                R(yy); D(2)

            ssd_iter(0, None, 0, True, False)
            pe.wait_ge(S["as_silu"], 4)
            for g in range(GROUPS):
                for c in range(TT):
                    m = nc.tensor.transpose(chunk(B[2 + g], c), chunk(bcA[:, g, :], c), ident)
                m.then_inc(S["pb_tr"], 1)
            for g in range(GROUPS):
                for c in range(TT):
                    m = mm(chunk(B[4 + g], c), chunk(bcA[:, g, :], c), chunk(bcA[:, 2 + g, :], c), start=True, stop=True)
                m.then_inc(S["pb_cb"], 1)
            pe.wait_ge(S["ab_tok"], GROUPS)
            pe.wait_ge(S["db_cb"], GROUPS)
            ssd_iter(1, 0, 1, True, True)
            with pe.Fori(1, XT // 2) as q:
                ssd_iter(2 * q, 2 * q - 1, 0, True, True)
                ssd_iter(2 * q + 1, 2 * q, 1, True, True)
            ssd_iter(None, XT - 1, 0, False, True)
            for g in range(GROUPS):
                for q in range(4):
                    pe.wait_ge(S["gn_sq"], 4 * g + q + 1)
                    m = mm(B[g][:], ones, y_sq[:, q, :], start=(q == 0), stop=(q == 3))
                m.then_inc(S["gn_sum"], 1)

            for i in range(MT):
                norm_tile(NM, i)
            pe.wait_ge(S["n_lo"], 2 * (TT + MT))
            pe.wait_ge(S["gn_mean"], GROUPS)
            pe.wait_ge(S["ds_y1"], XT)
            row_product(S_OUT, 0, MIX)

            def wk(n):
                if n < 2:
                    pe.wait_ge(S["x_add"], n + 1)
                else:
                    pe.wait_ge(S["km_ok"], n - 1)
                for k in range(KT):
                    dense_k(S_WK + n, n % 4, B[n % 2], k, m_hi, m_lo, M)

            for n in range(KT - TT):
                wk(n)
            for i in range(TT):
                wk(KT - TT + i)
                norm_tile(N2, i)
            pe.wait_ge(S["km_ok"], KT)
            vb = [B[6], B[7], B[0], B[1]]
            for k in range(KT):
                row_k(S_WV + k, k % 4, k, k == 0, k == KT - 1, lambda k, t: chunk(m_hi[:, k, :], t),
                      lambda k, t: chunk(m_lo[:, k, :], t), MT, vb)

            def wq(n):
                pe.wait_ge(S["vm_ok"], MT * 2)
                need(pe, S["qm_ok"], n - 1)
                for k in range(KT):
                    dense_k(S_WQ + n, n % 4, B[n % 2], k)

            pe.wait_ge(S["n_lo"], 2 * (2 * TT + MT))
            wq(0)
            wq(1)
            for hd in range(AH):
                pe.wait_ge(S["qm_ok"], 2 * hd + 2)
                need(pe, S["at_exp"], TT * hd)
                for t in range(TT):
                    o = B[2 + t // 2][:, (t % 2) * M:(t % 2 + 1) * M]
                    for u in range(2):
                        m = mm(o, chunk(qmT[:, 2 * hd + u, :], t), kmT[:, 2 * hd + u, :], start=(u == 0), stop=(u == 1))
                    if t % 2:
                        m.then_inc(S["at_s"], 1)
                if hd + 1 < AH:
                    wq(2 * hd + 2)
                    wq(2 * hd + 3)
                pe.wait_ge(S["at_pn"], hd + 1)
                need(pe, S["at_prt"], MT * hd)
                for mt_ in range(MT):
                    for t in range(TT):
                        m = nc.tensor.transpose(chunk(B[4 + mt_], t), pr[:, hd % 2, t, mt_ * P:(mt_ + 1) * P], ident)
                    m.then_inc(S["at_tr"], 1)
                pe.wait_ge(S["at_prt"], MT * (hd + 1))
                need(pe, S["at_o"], 2 * hd)
                for u in range(2):
                    for mt_ in range(MT):
                        d0 = hd * HD + u * P
                        m = mm(B[6 + u][:], v_m[:, mt_, d0:d0 + P], prT[:, hd % 2, mt_, :], start=(mt_ == 0), stop=(mt_ == 1))
                    m.then_inc(S["at_pv"], 1)

            pe.wait_ge(S["at_o"], 2 * AH)
            row_product(S_WO, MIX, KT)
            for i in range(TT):
                norm_tile(N3, i)
            pe.wait_ge(S["n_lo"], 2 * (3 * TT + MT))

            def up(i, j):
                n = 4 * i + j
                need(pe, S["up_relu"], n - 1)
                for k in range(KT):
                    dense_k(S_UP + n, j, B[j % 2], k)

            for j in range(4):
                up(0, j)
            with pe.Fori(1, FT // 4) as i:
                for j in range(4):
                    up(i, j)
            pe.wait_ge(S["up_relu"], FT)
            row_product(S_DOWN, MIX + KT, FT)

        @block.scalar
        def _(act):
            A = nc.scalar.activation

            def start_loads():
                def row(w, n):
                    return w.rearrange("(o n) -> o n", o=1).partition_broadcast(P)
                for t in range(TT):
                    act.dma_start(x_res[:, t, :], a["x"][0, t * P:(t + 1) * P, :]).then_inc(S["x_in"], 16)
                act.dma_start(nrow[:], row(a["norm1_w"], D)).then_inc(S["n_row"], 16)
                act.dma_start(cst[:], a["const"]).then_inc(S["cst_in"], 16)
                act.dma_start(negm[:], a["negm"]).then_inc(S["cst_in"], 16)
                w_in_v = a["w_in"].rearrange("(k p) n -> p k n", p=P)
                par = [
                    (wsm[:, :, 0:16], w_in_v[:, :, 4 * GDN:4 * GDN + 16]),
                    (wsm[:, :, 16:32], w_in_v[:, :, GDN_COLS + 2 * D + 2 * BC:]),
                    (brow[:, 0:HG], row(a["gdn_dt_bias"], HG)), (brow[:, HG:], row(a["ssm_dt_bias"], HS)),
                    (arow[:, 0:HG], row(a["gdn_a_log"], HG)), (arow[:, HG:], row(a["ssm_a_log"], HS)),
                    (rows_g[:], a["gdn_conv_w"].rearrange("k (j p) -> (k j) p", p=P)),
                    (rows_s[:], a["ssm_conv_w"].rearrange("k (j p) -> (k j) p", p=P)),
                    (rows_v[V_CB:V_NW, :], a["ssm_conv_b"].rearrange("(j p) -> j p", p=P)),
                    (rows_v[V_NW:V_GN, :], a["ssm_norm_w"].rearrange("(j p) -> j p", p=P)),
                    (rows_v[V_GN:VROWS, :], a["gdn_norm_w"].rearrange("(j p) -> j p", p=P)),
                ]
                for hh in range(2):
                    d = a["ssm_d"].rearrange("(o j u) -> o j u", o=1, u=2)[:, :, hh]
                    par.append((dcol[hh * HP:(hh + 1) * HP, :], d.partition_broadcast(HP)))
                assert len(par) == PAR_DMAS
                with nc.allow_non_contiguous_dma(reason="a few short rows and per-head scalars"):
                    for dst, src in par:
                        act.dma_start(dst, src).then_inc(S["par_in"], 16)

            def norm_sums(batch, src, ready):
                for i in range(batch[2]):
                    for f in range(2):
                        ready(i, f)
                        need(act, S["n_sq"], 2 * (batch[1] + i) + f)
                        A(B[6][:], src(i)[:, f * HALF:(f + 1) * HALF], ACT.Square,
                          accum_out=stat[:, f, i:i + 1]).then_inc(S["n_sq"], 1)

            def norm_root(batch):
                act.wait_ge(S["n_mean"], batch[0] + 1)
                A(stat[:, 4, 0:batch[2]], stat[:, 3, 0:batch[2]], ACT.Sqrt).then_inc(S["n_root"], 1)

            def norm_hi(batch, i, dst):
                g = batch[1] + i
                for f in range(2):
                    act.wait_ge(S["n_tr"], 2 * g + f + 1)
                    bank = B[2 + (2 * g + f) % 4]
                    A(dst[:, 4 * f:4 * f + 4, i * P:(i + 1) * P], bank[:].rearrange("p (q t) -> p q t", q=4),
                      ACT.Copy).then_inc(S["n_hi"], 1)

            def cut_hi(s0, c0, nk, src, ready):
                def step(i, j):
                    k = 4 * i + j
                    ready(k)
                    need(act, S["slab_used"], s0 + k - 1)
                    A(a_hi[:, j % 2, :], src(k), ACT.Copy).then_inc(S["cut_hi"], 1)
                    if not (isinstance(i, int) and i == 0 and j < 2):
                        w_cut(s0 // 4 + i + (j + 2) // 4, (j + 2) % 4)
                n = nk // 4
                for j in range(4):
                    step(0, j)
                if n > 2:
                    with act.Fori(1, n - 1) as i:
                        for j in range(4):
                            step(i, j)
                for j in range(4):
                    step(n - 1, j)
                for j in (2, 3):
                    w_cut((s0 + nk) // 4, j)

            def w_cut(i, j):
                if isinstance(i, int) and 4 * i + j >= N_SLABS:
                    return
                act.wait_ge(raw_in[j % RAW_SLOTS], 16 * (2 * i + j // 2 + 1))
                need(act, S["slab_used"], 4 * i + j - SLOTS + 1)
                A(w_hi[:, j, :], raw[:, j % RAW_SLOTS, :], ACT.Copy).then_inc(S["slab_hi"], 1)

            def load_row(w, nb, tiles_before):
                act.wait_ge(S["n_xn"], tiles_before)
                act.dma_start(nrow[:], w.rearrange("(o n) -> o n", o=1).partition_broadcast(P)).then_inc(S["n_row"], 16)

            start_loads()
            act.wait_ge(S["x_in"], 16 * TT)
            norm_sums(N1, lambda i: x_res[:, i, :], lambda i, f: None)
            norm_root(N1)
            for j in range(SLOTS):
                w_cut(0, j)
            act.wait_ge(S["par_in"], PAR_DMAS * 16)
            A(wsm_hi[:], wsm[:], ACT.Copy).then_inc(S["wsm_hi_ok"], 1)
            for i in range(TT):
                norm_hi(N1, i, h_hi)

            act.wait_ge(S["gate_raw"], 1)
            A(gt[:, 2], gt[:, 1], ACT.Exp, scale=-1.0)
            A(gt[:, 3, :, 0:HG], gr[:, :, 0:HG], ACT.Exp, scale=-1.0)
            A(arow[:], arow[:], ACT.Exp).then_inc(S["gate_act"], 1)
            act.wait_ge(S["gate_raw"], 2)
            A(gt[:, 1], gt[:, 0], ACT.Exp)
            A(gt[:, 2], gt[:, 8], ACT.Exp)
            A(gt[:, 3], gt[:, 9], ACT.Exp).then_inc(S["gate_act"], 1)

            def gdn_iter(h, a_, b, par, dense, inv, chain):
                pa, pb = 1 - par, par

                def eg_():
                    act.wait_ge(S["pe_g"], a_ + 1)
                    need(act, S["d_qd"], a_)
                    A(eg[:], B[7][:], ACT.Exp).then_inc(S["a_eg"], 1)

                def dt():
                    act.wait_ge(S["pe_gm"], a_ + 1)
                    act.wait_ge(S["d_cols"], a_ + 1)
                    need(act, S["d_u"], a_)
                    need(act, S["d_at"], a_)
                    for c in range(TT):
                        m = A(chunk(dt_, c), chunk(B[7], c), ACT.Exp, bias=colB[:, pa, G_NEG, c:c + 1])
                    m.then_inc(S["a_dt"], 1)

                def q2():
                    act.wait_ge(S["a_silu"], 3 * a_ + 1)
                    need(act, S["pe_f"], a_ - 1)
                    A(q_sqB[:, pa, :], qA[:], ACT.Square).then_inc(S["a_q2"], 1)

                def rinv():
                    act.wait_ge(S["d_sse"], a_ + 1)
                    need(act, S["d_v"], a_)
                    A(ssA[:, 1, :], ssA[:, 0, :], ACT.Sqrt).then_inc(S["a_rinv"], 1)

                def v(c):
                    act.wait_ge(S["pe_v"], 4 * b + c + 1)
                    A(vN[:], B[5][:, 0:P], ACT.Copy, scale=br2B[:, pb, 0, c:c + 1]).then_inc(S["a_v"], 1)

                def m_(l):
                    act.wait_ge(S["pe_mt"], 6 * a_ + l + 1)
                    A(mW[:], B[4][:], ACT.Copy).then_inc(S["a_m"], 1)

                def x_(l):
                    act.wait_ge(S["pe_x"], 6 * a_ + l)
                    A(xW[:], B[2][:], ACT.Copy).then_inc(S["a_x"], 1)

                def o2():
                    act.wait_ge(S["pe_o"], b + 1)
                    A(sqW[:], B[6][:], ACT.Square).then_inc(S["a_o2"], 1)

                def rf():
                    act.wait_ge(S["d_fe"], b + 1)
                    A(fW[:, 1, :], fW[:, 0, :], ACT.Sqrt).then_inc(S["a_rf"], 1)

                def tap(t):
                    act.wait_ge(S["slab_used"], 4 * h + t + 1)
                    act.wait_ge(S["d_cw"], h + 1)
                    need(act, S["a_silu"], 3 * h + t - 1)
                    A(cacc[:, t % 2, :], B[t % 2][:], ACT.Copy, scale=cwB[:, par, 9 + t:10 + t]).then_inc(S["a_tap"], 1)

                def silu(t):
                    act.wait_ge(S["d_tap"], 9 * h + 3 * t + 3)
                    if inv:
                        act.wait_ge(S[("pe_kq", "pe_kt", "pe_vt")[t]], a_ + 1)
                        if t < 2:
                            act.wait_ge(S[("d_qd", "d_kb")[t]], a_ + 1)
                        if t == 0:
                            act.wait_ge(S["a_q2"], a_ + 1)
                    A((qA, kA, vA)[t][:], cacc[:, t % 2, :], ACT.Silu).then_inc(S["a_silu"], 1)

                def k2():
                    act.wait_ge(S["a_silu"], 3 * h + 2)
                    if chain:
                        act.wait_ge(S["pe_f"], b + 1)
                    if inv:
                        act.wait_ge(S["pe_ss"], a_ + 1)
                    A(sqW[:], kA[:], ACT.Square).then_inc(S["a_k2"], 1)

                def z():
                    act.wait_ge(S["slab_used"], 4 * h + 4)
                    A(mix[:, bass.ds(h, 1), :].rearrange("p o t -> p (o t)"), B[1][:], ACT.Silu).then_inc(S["z_done"], 1)

                I = lambda f, *x: f(*x) if inv else None
                C = lambda f, *x: f(*x) if chain else None
                H = lambda f, *x: f(*x) if dense else None
                I(eg_); C(v, 0); I(dt); I(q2); I(rinv)
                C(v, 1); I(m_, 0)
                W = lambda j: w_cut(S_GDN // 4 + h + 1, j) if dense else None
                I(x_, 1); C(v, 2); H(tap, 0); W(0); I(m_, 1)
                I(x_, 2); C(v, 3); I(m_, 2); C(o2)
                I(x_, 3); C(rf); H(tap, 1); W(1); I(m_, 3)
                H(silu, 0)
                I(x_, 4); H(silu, 1); H(k2); I(m_, 4)
                I(x_, 5); H(tap, 2); W(2); I(m_, 5)
                I(x_, 6); H(silu, 2); H(z); W(3)

            gdn_iter(0, None, None, 0, True, False, False)
            gdn_iter(1, 0, None, 1, True, True, False)
            gdn_iter(2, 1, 0, 0, True, True, True)
            gdn_iter(3, 2, 1, 1, True, True, True)
            with act.Fori(2, HG // 2) as i:
                gdn_iter(2 * i, 2 * i - 1, 2 * i - 2, 0, True, True, True)
                gdn_iter(2 * i + 1, 2 * i, 2 * i - 1, 1, True, True, True)
            gdn_iter(None, HG - 1, HG - 2, 0, False, True, True)
            gdn_iter(None, None, HG - 1, 1, False, False, True)

            act.wait_ge(S["mix_done"], HG)
            def conv_tap(n, s, bank, w):
                act.wait_ge(S["slab_used"], s + 1)
                need(act, S["as_silu"], n - 1)
                A(cacc[:, (n if isinstance(n, int) else 0) % 2, :], bank[:], ACT.Copy, scale=w).then_inc(S["as_tap"], 1)

            def bc_silu(n):
                act.wait_ge(S["ds_tap"], 3 * n + 3)
                A(bcA[:, n, :], cacc[:, n % 2, :], ACT.Silu, bias=vec[:, V_CB + 8 + n:V_CB + 9 + n]).then_inc(S["as_silu"], 1)

            for n in range(4):
                conv_tap(n, S_BC + n, B[n % 2], cw_s[:, 3 * 12 + 8 + n:3 * 12 + 9 + n])
                bc_silu(n)
                w_cut(S_BC // 4 + 1, n)

            def ssd_iter(j, i, par, dense, ssd_, ring=None):
                def eg_(hh):
                    act.wait_ge(S["ps_g"], 2 * i + hh + 1)
                    need(act, S["ds_cd"], 2 * i)
                    A(egS[:, hh, :], (B[7], B[2])[hh][:], ACT.Exp).then_inc(S["as_eg"], 1)

                def dt(hh):
                    act.wait_ge(S["ps_m"], 2 * i + hh + 1)
                    act.wait_ge(S["ds_cols"], i + 1)
                    need(act, S["ds_sc"], 2 * i)
                    for c in range(TT):
                        m = A(chunk(dtS[:, hh, :], c), chunk((B[7], B[2])[hh], c), ACT.Exp, bias=colS[:, hh, G_NEG, c:c + 1])
                    m.then_inc(S["as_dt"], 1)

                def x():
                    act.wait_ge(S["slab_used"], S_XZ + 2 * j + 1)
                    act.wait_ge(S["ds_cw"], j + 1)
                    act.wait_ge(S["as_silu"], 3 + j)
                    A(cacc[:, par, :], B[0][:], ACT.Copy, scale=cwS[:, par, 3:4]).then_inc(S["as_tap"], 1)

                def silu():
                    act.wait_ge(S["ds_tap"], 3 * (4 + j) + 3)
                    need(act, S["ps_x"], j - 1)
                    need(act, S["ds_y1"], j - 1)
                    A(xA[:, par, :], cacc[:, par, :], ACT.Silu, bias=cwS[:, par, 4:5]).then_inc(S["as_silu"], 1)

                def z():
                    act.wait_ge(S["slab_used"], S_XZ + 2 * j + 2)
                    A(mix[:, bass.ds(HG + j, 1), :].rearrange("p o t -> p (o t)"), B[1][:], ACT.Silu).then_inc(S["zs_done"], 1)

                if ssd_:
                    eg_(0); eg_(1); dt(0); dt(1)
                if dense:
                    x(); w_cut(ring + 1, 2 * par); silu(); z(); w_cut(ring + 1, 2 * par + 1)

            ssd_iter(0, None, 0, True, False, S_XZ // 4)
            for g in range(GROUPS):
                act.wait_ge(S["pb_tr"], g + 1)
                A(b_tok[:, g, :], B[2 + g][:], ACT.Copy).then_inc(S["ab_tok"], 1)
            ssd_iter(1, 0, 1, True, True, S_XZ // 4)
            with act.Fori(1, XT // 2) as q:
                ssd_iter(2 * q, 2 * q - 1, 0, True, True, S_XZ // 4 + q)
                ssd_iter(2 * q + 1, 2 * q, 1, True, True, S_XZ // 4 + q)
            ssd_iter(None, XT - 1, 0, False, True)
            for g in range(GROUPS):
                for q in range(4):
                    act.wait_ge(S["ds_mix"], 4 * g + q + 1)
                    need(act, S["gn_sum"], g)
                    A(y_sq[:, q, :], mix[:, HG + 4 * g + q, :], ACT.Square).then_inc(S["gn_sq"], 1)
            for g in range(GROUPS):
                act.wait_ge(S["gn_mean"], g + 1)
                A(y_root[:, g, :], y_root[:, g, :], ACT.Sqrt).then_inc(S["gn_root"], 1)

            load_row(a["mem_norm_w"], 1, TT)
            act.wait_ge(S["ds_mix"], XT)
            act.dma_start(mx[:], a["mem"].rearrange("b (t p) d -> p (b t) d", p=P)).then_inc(S["mem_in"], 16)
            act.wait_ge(S["mem_in"], 16)
            norm_sums(NM, lambda i: mx[:, i, :], lambda i, f: need(act, S["ds_y1"], XT))
            norm_root(NM)
            for i in range(MT):
                norm_hi(NM, i, m_hi)

            load_row(a["norm2_w"], 2, TT + MT)

            def mix_ready(k):
                if isinstance(k, int) and k >= HG:
                    act.wait_ge(S["gn_mix"], k - HG + 1)
                elif not isinstance(k, int):
                    act.wait_ge(S["gn_mix"], XT)
            act.wait_ge(S["mix_done"], HG)
            cut_hi(S_OUT, 0, MIX, lambda k: mix[:, bass.ds(k, 1), :].rearrange("p o t -> p (o t)"), mix_ready)

            norm_sums(N2, lambda i: x_res[:, i, :], lambda i, f: act.wait_ge(S["x_add"], 8))

            def km(n):
                act.wait_ge(S["slab_used"], S_WK + n + 1)
                A(kmT[:, n, :], B[n % 2][:, 0:M], ACT.Copy).then_inc(S["km_ok"], 1)
                w_cut(S_WK // 4 + 1 + n // 4, n % 4)

            for n in range(KT - TT):
                km(n)
                if n == 0:
                    norm_root(N2)
            for i in range(TT):
                km(KT - TT + i)
                norm_hi(N2, i, h_hi)
            load_row(a["norm3_w"], 3, 2 * TT + MT)
            for k in range(KT):
                w_cut(S_WV // 4 + 1 + k // 4, k % 4)
            act.wait_ge(S["slab_used"], S_WV + KT)
            for q, bank in enumerate([B[6], B[7], B[0], B[1]]):
                A(v_m[:, q // 2, (q % 2) * HALF:(q % 2 + 1) * HALF], bank[:], ACT.Copy).then_inc(S["vm_ok"], 1)

            def qm(n):
                act.wait_ge(S["slab_used"], S_WQ + n + 1)
                A(qmT[:, n, :], B[n % 2][:], ACT.Copy).then_inc(S["qm_ok"], 1)
                w_cut(S_WQ // 4 + 1 + n // 4, n % 4)

            qm(0)
            qm(1)
            for hd in range(AH):
                act.wait_ge(S["at_neg"], hd + 1)
                need(act, S["at_tr"], MT * (hd - 1))
                need(act, S["at_rec"], hd - 1)
                for t in range(TT):
                    A(pr[:, hd % 2, t, :], B[2 + t // 2][:, (t % 2) * M:(t % 2 + 1) * M], ACT.Exp,
                      bias=sm[:, hd % 2, 1, t:t + 1], scale=float(HD) ** -0.5,
                      accum_out=sm[:, hd % 2, 2, t:t + 1]).then_inc(S["at_exp"], 1)
                if hd + 1 < AH:
                    qm(2 * hd + 2)
                    qm(2 * hd + 3)
                for u in range(2):
                    act.wait_ge(S["at_pv"], 2 * hd + u + 1)
                    A(oT[:, 2 * hd + u, :], B[6 + u][:], ACT.Copy).then_inc(S["at_o"], 1)

            act.wait_ge(S["at_o"], 2 * AH)
            cut_hi(S_WO, MIX, KT, lambda k: oT[:, k, :], lambda k: None)
            norm_sums(N3, lambda i: x_res[:, i, :], lambda i, f: act.wait_ge(S["x_add"], 16))
            norm_root(N3)
            for i in range(TT):
                norm_hi(N3, i, h_hi)
            load_row(a["final_norm_w"], 4, 3 * TT + MT)

            def relu(i, j):
                n = 4 * i + j
                act.wait_ge(S["slab_used"], S_UP + n + 1)
                need(act, S["up_sq"], n - 1)
                A(ur[:, j % 2, :], B[j % 2][:], ACT.Relu).then_inc(S["up_relu"], 1)
                w_cut(S_UP // 4 + i + 1, j)

            for j in range(4):
                relu(0, j)
            with act.Fori(1, FT // 4) as i:
                for j in range(4):
                    relu(i, j)
            act.wait_ge(S["up_sq"], FT)
            cut_hi(S_DOWN, MIX + KT, FT, lambda k: uT[:, bass.ds(k, 1), :].rearrange("p o t -> p (o t)"), lambda k: None)
            norm_sums(NF, lambda i: x_res[:, i, :], lambda i, f: act.wait_ge(S["x_add"], 24))
            norm_root(NF)

        @block.vector
        def _(dve):
            V = nc.vector
            TTn = V.tensor_tensor

            def norm_stats(batch):
                nb, g0, n = batch
                dve.wait_ge(S["n_sq"], 2 * (g0 + n))
                TTn(stat[:, 2, 0:n], stat[:, 0, 0:n], stat[:, 1, 0:n], ALU.add).then_inc(S["n_add"], 1)
                dve.wait_ge(S["n_add"], nb + 1)
                V.tensor_scalar(stat[:, 3, 0:n], stat[:, 2, 0:n], 1.0 / D, EPS, ALU.mult, ALU.add).then_inc(S["n_mean"], 1)
                dve.wait_ge(S["n_root"], nb + 1)
                V.reciprocal(stat[:, 5, 0:n], stat[:, 4, 0:n]).then_inc(S["n_rstd"], 1)
                dve.wait_ge(S["n_rstd"], nb + 1)
                dve.wait_ge(S["n_row"], 16 * (nb + 1))

            def norm_xn(batch, i, src):
                g = batch[1] + i
                need(dve, S["n_tr"], 2 * g)
                V.scalar_tensor_tensor(out=xn[:], in0=src(i), scalar=stat[:, 5, i:i + 1], in1=nrow[:],
                                       op0=ALU.mult, op1=ALU.mult).then_inc(S["n_xn"], 1)

            def norm_lo(batch, i, d_hi, d_lo):
                g = batch[1] + i
                for f in range(2):
                    dve.wait_ge(S["n_hi"], 2 * g + f + 1)
                    bank = B[2 + (2 * g + f) % 4]
                    fs, ts = slice(4 * f, 4 * f + 4), slice(i * P, (i + 1) * P)
                    TTn(d_lo[:, fs, ts], bank[:].rearrange("p (q t) -> p q t", q=4), d_hi[:, fs, ts].bitcast(F32),
                        ALU.subtract).then_inc(S["n_lo"], 1)

            def norm(batch, src, d_hi, d_lo):
                norm_stats(batch)
                for i in range(batch[2]):
                    norm_xn(batch, i, src)
                    if i:
                        norm_lo(batch, i - 1, d_hi, d_lo)
                norm_lo(batch, batch[2] - 1, d_hi, d_lo)

            def cut_lo(s0, c0, nk, src):
                def step(i, j):
                    k = 4 * i + j
                    dve.wait_ge(S["cut_hi"], c0 + k + 1)
                    TTn(a_lo[:, j % 2, :], src(k), a_hi[:, j % 2, :].bitcast(F32), ALU.subtract).then_inc(S["cut_lo"], 1)
                n = nk // 4
                for j in range(4):
                    step(0, j)
                if n > 2:
                    with dve.Fori(1, n - 1) as i:
                        for j in range(4):
                            step(i, j)
                for j in range(4):
                    step(n - 1, j)

            def add_residual(s_end):
                dve.wait_ge(S["slab_used"], s_end)
                for t in range(TT):
                    for f in range(2):
                        x = x_res[:, t, f * HALF:(f + 1) * HALF]
                        TTn(x, x, B[2 * t + f][:], ALU.add).then_inc(S["x_add"], 1)

            dve.wait_ge(S["x_in"], 16 * TT)
            norm_stats(N1)
            norm_xn(N1, 0, lambda i: x_res[:, i, :])
            dve.wait_ge(S["par_in"], PAR_DMAS * 16)
            dve.wait_ge(S["rows_tr"], 1)
            V.tensor_copy(cw_g[:], B[0][:, 0:96])
            V.tensor_copy(cw_s[:], B[0][:, 96:144])
            V.tensor_copy(vec[:], B[0][:, 144:144 + VROWS]).then_inc(S["rows_cp"], 1)
            dve.wait_ge(S["wsm_hi_ok"], 1)
            TTn(wsm_lo[:], wsm[:], wsm_hi[:].bitcast(F32), ALU.subtract).then_inc(S["wsm_lo_ok"], 1)
            for i in range(1, TT):
                norm_xn(N1, i, lambda i: x_res[:, i, :])
                norm_lo(N1, i - 1, h_hi, h_lo)
            norm_lo(N1, TT - 1, h_hi, h_lo)

            step = [0]

            def link(ins):
                step[0] += 1
                ins.then_inc(S["gate_dve"], 1)
                dve.wait_ge(S["gate_dve"], step[0])

            def heads(ap):
                return ap.unsqueeze(1).to_broadcast([P, TT, HEADS])

            def kind(k, lo=0, hi=HEADS):
                return gates[:, lo:hi, k, :].rearrange("p h c -> p c h")

            dve.wait_ge(S["gate_mm"], 1)
            link(V.tensor_copy(gr[:], B[1][:, 0:TT * 32].rearrange("p (c n) -> p c n", c=TT)))
            link(TTn(gt[:, 0], gr[:, :, HG:], heads(brow[:]), ALU.add))
            V.scalar_tensor_tensor(out=gt[:, 1], in0=gt[:, 0], scalar=-1.0, in1=gt[:, 0], op0=ALU.mult, op1=ALU.max).then_inc(S["gate_raw"], 1)
            dve.wait_ge(S["gate_act"], 1)
            link(V.tensor_scalar(gt[:, 3, :, 0:HG], gt[:, 3, :, 0:HG], 1.0, None, ALU.add))
            link(V.reciprocal(kind(G_BETA, 0, HG), gt[:, 3, :, 0:HG]))
            link(V.tensor_scalar(gt[:, 4], gt[:, 2], 2.0, None, ALU.add))
            link(V.reciprocal(gt[:, 4], gt[:, 4]))
            link(TTn(gt[:, 4], gt[:, 4], gt[:, 2], ALU.mult))
            link(TTn(gt[:, 5], gt[:, 4], gt[:, 4], ALU.mult))
            link(V.tensor_scalar(gt[:, 6], gt[:, 5], 1.0 / 15, None, ALU.mult))
            for n in (13, 11, 9, 7, 5, 3):
                link(V.scalar_tensor_tensor(out=gt[:, 6], in0=gt[:, 6], scalar=1.0 / n, in1=gt[:, 5], op0=ALU.add, op1=ALU.mult))
            link(V.scalar_tensor_tensor(out=gt[:, 6], in0=gt[:, 6], scalar=1.0, in1=gt[:, 4], op0=ALU.add, op1=ALU.mult))
            link(V.tensor_scalar(gt[:, 6], gt[:, 6], 2.0, None, ALU.mult))
            link(V.scalar_tensor_tensor(out=gt[:, 7], in0=gt[:, 0], scalar=0.0, in1=gt[:, 6], op0=ALU.max, op1=ALU.add))
            V.tensor_copy(kind(G_BETA, HG), gt[:, 7, :, HG:])
            link(V.scalar_tensor_tensor(out=gt[:, 5], in0=gt[:, 7], scalar=-1.0, in1=heads(arow[:]), op0=ALU.mult, op1=ALU.mult))
            V.tensor_copy(kind(G_G), gt[:, 5]).then_inc(S["gate_cs"], 1)
            dve.wait_ge(S["gate_mm"], 2)
            link(V.tensor_copy(gt[:, 8].rearrange("p c h -> p (c h)"), B[2][:, 0:TT * HEADS]))
            link(V.tensor_copy(gt[:, 9].rearrange("p c h -> p (c h)"), B[3][:, 0:TT * HEADS]))
            TTn(gt[:, 0], gt[:, 9], gt[:, 8], ALU.subtract).then_inc(S["gate_raw"], 1)
            dve.wait_ge(S["gate_act"], 2)
            V.tensor_scalar(kind(G_NEG), gt[:, 8], -1.0, None, ALU.mult)
            V.tensor_scalar(kind(G_NEXP), gt[:, 2], -1.0, None, ALU.mult)
            V.tensor_copy(kind(G_DEC), gt[:, 1])
            V.tensor_copy(kind(G_CD), gt[:, 3]).then_inc(S["gates_ok"], 1)
            dve.wait_ge(S["gates_ok"], 1)

            def taps(acc, bank, w, sem_, n0):
                for d in range(1, TAPS):
                    if d > 1:
                        dve.wait_ge(sem_, n0 + d - 1)
                    V.scalar_tensor_tensor(out=acc[:, d:], in0=bank[:, 0:T - d], scalar=w(TAPS - 1 - d), in1=acc[:, d:],
                                           op0=ALU.mult, op1=ALU.add).then_inc(sem_, 1)

            def gdn_iter(h, a_, b, par, dense, inv, chain):
                pa, pb = 1 - par, par

                def cw():
                    V.tensor_copy(cwB[:, par, :], cw_g[:].rearrange("p (x h) -> p x h", h=HG)[:, :, bass.ds(h, 1)]
                                  .rearrange("p x o -> p (x o)")).then_inc(S["d_cw"], 1)

                def cols():
                    V.tensor_copy(colB[:, pa, :, :].rearrange("p k c -> p (k c)"),
                                  gates[:, bass.ds(a_, 1), :, :].rearrange("p o k c -> p (o k c)")).then_inc(S["d_cols"], 1)

                def ss():
                    dve.wait_ge(S["pe_ss"], a_ + 1)
                    need(dve, S["a_rinv"], a_)
                    V.tensor_scalar(ssA[:, 0, :], B[5][:, 0:TT], EPS, None, ALU.add).then_inc(S["d_sse"], 1)
                    dve.wait_ge(S["d_sse"], a_ + 1)
                    V.reciprocal(ssA[:, 2, :], ssA[:, 0, :]).then_inc(S["d_rec"], 1)
                    dve.wait_ge(S["d_rec"], a_ + 1)
                    dve.wait_ge(S["d_cols"], a_ + 1)
                    need(dve, S["a_v"], 4 * (a_ - 1))
                    TTn(br2B[:, pa, 0, :], ssA[:, 2, :], colB[:, pa, G_BETA, :], ALU.mult).then_inc(S["d_br"], 1)
                    dve.wait_ge(S["d_br"], a_ + 1)
                    V.tensor_scalar(br2B[:, pa, 1, :], br2B[:, pa, 0, :], -1.0, None, ALU.mult).then_inc(S["d_nb"], 1)

                def kb():
                    dve.wait_ge(S["a_silu"], 3 * a_ + 2)
                    need(dve, S["pe_o"], a_ - 1)
                    V.tensor_copy(kB[:, pa, :], kA[:]).then_inc(S["d_kb"], 1)

                def qd():
                    dve.wait_ge(S["a_eg"], a_ + 1)
                    TTn(qdB[:, pa, :], qA[:], eg[:], ALU.mult).then_inc(S["d_qd"], 1)

                def kd():
                    dve.wait_ge(S["pe_kt"], a_ + 1)
                    TTn(kdB[:, pa, :].rearrange("p (c d) -> p c d", c=TT), B[4][:].rearrange("p (c d) -> p c d", c=TT),
                        bcast(colB[:, pa, G_DEC, :], P), ALU.mult).then_inc(S["d_kd"], 1)

                def u():
                    dve.wait_ge(S["pe_kk"], a_ + 1)
                    dve.wait_ge(S["a_dt"], a_ + 1)
                    dve.wait_ge(S["d_nb"], a_ + 1)
                    for c in range(TT):
                        m = V.scalar_tensor_tensor(out=chunk(u_neg, c), in0=chunk(B[2], c), scalar=br2B[:, pa, 1, c:c + 1],
                                                   in1=chunk(dt_, c), op0=ALU.mult, op1=ALU.mult)
                    m.then_inc(S["d_u"], 1)

                def off(l):
                    dve.wait_ge(S["d_u"], a_ + 1)
                    need(dve, S["pe_x"], 6 * a_ + max(l - 2, 0))
                    TTn(u_off[:, l % 2, :].rearrange("p (c t) -> p c t", c=TT), u_neg[:].rearrange("p (c t) -> p c t", c=TT),
                        cst[:, C_MASK + l, :].unsqueeze(1).to_broadcast([P, TT, P]), ALU.mult).then_inc(S["d_off"], 1)

                def n1():
                    dve.wait_ge(S["d_off"], 7 * a_ + 1)
                    need(dve, S["pe_n"], 6 * a_)
                    TTn(nW[:].rearrange("p (c t) -> p c t", c=TT), u_off[:, 0, :].rearrange("p (c t) -> p c t", c=TT),
                        ident.unsqueeze(1).to_broadcast([P, TT, P]), ALU.add).then_inc(S["d_n"], 1)

                def at():
                    dve.wait_ge(S["pe_kq"], a_ + 1)
                    TTn(atB[:, pa, :], B[3][:], dt_[:], ALU.mult).then_inc(S["d_at"], 1)

                def vb():
                    dve.wait_ge(S["pe_vt"], a_ + 1)
                    dve.wait_ge(S["a_rinv"], a_ + 1)
                    TTn(vB[:, pa, :].rearrange("p (c d) -> p c d", c=TT), B[7][:].rearrange("p (c d) -> p c d", c=TT),
                        bcast(ssA[:, 1, :], P), ALU.mult).then_inc(S["d_v"], 1)

                def nn(l):
                    dve.wait_ge(S["pe_n"], 6 * a_ + l)
                    dve.wait_ge(S["d_n"], 7 * a_ + l)
                    dst = nB[:, pa, :] if l == LEVELS - 1 else nW[:]
                    TTn(dst, nW[:], B[3][:], ALU.add).then_inc(S["d_n"], 1)

                def r(c):
                    dve.wait_ge(S["pe_ks"], 3 * b + c)
                    V.scalar_tensor_tensor(out=rR[:], in0=B[5][:, 0:P], scalar=colB[:, pb, G_NEXP, c:c + 1],
                                           in1=chunk(vB[:, pb, :], c), op0=ALU.mult, op1=ALU.add).then_inc(S["d_r"], 1)

                def s(c):
                    dve.wait_ge(S["pe_s"], 3 * b + c + 1)
                    if c == 0:
                        V.tensor_copy(stS[:], B[5][:, 0:P]).then_inc(S["d_s"], 1)
                    else:
                        dve.wait_ge(S["d_s"], 3 * b + c)
                        V.scalar_tensor_tensor(out=stS[:], in0=stS[:], scalar=colB[:, pb, G_CD, c:c + 1], in1=B[5][:, 0:P],
                                               op0=ALU.mult, op1=ALU.add).then_inc(S["d_s"], 1)

                def mixb():
                    return mix[:, bass.ds(b, 1), :].rearrange("p o t -> p (o t)")

                def oz_():
                    dve.wait_ge(S["a_o2"], b + 1)
                    dve.wait_ge(S["z_done"], b + 1)
                    need(dve, S["mix_done"], b)
                    V.scalar_tensor_tensor(out=oz[:], in0=B[6][:], scalar=vec[:, V_GN:V_GN + 1], in1=mixb(),
                                           op0=ALU.mult, op1=ALU.mult).then_inc(S["d_oz"], 1)

                def fe():
                    dve.wait_ge(S["pe_f"], b + 1)
                    V.tensor_scalar(fW[:, 0, :], B[5][:, 0:TT], EPS * EPS * P, None, ALU.add).then_inc(S["d_fe"], 1)

                def fr():
                    dve.wait_ge(S["a_rf"], b + 1)
                    V.reciprocal(fW[:, 2, :], fW[:, 1, :]).then_inc(S["d_fr"], 1)

                def mx_():
                    dve.wait_ge(S["pe_fb"], b + 1)
                    dve.wait_ge(S["d_oz"], b + 1)
                    TTn(mixb(), oz[:], B[5][:], ALU.mult).then_inc(S["mix_done"], 1)

                def conv(t):
                    dve.wait_ge(S["a_tap"], 3 * h + t + 1)
                    taps(cacc[:, t % 2, :], B[t % 2], lambda x: cwB[:, par, 3 * x + t:3 * x + t + 1], S["d_tap"], 9 * h + 3 * t)

                I = lambda f, *x: f(*x) if inv else None
                C = lambda f, *x: f(*x) if chain else None
                H = lambda f, *x: f(*x) if dense else None
                I(cols); H(cw); I(ss); I(kb); I(qd); I(kd)
                C(s, 0); C(r, 1)
                I(u); I(off, 0); I(n1); I(at); I(off, 1)
                C(s, 1); I(vb); C(r, 2)
                I(nn, 1); C(s, 2); I(off, 2); C(r, 3)
                H(conv, 0); I(nn, 2); I(off, 3)
                C(oz_); C(fe); C(fr); I(nn, 3); I(off, 4)
                C(mx_); H(conv, 1)
                I(nn, 4); I(off, 5)
                I(nn, 5); I(off, 6)
                H(conv, 2)
                I(nn, 6)

            gdn_iter(0, None, None, 0, True, False, False)
            gdn_iter(1, 0, None, 1, True, True, False)
            gdn_iter(2, 1, 0, 0, True, True, True)
            gdn_iter(3, 2, 1, 1, True, True, True)
            with dve.Fori(2, HG // 2) as i:
                gdn_iter(2 * i, 2 * i - 1, 2 * i - 2, 0, True, True, True)
                gdn_iter(2 * i + 1, 2 * i, 2 * i - 1, 1, True, True, True)
            gdn_iter(None, HG - 1, HG - 2, 0, False, True, True)
            gdn_iter(None, None, HG - 1, 1, False, False, True)

            for n in range(4):
                dve.wait_ge(S["as_tap"], n + 1)
                taps(cacc[:, n % 2, :], B[n % 2], lambda x: cw_s[:, 12 * x + 8 + n:12 * x + 9 + n], S["ds_tap"], 3 * n)

            def ssd_iter(j, i, par, dense, ssd_):
                pi = 1 - par

                def v3(ap):
                    return ap.rearrange("p (c u d) -> p c u d", c=TT, u=2)

                def hcol(k):
                    x = colS[:, :, k, :].rearrange("p u c -> p c u")
                    return x.unsqueeze(3).to_broadcast([P, TT, 2, HP])

                if dense:
                    V.tensor_copy(cwS[:, par, 0:TAPS], cw_s[:].rearrange("p (x n) -> p x n", n=12)[:, :, bass.ds(j, 1)]
                                  .rearrange("p x o -> p (x o)"))
                    V.tensor_copy(cwS[:, par, 5:6], dcol[:, bass.ds(j, 1)])
                    V.tensor_copy(cwS[:, par, 4:5], vec[:, bass.ds(V_CB + j, 1)]).then_inc(S["ds_cw"], 1)
                if ssd_:
                    g = i // 4
                    need(dve, S["ps_g"], 2 * i)
                    need(dve, S["as_dt"], 2 * i)
                    V.tensor_copy(colS[:].rearrange("p u k c -> p (u k c)"),
                                  gates[:, bass.ds(HG + 2 * i, 2), :, :].rearrange("p u k c -> p (u k c)")).then_inc(S["ds_cols"], 1)
                    need(dve, S["ps_st"], i)
                    V.tensor_copy(b_cur[:], b_tok[:, bass.ds(g, 1), :].rearrange("p o t -> p (o t)")).then_inc(S["ds_bcur"], 1)
                    dve.wait_ge(S["ps_x"], i + 1)
                    dve.wait_ge(S["ds_cols"], i + 1)
                    need(dve, S["ps_y"], i)
                    TTn(v3(xdt[:]), v3(B[3][:]), hcol(G_BETA), ALU.mult).then_inc(S["ds_xdt"], 1)
                    dve.wait_ge(S["ds_xdt"], i + 1)
                    TTn(v3(xdd[:]), v3(xdt[:]), hcol(G_DEC), ALU.mult).then_inc(S["ds_xdd"], 1)
                    for hh in range(2):
                        dve.wait_ge(S["as_eg"], 2 * i + hh + 1)
                        TTn(cdS[:, hh, :], bcA[:, bass.ds(GROUPS + g, 1), :].rearrange("p o t -> p (o t)"), egS[:, hh, :],
                            ALU.mult).then_inc(S["ds_cd"], 1)
                    for hh in range(2):
                        dve.wait_ge(S["as_dt"], 2 * i + hh + 1)
                        TTn(scS[:, hh, :], cb[:, bass.ds(g, 1), :].rearrange("p o t -> p (o t)"), dtS[:, hh, :],
                            ALU.mult).then_inc(S["ds_sc"], 1)
                if dense:
                    dve.wait_ge(S["as_tap"], 5 + j)
                    taps(cacc[:, par, :], B[0], lambda x: cwS[:, par, x:x + 1], S["ds_tap"], 3 * (4 + j))
                if ssd_:
                    dve.wait_ge(S["ps_st"], i + 1)
                    V.tensor_copy(hst[:, 0, :], B[4][:, 0:P]).then_inc(S["ds_h"], 1)
                    for c in (1, 2):
                        dve.wait_ge(S["ds_h"], 3 * i + c)
                        for hh in range(2):
                            hs = slice(hh * HP, (hh + 1) * HP)
                            m = V.scalar_tensor_tensor(out=hst[:, c, hs], in0=hst[:, c - 1, hs], scalar=colS[:, hh, G_CD, c:c + 1],
                                                       in1=B[4][:, c * P + hh * HP:c * P + (hh + 1) * HP],
                                                       op0=ALU.mult, op1=ALU.add)
                        m.then_inc(S["ds_h"], 1)
                    dve.wait_ge(S["ps_y"], i + 1)
                    V.scalar_tensor_tensor(out=y1[:], in0=xA[:, pi, :], scalar=cwS[:, pi, 5:6], in1=B[6][:],
                                           op0=ALU.mult, op1=ALU.add).then_inc(S["ds_y1"], 1)
                    dve.wait_ge(S["ds_y1"], i + 1)
                    dve.wait_ge(S["zs_done"], i + 1)
                    mi = mix[:, bass.ds(HG + i, 1), :].rearrange("p o t -> p (o t)")
                    TTn(mi, y1[:], mi, ALU.mult).then_inc(S["ds_mix"], 1)

            ssd_iter(0, None, 0, True, False)
            for g in range(GROUPS):
                dve.wait_ge(S["pb_cb"], g + 1)
                V.tensor_copy(cb[:, g, :], B[4 + g][:]).then_inc(S["db_cb"], 1)
            dve.wait_ge(S["db_cb"], GROUPS)
            dve.wait_ge(S["ab_tok"], GROUPS)
            ssd_iter(1, 0, 1, True, True)
            with dve.Fori(1, XT // 2) as q:
                ssd_iter(2 * q, 2 * q - 1, 0, True, True)
                ssd_iter(2 * q + 1, 2 * q, 1, True, True)
            ssd_iter(None, XT - 1, 0, False, True)
            for g in range(GROUPS):
                dve.wait_ge(S["gn_sum"], g + 1)
                V.tensor_scalar(y_root[:, g, :], B[g][:], 1.0 / (4 * P), EPS, ALU.mult, ALU.add).then_inc(S["gn_mean"], 1)
            norm(NM, lambda i: mx[:, i, :], m_hi, m_lo)
            for g in range(GROUPS):
                dve.wait_ge(S["gn_root"], g + 1)
                V.reciprocal(y_root[:, g, :], y_root[:, g, :]).then_inc(S["gn_rec"], 1)
                dve.wait_ge(S["gn_rec"], g + 1)
                for q in range(4):
                    mi = mix[:, HG + 4 * g + q, :]
                    V.scalar_tensor_tensor(out=mi, in0=mi, scalar=vec[:, V_NW + 4 * g + q:V_NW + 4 * g + q + 1],
                                           in1=y_root[:, g, :], op0=ALU.mult, op1=ALU.mult).then_inc(S["gn_mix"], 1)

            cut_lo(S_OUT, 0, MIX, lambda k: mix[:, bass.ds(k, 1), :].rearrange("p o t -> p (o t)"))
            add_residual(S_OUT + MIX)
            norm(N2, lambda i: x_res[:, i, :], h_hi, h_lo)

            for hd in range(AH):
                e = hd % 2
                need(dve, S["at_exp"], TT * (hd - 1))
                for u in range(2):
                    dve.wait_ge(S["at_s"], 2 * hd + u + 1)
                    m = V.tensor_reduce(sm[:, e, 0, 2 * u:2 * u + 2], B[2 + u][:].rearrange("p (t m) -> p t m", t=2), AX.X, ALU.max)
                m.then_inc(S["at_max"], 1)
                dve.wait_ge(S["at_max"], hd + 1)
                V.tensor_scalar(sm[:, e, 1, :], sm[:, e, 0, :], -float(HD) ** -0.5, None, ALU.mult).then_inc(S["at_neg"], 1)
                dve.wait_ge(S["at_exp"], TT * (hd + 1))
                V.reciprocal(sm[:, e, 3, :], sm[:, e, 2, :]).then_inc(S["at_rec"], 1)
                dve.wait_ge(S["at_rec"], hd + 1)
                TTn(pr[:, e], pr[:, e], bcast(sm[:, e, 3, :], M), ALU.mult).then_inc(S["at_pn"], 1)
                for mt_ in range(MT):
                    dve.wait_ge(S["at_tr"], MT * hd + mt_ + 1)
                    need(dve, S["at_pv"], 2 * (hd - 1))
                    V.tensor_copy(prT[:, e, mt_, :], B[4 + mt_][:]).then_inc(S["at_prt"], 1)

            dve.wait_ge(S["at_o"], 2 * AH)
            cut_lo(S_WO, MIX, KT, lambda k: oT[:, k, :])
            add_residual(S_WO + KT)
            norm(N3, lambda i: x_res[:, i, :], h_hi, h_lo)

            def square(i, j):
                n = 4 * i + j
                dve.wait_ge(S["up_relu"], n + 1)
                TTn(uT[:, bass.ds(n, 1), :].rearrange("p o t -> p (o t)"), ur[:, j % 2, :], ur[:, j % 2, :],
                    ALU.mult).then_inc(S["up_sq"], 1)

            for j in range(4):
                square(0, j)
            with dve.Fori(1, FT // 4) as i:
                for j in range(4):
                    square(i, j)
            dve.wait_ge(S["up_sq"], FT)
            cut_lo(S_DOWN, MIX + KT, FT, lambda k: uT[:, bass.ds(k, 1), :].rearrange("p o t -> p (o t)"))
            add_residual(S_DOWN + FT)
            norm_stats(NF)
            for i in range(TT):
                V.scalar_tensor_tensor(out=x_res[:, i, :], in0=x_res[:, i, :], scalar=stat[:, 5, i:i + 1], in1=nrow[:],
                                       op0=ALU.mult, op1=ALU.mult).then_inc(S["fin_y"], 1)


PAR_DMAS = 13
N_SLABS = S_END

INPUTS = ["x", "mem", "norm1_w", "w_in", "gdn_conv_w", "gdn_a_log", "gdn_dt_bias", "gdn_norm_w", "ssm_conv_w",
          "ssm_conv_b", "ssm_a_log", "ssm_dt_bias", "ssm_d", "ssm_norm_w", "w_out", "norm2_w", "mem_norm_w",
          "wq_mem", "wk_mem", "wv_mem", "wo_mem", "norm3_w", "w_up", "w_down", "final_norm_w"]


def kernel(**inputs):
    import ml_dtypes
    import concourse.bacc as bacc
    from concourse.bass_utils import run_bass_kernel_spmd

    nc = bacc.Bacc("TRN2", target_bir_lowering=False, num_devices=1)
    arrays, aps = {}, {}
    host = {n: np.ascontiguousarray(inputs[n]) for n in INPUTS}
    host["const"] = constants()
    host["negm"] = neg_mask().astype(ml_dtypes.bfloat16)
    for name, arr in host.items():
        arrays[f"in_{name}"] = arr
        aps[name] = nc.dram_tensor(f"in_{name}", arr.shape, mybir.dt.from_np(arr.dtype), kind="ExternalInput").ap()
    out = nc.dram_tensor("out_0", (1, T, D), F32, kind="ExternalOutput").ap()
    layer(nc, aps, out)
    r = run_bass_kernel_spmd(nc, [arrays], core_ids=[0])
    return r.results[0]["out_0"]
```

```python
from contextlib import ExitStack

import concourse.bass as bass
import numpy as np
from concourse import mybir

F32 = mybir.dt.float32
F32R = mybir.dt.float32r
BF16 = mybir.dt.bfloat16
ALU = mybir.AluOpType
ACT = mybir.ActivationFunctionType
AX = mybir.AxisListType

P = 128
D = 1024
T = 512
M = 256
KT = D // P
TT = T // P
MT = M // P
HALF = 512
EPS = 1e-6
TAPS = 4
HG = 8
GDN = HG * P
GDN_COLS = 4 * GDN + 2 * HG
HS = 16
HP = 64
XT = D // P
GROUPS = 2
BC = GROUPS * P
HEADS = HG + HS
MIX = (GDN + D) // P
FF = 4 * D
FT = FF // P
AH = 4
HD = D // AH
LEVELS = 7
SLOTS = 4
RAW_SLOTS = 2
SLAB = 1024

S_GDN = 0
S_BC = S_GDN + 4 * HG
S_XZ = S_BC + 4
S_OUT = S_XZ + 2 * XT
S_WK = S_OUT + MIX
S_WV = S_WK + KT
S_WQ = S_WV + KT
S_WO = S_WQ + KT
S_UP = S_WO + KT
S_DOWN = S_UP + FT
S_END = S_DOWN + FT

C_ID, C_TRI, C_ONES, C_VEC, C_MASK = 0, 1, 2, 3, 4
NCONST = C_MASK + LEVELS
V_CB, V_NW, V_GN, VROWS = 0, 12, 20, 21
G_G, G_NEG, G_NEXP, G_DEC, G_CD, G_BETA, KINDS = 0, 1, 2, 3, 4, 5, 6
NORM_TILES = 4 * TT + MT


def constants():
    c = np.zeros((P, NCONST, P), np.float32)
    s, t = np.arange(P)[:, None], np.arange(P)[None, :]
    c[:, C_ID] = s == t
    c[:, C_TRI] = s <= t
    c[:, C_ONES] = 1.0
    c[:, C_VEC, 0] = 1.0 / P
    c[:, C_VEC, 1] = EPS * P
    c[:, C_VEC, 2] = 1.0
    for l in range(LEVELS):
        c[:, C_MASK + l] = ((s >> (l + 1)) == (t >> (l + 1))) & ((s >> l) + 1 == (t >> l))
    return c


def neg_mask():
    m = np.zeros((P, 1 + TT, P), np.float32)
    s, t = np.arange(P)[:, None], np.arange(P)[None, :]
    m[:, 0] = s == t
    m[:, 1:] = np.where(s > t, -1e30, 0.0)[:, None, :]
    return m


def need(eng, sem, n):
    if isinstance(n, int) and n <= 0:
        return
    eng.wait_ge(sem, n)


def layer(nc, a, out):
    with ExitStack() as ctx:
        def sb(name, shape, dt=F32):
            return ctx.enter_context(nc.sbuf_tensor(name, shape, dt))

        def sem(name):
            return ctx.enter_context(nc.semaphore(name))

        B = [ctx.enter_context(nc.psum_tensor(f"bank{i}", [P, HALF], F32)) for i in range(8)]

        raw = sb("raw", [P, RAW_SLOTS, SLAB])
        w_hi = sb("w_hi", [P, SLOTS, SLAB], F32R)
        w_lo = sb("w_lo", [P, SLOTS, SLAB], F32R)
        h_hi = sb("h_hi", [P, KT, T], F32R)
        h_lo = sb("h_lo", [P, KT, T], F32R)
        cst = sb("cst", [P, NCONST, P])
        negm = sb("negm", [P, 1 + TT, P], BF16)
        x0_scope = ExitStack()
        x0 = x0_scope.enter_context(nc.sbuf_tensor("x0", [P, TT, D], F32))
        x0_scope.close()
        m_hi = sb("m_hi", [P, KT, M], F32R)
        m_lo = sb("m_lo", [P, KT, M], F32R)
        nrow = sb("nrow", [P, D])
        xn = sb("xn", [P, D])
        stat = sb("stat", [P, 6, NORM_TILES])
        ident, tri, ones = cst[:, C_ID, :], cst[:, C_TRI, :], cst[:, C_ONES, :]

        def mb(name, shape, dt=F32, where=ctx):
            return where.enter_context(nc.sbuf_tensor(name, shape, dt))

        mixing = ExitStack()
        mix = mb("mix", [P, MIX, T], where=mixing)
        vec = mb("vec", [P, VROWS], where=mixing)
        inner = ExitStack()
        cw_g = mb("cw_g", [P, TAPS * 24], where=inner)
        cw_s = mb("cw_s", [P, TAPS * 12], where=inner)
        dcol = mb("dcol", [P, XT], where=inner)
        gates = mb("gates", [P, HEADS, KINDS, TT], where=inner)
        cacc = mb("cacc", [P, 2, T], where=inner)

        bcA = mb("bcA", [P, 4, T], where=inner)

        gdn = ExitStack()
        qA = mb("qA", [P, T], where=gdn)
        kA = mb("kA", [P, T], where=gdn)
        vA = mb("vA", [P, T], where=gdn)
        cwB = mb("cwB", [P, 2, 12], where=gdn)
        colB = mb("colB", [P, 2, KINDS, TT], where=gdn)
        br2B = mb("br2B", [P, 2, 2, TT], where=gdn)
        ssA = mb("ssA", [P, 3, TT], where=gdn)
        sqW = mb("sqW", [P, T], where=gdn)

        start = ExitStack()
        rows_g = mb("rows_g", [96, P], where=start)
        rows_s = mb("rows_s", [48, P], where=start)
        rows_v = mb("rows_v", [VROWS, P], where=start)
        wsm = mb("wsm", [P, KT, 32], where=start)
        wsm_hi = mb("wsm_hi", [P, KT, 32], F32R, start)
        wsm_lo = mb("wsm_lo", [P, KT, 32], F32R, start)
        brow = mb("brow", [P, HEADS], where=start)
        arow = mb("arow", [P, HEADS], where=start)
        graw = mb("graw", [32, T], where=start)
        gr = mb("gr", [P, TT, 32], where=start)
        gt = mb("gt", [P, 10, TT, HEADS], where=start)
        mx = mb("mx", [P, MT, D], where=start)
        start.close()

        kB = mb("kB", [P, 2, T], where=gdn)
        qdB = mb("qdB", [P, 2, T], where=gdn)
        q_sqB = mb("q_sqB", [P, 2, T], where=gdn)
        vB = mb("vB", [P, 2, T], where=gdn)
        kdB = mb("kdB", [P, 2, T], where=gdn)
        atB = mb("atB", [P, 2, T], where=gdn)
        nB = mb("nB", [P, 2, T], where=gdn)
        eg = mb("eg", [P, T], where=gdn)
        dt_ = mb("dt_", [P, T], where=gdn)
        u_neg = mb("u_neg", [P, T], where=gdn)
        u_off = mb("u_off", [P, 2, T], where=gdn)
        nW = mb("nW", [P, T], where=gdn)
        mW = mb("mW", [P, T], where=gdn)
        xW = mb("xW", [P, T], where=gdn)
        stS = mb("stS", [P, P], where=gdn)
        rR = mb("rR", [P, P], where=gdn)
        vN = mb("vN", [P, P], where=gdn)
        oz = mb("oz", [P, T], where=gdn)
        fW = mb("fW", [P, 3, TT], where=gdn)
        gdn.close()

        ssd = ExitStack()
        b_tok = mb("b_tok", [P, GROUPS, T], where=ssd)
        cb = mb("cb", [P, GROUPS, T], where=ssd)
        b_cur = mb("b_cur", [P, T], where=ssd)
        colS = mb("colS", [P, 2, KINDS, TT], where=ssd)
        cwS = mb("cwS", [P, 2, 6], where=ssd)
        ssq = mb("ssq", [P, XT, TT], where=ssd)
        gnS = mb("gnS", [P, 4, GROUPS, TT], where=ssd)
        xA = mb("xA", [P, 2, T], where=ssd)
        egS = mb("egS", [P, 2, T], where=ssd)
        dtS = mb("dtS", [P, 2, T], where=ssd)
        cdS = mb("cdS", [P, 2, T], where=ssd)
        scS = mb("scS", [P, 2, T], where=ssd)
        xdt = mb("xdt", [P, T], where=ssd)
        xdd = mb("xdd", [P, T], where=ssd)
        hst = mb("hst", [P, 3, P], where=ssd)
        y1, y_sq = bcA[:, 0, :], bcA[:, 1, :]
        ssd.close()
        inner.close()
        mixing.close()

        att = ExitStack()
        kmT = mb("kmT", [P, KT, M], where=att)
        v_m = mb("v_m", [P, MT, D], where=att)
        pr = mb("pr", [P, 2, TT, M], where=att)
        prT = mb("prT", [P, 2, MT, T], where=att)
        qmT = mb("qmT", [P, KT, T], where=att)
        oT = mb("oT", [P, KT, T], where=att)
        att.close()

        uT = mb("uT", [P, FT, T])
        ur = mb("ur", [P, 2, T])
        x_res = mb("x_res", [P, TT, D])
        a_hi = mb("a_hi", [P, 4, T], F32R)
        a_lo = mb("a_lo", [P, 4, T], F32R)
        sq_out = mb("sq_out", [P, HALF])
        sm = mb("sm", [P, 2, 4, TT])

        names = """
        par_in cst_in n_row mem_in xr_in out_done
        slab_hi slab_ready slab_used
        n_sq n_add n_mean n_root n_rstd n_xn n_tr n_hi n_lo
        rows_tr rows_cp wsm_hi_ok wsm_lo_ok gate_mm gate_cp gate_raw gate_dve gate_act gate_cs gates_ok
        d_cols d_cw d_sse d_rec d_br d_nb d_kb d_qd d_kd d_u d_at d_v d_off d_n d_r d_s d_oz d_fe d_fr mix_done
        d_tap a_tap a_silu z_done
        pe_ss pe_g pe_gm pe_kk pe_kq pe_kt pe_vt pe_mt pe_x pe_n pe_ks pe_v pe_s pe_o pe_f pe_fb
        a_eg a_dt a_q2 a_rinv a_x a_m a_v a_o2 a_k2 a_rf
        as_tap ds_tap as_silu zs_done pb_tr pb_cb ab_tok db_cb
        ds_cw ds_cols ds_bcur ds_xdt ds_xdd ds_cd ds_sc ds_h ds_y1 ds_mix
        ps_g ps_m ps_x ps_st ps_y as_eg as_dt as_sq ps_sq ds_sq
        gn_sum gn_mean gn_root gn_rec
        cut_hi cut_lo row_done x_add km_ok vm_ok qm_ok
        at_s at_max at_neg at_exp at_rec at_pn at_tr at_prt at_pv at_o
        up_relu up_sq fin_y
        """.split()
        S = {n: sem(n) for n in names}
        x_in = [sem(f"x_in{t}") for t in range(TT)]
        raw_in = [sem(f"raw_in{j}") for j in range(RAW_SLOTS)]
        block = ctx.enter_context(nc.Block())

        def row(w):
            return w.rearrange("(o n) -> o n", o=1).partition_broadcast(P)

        N1, NM, N2, N3, NF = (0, 0, TT, 0), (1, TT, MT, 1), (2, TT + MT, TT, 0), (3, 2 * TT + MT, TT, 0), (4, 3 * TT + MT, TT, 0)

        def chunk(ap, c):
            return ap[:, c * P:(c + 1) * P]

        def bcast(ap, n):
            return ap.unsqueeze(2).to_broadcast([P, ap.shape[1], n])

        @block.sync
        def _(sp):
            w_in_v = a["w_in"].rearrange("(k p) n -> p k n", p=P)

            def slab(s, j, src):
                need(sp, S["slab_ready"], s - RAW_SLOTS + 1)
                dst = raw[:, j % RAW_SLOTS, :]
                if len(src.shape) == 3:
                    dst = dst.rearrange("p (k n) -> p k n", k=KT)
                sp.dma_start(dst, src).then_inc(raw_in[j % RAW_SLOTS], 16)

            def cols(w, c0):
                return w[:, :, bass.ds(c0, P)]

            def rows(w, r0):
                return w[bass.ds(r0, P), :]

            def gdn_slabs(h):
                for j in range(4):
                    slab(S_GDN + 4 * h + j, j, cols(w_in_v, j * GDN + h * P))

            for t in range(TT):
                sp.dma_start(x0[:, t, :], a["x"][0, t * P:(t + 1) * P, :]).then_inc(x_in[t], 16)
            slab(0, 0, cols(w_in_v, 0))
            slab(1, 1, cols(w_in_v, GDN))
            par = [
                (wsm[:, :, 0:16], w_in_v[:, :, 4 * GDN:4 * GDN + 16]),
                (wsm[:, :, 16:32], w_in_v[:, :, GDN_COLS + 2 * D + 2 * BC:]),
                (rows_g[:], a["gdn_conv_w"].rearrange("k (j p) -> (k j) p", p=P)),
                (rows_s[:], a["ssm_conv_w"].rearrange("k (j p) -> (k j) p", p=P)),
                (rows_v[V_CB:V_NW, :], a["ssm_conv_b"].rearrange("(j p) -> j p", p=P)),
                (rows_v[V_NW:V_GN, :], a["ssm_norm_w"].rearrange("(j p) -> j p", p=P)),
                (rows_v[V_GN:VROWS, :], a["gdn_norm_w"].rearrange("(j p) -> j p", p=P)),
                (brow[:, 0:HG], row(a["gdn_dt_bias"])), (brow[:, HG:], row(a["ssm_dt_bias"])),
                (arow[:, 0:HG], row(a["gdn_a_log"])), (arow[:, HG:], row(a["ssm_a_log"])),
                (negm[:], a["negm"]),
            ]
            for hh in range(2):
                d = a["ssm_d"].rearrange("(o j u) -> o j u", o=1, u=2)[:, :, hh]
                par.append((dcol[hh * HP:(hh + 1) * HP, :], d.partition_broadcast(HP)))
            assert len(par) == PAR_DMAS
            with nc.allow_non_contiguous_dma(reason="a few short rows and per-head scalars"):
                for dst, src in par:
                    sp.dma_start(dst, src).then_inc(S["par_in"], 16)
            sp.dma_start(mx[:], a["mem"].rearrange("b (t p) d -> p (b t) d", p=P)).then_inc(S["mem_in"], 16)
            slab(2, 2, cols(w_in_v, 2 * GDN))
            slab(3, 3, cols(w_in_v, 3 * GDN))
            with sp.Fori(1, HG) as h:
                gdn_slabs(h)
            for n in range(4):
                slab(S_BC + n, n, cols(w_in_v, GDN_COLS + 2 * D + n * P))

            def xz_slabs(i):
                for u in range(2):
                    slab(S_XZ + 4 * i + 2 * u, 2 * u, cols(w_in_v, GDN_COLS + D + (2 * i + u) * P))
                    slab(S_XZ + 4 * i + 2 * u + 1, 2 * u + 1, cols(w_in_v, GDN_COLS + (2 * i + u) * P))

            with sp.Fori(0, XT // 2) as i:
                xz_slabs(i)

            def row_slabs(w, s0, n):
                with sp.Fori(0, n // 4) as i:
                    for j in range(4):
                        slab(s0 + 4 * i + j, j, rows(w, (4 * i + j) * P))

            def col_slabs(w, s0, n):
                wv = w.rearrange("(k p) n -> p k n", p=P)
                with sp.Fori(0, n // 4) as i:
                    for j in range(4):
                        slab(s0 + 4 * i + j, j, cols(wv, (4 * i + j) * P))

            for k in range(6):
                slab(S_OUT + k, k % 4, rows(a["w_out"], k * P))
            sp.wait_ge(S["ds_mix"], XT)
            sp.wait_ge(S["ps_y"], XT)
            for t in range(TT):
                sp.dma_start(x_res[:, t, :], a["x"][0, t * P:(t + 1) * P, :]).then_inc(S["xr_in"], 16)
            for k in range(6, MIX):
                slab(S_OUT + k, k % 4, rows(a["w_out"], k * P))
            col_slabs(a["wk_mem"], S_WK, KT)
            row_slabs(a["wv_mem"], S_WV, KT)
            col_slabs(a["wq_mem"], S_WQ, KT)
            row_slabs(a["wo_mem"], S_WO, KT)
            col_slabs(a["w_up"], S_UP, FT)
            row_slabs(a["w_down"], S_DOWN, FT)
            for t in range(TT):
                sp.wait_ge(S["fin_y"], t + 1)
                sp.dma_start(out[0, t * P:(t + 1) * P, :], x_res[:, t, :]).then_inc(S["out_done"], 16)
            sp.wait_ge(S["out_done"], 16 * TT)

        @block.gpsimd
        def _(pool):
            def cut(i, j):
                s = 4 * i + j
                pool.wait_ge(S["slab_hi"], s + 1)
                nc.gpsimd.tensor_tensor(w_lo[:, j, :], raw[:, j % RAW_SLOTS, :], w_hi[:, j, :].bitcast(F32),
                                        ALU.subtract).then_inc(S["slab_ready"], 1)

            for j in range(SLOTS):
                cut(0, j)
            with pool.Fori(1, N_SLABS // SLOTS) as i:
                for j in range(SLOTS):
                    cut(i, j)

        @block.tensor
        def _(pe):
            mm = nc.tensor.matmul

            def dense_k(s, j, bank, k, r_hi=h_hi, r_lo=h_lo, n=T):
                if k == 0:
                    pe.wait_ge(S["slab_ready"], s + 1)
                wh, wl = w_hi[:, j, k * P:(k + 1) * P], w_lo[:, j, k * P:(k + 1) * P]
                mm(bank[:, 0:n], wh, r_hi[:, k, :], start=(k == 0), stop=False)
                mm(bank[:, 0:n], wh, r_lo[:, k, :], start=False, stop=False)
                m = mm(bank[:, 0:n], wl, r_hi[:, k, :], start=False, stop=(k == KT - 1))
                if k == KT - 1:
                    m.then_inc(S["slab_used"], 1)

            def norm_tile(batch, i):
                g = batch[1] + i
                pe.wait_ge(S["n_xn"], g + 1)
                for f in range(2):
                    bank = B[2 * (i + batch[3]) + f]
                    for q in range(4):
                        m = nc.tensor.transpose(chunk(bank, q), xn[:, (4 * f + q) * P:(4 * f + q + 1) * P], ident)
                    m.then_inc(S["n_tr"], 1)

            def row_tile(j, t, lh, ll, first, last, banks):
                for f in range(2):
                    fs = slice(f * HALF, (f + 1) * HALF)
                    mm(banks[2 * t + f][:], lh, w_hi[:, j, fs], start=first, stop=False)
                    mm(banks[2 * t + f][:], lh, w_lo[:, j, fs], start=False, stop=False)
                for f in range(2):
                    fs = slice(f * HALF, (f + 1) * HALF)
                    m = mm(banks[2 * t + f][:], ll, w_hi[:, j, fs], start=False, stop=last)
                return m

            def row_part(s0, c0, i, j, t, first=False, last=False):
                k = 4 * i + j
                pe.wait_ge(S["slab_ready"], s0 + k + 1)
                pe.wait_ge(S["cut_lo"], c0 + k + 1)
                m = row_tile(j, t, chunk(a_hi[:, j, :], t), chunk(a_lo[:, j, :], t), first, last, B)
                if t == TT - 1:
                    m.then_inc(S["slab_used"], 1)
                elif last:
                    m.then_inc(S["row_done"], 1)

            def row_last(s0, c0, i, first, norm_batch):
                for t in range(TT):
                    if first:
                        pe.wait_ge(S["x_add"], 2 * TT + 2 * t + 2)
                    for j in range(4):
                        row_part(s0, c0, i, j, t, first and j == 0, j == 3)
                    if t and norm_batch:
                        norm_tile(norm_batch, t - 1)

            pe.wait_ge(S["cst_in"], 16)
            for i in range(TT):
                norm_tile(N1, i)
            pe.wait_ge(S["par_in"], PAR_DMAS * 16)
            pe.wait_ge(S["n_lo"], 4)
            nc.tensor.transpose(B[2][:, 0:96], rows_g[:], cst[0:96, C_ID, 0:96])
            nc.tensor.transpose(B[2][:, 96:144], rows_s[:], cst[0:48, C_ID, 0:48])
            nc.tensor.transpose(B[2][:, 144:144 + VROWS], rows_v[:],
                                cst[0:VROWS, C_ID, 0:VROWS]).then_inc(S["rows_tr"], 1)
            pe.wait_ge(S["n_lo"], 2 * TT)
            pe.wait_ge(S["wsm_lo_ok"], 1)
            for k in range(KT):
                mm(B[6][0:32, :], wsm_hi[:, k, :], h_hi[:, k, :], start=(k == 0), stop=False)
                mm(B[6][0:32, :], wsm_hi[:, k, :], h_lo[:, k, :], start=False, stop=False)
                m = mm(B[6][0:32, :], wsm_lo[:, k, :], h_hi[:, k, :], start=False, stop=(k == KT - 1))
            m.then_inc(S["gate_mm"], 1)

            def gate_tokens():
                pe.wait_ge(S["gate_cp"], 1)
                pe.wait_ge(S["n_sq"], 2 * (TT + MT))
                for t in range(TT):
                    m = nc.tensor.transpose(B[7][:, t * 32:(t + 1) * 32], graw[:, t * P:(t + 1) * P], cst[0:32, C_ID, 0:32])
                m.then_inc(S["gate_mm"], 1)

            def gate_sums():
                pe.wait_ge(S["gate_cs"], 1)
                gsrc = gt[:, 5].rearrange("p c h -> p (c h)")
                mm(B[7][:, P:P + TT * HEADS], tri, gsrc, start=True, stop=True)
                mm(B[7][:, 2 * P:2 * P + TT * HEADS], ones, gsrc, start=True, stop=True).then_inc(S["gate_mm"], 1)

            for x in range(32):
                if x == 4:
                    gate_tokens()
                if x == 12:
                    pe.wait_ge(S["rows_cp"], 1)
                if x in (12, 15):
                    norm_tile(NM, (x - 12) // 3)
                if x == 28:
                    gate_sums()
                if x in (16, 24):
                    pe.wait_ge(S["d_tap"], 3 * (x // 8 - 1))
                dense_k(x // 8, x // 8, B[(x // 8) % 2], x % 8)

            def gdn_iter(h, a_, b, par, dense, inv, chain):
                pa, pb = 1 - par, par
                steps = iter(range({"head": 32, "bc": 32, "xz": 16, None: 0}[dense]))

                def D(n):
                    for _ in range(n):
                        x = next(steps, None)
                        if x is None:
                            return
                        j, k = x // 8, x % 8
                        if dense == "head":
                            if k == 0:
                                if j == 1:
                                    need(pe, S["z_done"], h)
                                else:
                                    need(pe, S["d_tap"], 9 * h + 3 * max(j - 1, 0))
                            dense_k(4 * h + j, j, B[j % 2], k)
                        elif dense == "bc":
                            if k == 0:
                                if j == 0:
                                    pe.wait_ge(S["d_tap"], 9 * HG)
                                elif j == 1:
                                    pe.wait_ge(S["z_done"], HG)
                                else:
                                    pe.wait_ge(S["ds_tap"], 3 * (j - 1))
                            dense_k(S_BC + j, j, B[j % 2], k)
                        else:
                            if k == 0:
                                pe.wait_ge(S["ds_tap"], 3 * (3 + j))
                            dense_k(S_XZ + j, j, B[j], k)

                def ss():
                    pe.wait_ge(S["a_k2"], a_ + 1)
                    need(pe, S["mix_done"], a_ - 1)
                    for c in range(TT):
                        m = mm(B[5][:, c:c + 1], chunk(sqW, c), ones[:, 0:1], start=True, stop=True)
                    m.then_inc(S["pe_ss"], 1)

                def gsum():
                    pe.wait_ge(S["d_cols"], a_ + 1)
                    need(pe, S["d_v"], a_)
                    for c in range(TT):
                        m = mm(chunk(B[7], c), colB[:, pa, G_G, c:c + 1].to_broadcast([P, P]), tri,
                               start=(c == 0), stop=False, skip_group_check=True)
                    m.then_inc(S["pe_g"], 1)

                def mask():
                    pe.wait_ge(S["a_eg"], a_ + 1)
                    mm(B[7][:], negm[:, 0, :], negm[:, 1:, :].rearrange("p c t -> p (c t)"), start=False,
                       stop=True, skip_group_check=True).then_inc(S["pe_gm"], 1)

                def kk():
                    need(pe, S["a_x"], 6 * a_)
                    pe.wait_ge(S["a_silu"], 3 * a_ + 2)
                    for c in range(TT):
                        m = mm(chunk(B[2], c), chunk(kA, c), chunk(kA, c), start=True, stop=True)
                    m.then_inc(S["pe_kk"], 1)

                def kq():
                    need(pe, S["d_n"], 7 * a_)
                    for c in range(TT):
                        m = mm(chunk(B[3], c), chunk(kA, c), chunk(qA, c), start=True, stop=True)
                    m.then_inc(S["pe_kq"], 1)

                def kt():
                    need(pe, S["a_m"], 6 * a_)
                    for c in range(TT):
                        m = nc.tensor.transpose(chunk(B[4], c), chunk(kA, c), ident)
                    m.then_inc(S["pe_kt"], 1)

                def vt():
                    pe.wait_ge(S["a_dt"], a_ + 1)
                    pe.wait_ge(S["a_silu"], 3 * a_ + 3)
                    for c in range(TT):
                        m = nc.tensor.transpose(chunk(B[7], c), chunk(vA, c), ident)
                    m.then_inc(S["pe_vt"], 1)

                def mt(l):
                    pe.wait_ge(S["d_n"], 7 * a_ + l + 1)
                    if l == 0:
                        pe.wait_ge(S["d_kd"], a_ + 1)
                    else:
                        pe.wait_ge(S["a_m"], 6 * a_ + l)
                    for c in range(TT):
                        m = nc.tensor.transpose(chunk(B[4], c), chunk(nW, c), ident)
                    m.then_inc(S["pe_mt"], 1)

                def xm(l):
                    pe.wait_ge(S["a_m"], 6 * a_ + l)
                    pe.wait_ge(S["d_off"], 7 * a_ + l + 1)
                    if l == 1:
                        pe.wait_ge(S["d_u"], a_ + 1)
                    else:
                        pe.wait_ge(S["a_x"], 6 * a_ + l - 1)
                    for c in range(TT):
                        m = mm(chunk(B[2], c), chunk(u_off[:, l % 2, :], c), chunk(mW, c), start=True, stop=True)
                    m.then_inc(S["pe_x"], 1)

                def nn(l):
                    pe.wait_ge(S["a_x"], 6 * a_ + l)
                    pe.wait_ge(S["d_n"], 7 * a_ + l)
                    if l == 1:
                        pe.wait_ge(S["d_at"], a_ + 1)
                    for c in range(TT):
                        m = mm(chunk(B[3], c), chunk(xW, c), chunk(nW, c), start=True, stop=True)
                    m.then_inc(S["pe_n"], 1)

                def ks(c):
                    pe.wait_ge(S["d_s"], 3 * b + c)
                    mm(B[5][:, 0:P], chunk(kB[:, pb, :], c), stS[:], start=True, stop=True).then_inc(S["pe_ks"], 1)

                def vv(c):
                    if c == 0:
                        pe.wait_ge(S["d_n"], 7 * b + 7)
                        pe.wait_ge(S["d_v"], b + 1)
                        if inv:
                            pe.wait_ge(S["d_sse"], a_ + 1)
                        else:
                            need(pe, S["mix_done"], b)
                        rhs = chunk(vB[:, pb, :], 0)
                    else:
                        pe.wait_ge(S["d_r"], 3 * b + c)
                        rhs = rR[:]
                    mm(B[5][:, 0:P], chunk(nB[:, pb, :], c), rhs, start=True, stop=True).then_inc(S["pe_v"], 1)

                def oo(c):
                    if c == 0:
                        need(pe, S["d_oz"], b)
                        pe.wait_ge(S["d_at"], b + 1)
                    else:
                        mm(chunk(B[6], c), stS[:], chunk(qdB[:, pb, :], c), start=True, stop=False)
                    pe.wait_ge(S["a_v"], 4 * b + c + 1)
                    m = mm(chunk(B[6], c), vN[:], chunk(atB[:, pb, :], c), start=(c == 0), stop=True)
                    if c < TT - 1:
                        mm(B[5][:, 0:P], chunk(kdB[:, pb, :], c), vN[:], start=True, stop=True).then_inc(S["pe_s"], 1)
                    else:
                        m.then_inc(S["pe_o"], 1)

                def fsum():
                    pe.wait_ge(S["a_o2"], b + 1)
                    for c in range(TT):
                        mm(B[5][:, c:c + 1], chunk(sqW, c), cst[:, C_VEC, 0:1], start=True, stop=False)
                        m = mm(B[5][:, c:c + 1], chunk(q_sqB[:, pb, :], c), cst[:, C_VEC, 1:2], start=False, stop=True)
                    m.then_inc(S["pe_f"], 1)

                def fb():
                    pe.wait_ge(S["d_fr"], b + 1)
                    for c in range(TT):
                        m = mm(chunk(B[5], c), fW[:, 2, c:c + 1].to_broadcast([P, P]), ident, start=True, stop=True)
                    m.then_inc(S["pe_fb"], 1)

                I = lambda f, *x: f(*x) if inv else None
                C = lambda f, *x: f(*x) if chain else None
                I(ss); I(gsum); I(kk); D(1)
                I(kq); I(kt); C(vv, 0); D(1)
                I(mask); C(oo, 0); D(1)
                C(ks, 1); D(2)
                I(vt); C(vv, 1); D(1)
                I(mt, 0); C(oo, 1); D(1)
                I(xm, 1); C(ks, 2); D(1)
                I(nn, 1); C(vv, 2); D(1)
                I(mt, 1); C(oo, 2); D(2)
                I(xm, 2); C(ks, 3); D(1)
                I(nn, 2); C(vv, 3); D(1)
                I(mt, 2); C(oo, 3); D(2)
                I(xm, 3); C(fsum); D(1)
                I(nn, 3); D(2)
                I(mt, 3); C(fb); D(1)
                I(xm, 4); D(2)
                I(nn, 4); D(1)
                I(mt, 4); D(2)
                I(xm, 5); D(2)
                I(nn, 5); D(1)
                I(mt, 5); D(2)
                I(xm, 6); D(1)
                I(nn, 6); D(32)

            gdn_iter(1, 0, None, 1, "head", True, False)
            gdn_iter(2, 1, 0, 0, "head", True, True)
            gdn_iter(3, 2, 1, 1, "head", True, True)
            with pe.Fori(2, HG // 2) as i:
                gdn_iter(2 * i, 2 * i - 1, 2 * i - 2, 0, "head", True, True)
                gdn_iter(2 * i + 1, 2 * i, 2 * i - 1, 1, "head", True, True)
            gdn_iter(None, HG - 1, HG - 2, 0, "bc", True, True)
            gdn_iter(None, None, HG - 1, 1, "xz", False, True)

            def ssd_iter(j, i, par, dense, ssd_):
                pi = 1 - par
                steps = iter(range(16))

                def D(n):
                    if not dense:
                        return
                    for _ in range(n):
                        x = next(steps)
                        u, k = x // 8, x % 8
                        if k == 0 and u == 0:
                            pe.wait_ge(S["ds_tap"], 3 * (3 + j))
                        elif k == 0:
                            pe.wait_ge(S["zs_done"], j)
                        dense_k(S_XZ + 2 * j + u, (2 * par + u), B[u], k)

                def gsum(hh):
                    bank = B[7] if hh == 0 else B[2]
                    if hh == 0:
                        pe.wait_ge(S["ds_cols"], i + 1)
                    need(pe, S["as_dt"], 2 * i - 1 + hh)
                    for c in range(TT):
                        m = mm(chunk(bank, c), colS[:, hh, G_G, c:c + 1].to_broadcast([P, P]), tri,
                               start=(c == 0), stop=False, skip_group_check=True)
                    m.then_inc(S["ps_g"], 1)

                def mask(hh):
                    bank = B[7] if hh == 0 else B[2]
                    pe.wait_ge(S["as_eg"], 2 * i + 1 + hh)
                    mm(bank[:], negm[:, 0, :], negm[:, 1:, :].rearrange("p c t -> p (c t)"), start=False,
                       stop=True, skip_group_check=True).then_inc(S["ps_m"], 1)

                def xt():
                    pe.wait_ge(S["as_silu"], i + 5)
                    need(pe, S["ds_xdt"], i)
                    for c in range(TT):
                        m = nc.tensor.transpose(chunk(B[3], c), chunk(xA[:, pi, :], c), ident)
                    m.then_inc(S["ps_x"], 1)

                def st():
                    pe.wait_ge(S["ds_xdd"], i + 1)
                    pe.wait_ge(S["ds_bcur"], i + 1)
                    need(pe, S["ds_h"], 3 * i)
                    for c in range(TT - 1):
                        m = mm(chunk(B[4], c), chunk(b_cur, c), chunk(xdd, c), start=True, stop=True)
                    m.then_inc(S["ps_st"], 1)

                def yy():
                    pe.wait_ge(S["ds_sc"], 2 * i + 2)
                    pe.wait_ge(S["ds_cd"], 2 * i + 2)
                    pe.wait_ge(S["ds_h"], 3 * i + 3)
                    need(pe, S["ds_y1"], i)
                    for c in range(TT):
                        for hh in range(2):
                            o = B[6][hh * HP:(hh + 1) * HP, c * P:(c + 1) * P]
                            hs = slice(c * P + hh * HP, c * P + (hh + 1) * HP)
                            m = mm(o, xdt[:, hs], chunk(scS[:, hh, :], c), start=True, stop=(c == 0))
                            if c:
                                m = mm(o, hst[:, c - 1, hh * HP:(hh + 1) * HP], chunk(cdS[:, hh, :], c),
                                       start=False, stop=True)
                    m.then_inc(S["ps_y"], 1)

                def out_part(j):
                    if not dense:
                        row_part(S_OUT, 0, 0, j, 0, j == 0)

                gsum(0); xt(); D(2)
                out_part(0)
                gsum(1); D(2)
                mask(0); D(2)
                out_part(1)
                mask(1); D(2)
                if not (isinstance(i, int) and i == 0):
                    square_sums(i - 1)
                out_part(2)
                st(); D(6)
                out_part(3)
                yy(); D(2)

            def square_sums(i):
                pe.wait_ge(S["as_sq"], i + 1)
                need(pe, S["ds_sq"], i)
                for c in range(TT):
                    m = mm(B[5][:, c:c + 1], chunk(y_sq, c), ones[:, 0:1], start=True, stop=True)
                m.then_inc(S["ps_sq"], 1)

            pe.wait_ge(S["as_silu"], 4)
            for g in range(GROUPS):
                for c in range(TT):
                    m = nc.tensor.transpose(chunk(B[2 + g], c), chunk(bcA[:, g, :], c), ident)
                m.then_inc(S["pb_tr"], 1)
            pe.wait_ge(S["mix_done"], HG)
            for g in range(GROUPS):
                for c in range(TT):
                    m = mm(chunk(B[4 + g], c), chunk(bcA[:, g, :], c), chunk(bcA[:, 2 + g, :], c), start=True, stop=True)
                m.then_inc(S["pb_cb"], 1)
            pe.wait_ge(S["ab_tok"], GROUPS)
            pe.wait_ge(S["db_cb"], GROUPS)
            ssd_iter(1, 0, 1, True, True)
            with pe.Fori(1, XT // 2) as q:
                ssd_iter(2 * q, 2 * q - 1, 0, True, True)
                ssd_iter(2 * q + 1, 2 * q, 1, True, True)
            pe.wait_ge(S["zs_done"], XT)
            pe.wait_ge(S["ds_tap"], 3 * (4 + XT))
            ssd_iter(None, XT - 1, 0, False, True)

            pe.wait_ge(S["as_dt"], 2 * XT)
            pe.wait_ge(S["ds_xdt"], XT)
            for j in range(4):
                row_part(S_OUT, 0, 0, j, 1, j == 0)
            square_sums(XT - 1)
            pe.wait_ge(S["ds_h"], 3 * XT)
            pe.wait_ge(S["ds_sq"], XT)
            pe.wait_ge(S["ds_y1"], XT)
            for j in range(4):
                for t in (2, 3):
                    row_part(S_OUT, 0, 0, j, t, j == 0)
            for i in (1, 2):
                for j in range(4):
                    for t in range(TT):
                        if i == 2 and j == 0:
                            pe.wait_ge(S["x_add"], 2 * t + 2)
                        row_part(S_OUT, 0, i, j, t, i == 2 and j == 0, j == 3)
            row_last(S_OUT, 0, 3, True, N2)

            def wk(n):
                if n < 2:
                    pe.wait_ge(S["n_lo"], 2 * (TT + MT + 1))
                else:
                    pe.wait_ge(S["km_ok"], n - 1)
                for k in range(KT):
                    dense_k(S_WK + n, n % 4, B[n % 2], k, m_hi, m_lo, M)

            wk(0)
            wk(1)
            norm_tile(N2, TT - 1)
            for n in range(2, KT):
                wk(n)
            pe.wait_ge(S["n_lo"], 2 * (2 * TT + MT))
            for k in range(KT):
                pe.wait_ge(S["slab_ready"], S_WV + k + 1)
                for t in range(MT):
                    m = row_tile(k % 4, t, chunk(m_hi[:, k, :], t), chunk(m_lo[:, k, :], t), k == 0, k == KT - 1, B[4:])
                m.then_inc(S["slab_used"], 1)

            def wq(n):
                if n < 2:
                    pe.wait_ge(S["km_ok"], KT - 1 + n)
                else:
                    pe.wait_ge(S["qm_ok"], n - 1)
                for k in range(KT):
                    dense_k(S_WQ + n, n % 4, B[n % 2], k)

            def scores(hd):
                pe.wait_ge(S["qm_ok"], 2 * hd + 2)
                need(pe, S["at_exp"], TT * hd)
                for t in range(TT):
                    o = B[2 + t // 2][:, (t % 2) * M:(t % 2 + 1) * M]
                    for u in range(2):
                        m = mm(o, chunk(qmT[:, 2 * hd + u, :], t), kmT[:, 2 * hd + u, :], start=(u == 0), stop=(u == 1))
                    if t % 2:
                        m.then_inc(S["at_s"], 1)

            def probs_tr(hd):
                pe.wait_ge(S["at_pn"], hd + 1)
                if hd:
                    pe.wait_ge(S["at_prt"], MT * hd)
                else:
                    pe.wait_ge(S["vm_ok"], 2 * MT)
                for mt_ in range(MT):
                    for t in range(TT):
                        m = nc.tensor.transpose(chunk(B[4 + mt_], t), pr[:, hd % 2, t, mt_ * P:(mt_ + 1) * P], ident)
                    m.then_inc(S["at_tr"], 1)

            def values(hd):
                pe.wait_ge(S["at_prt"], MT * (hd + 1))
                need(pe, S["at_o"], 2 * hd)
                for u in range(2):
                    for mt_ in range(MT):
                        d0 = hd * HD + u * P
                        m = mm(B[6 + u][:], v_m[:, mt_, d0:d0 + P], prT[:, hd % 2, mt_, :], start=(mt_ == 0), stop=(mt_ == 1))
                    m.then_inc(S["at_pv"], 1)

            wq(0)
            wq(1)
            scores(0)
            for hd in range(AH - 1):
                wq(2 * hd + 2)
                wq(2 * hd + 3)
                probs_tr(hd)
                scores(hd + 1)
                values(hd)
            for j in range(4):
                if j == 0:
                    pe.wait_ge(S["qm_ok"], KT)
                row_part(S_WO, MIX, 0, j, 0, j == 0)
            probs_tr(AH - 1)
            pe.wait_ge(S["at_exp"], TT * AH)
            for j in range(4):
                row_part(S_WO, MIX, 0, j, 1, j == 0)
            values(AH - 1)
            pe.wait_ge(S["at_prt"], MT * AH)
            pe.wait_ge(S["at_o"], 2 * AH)
            for j in range(4):
                for t in (2, 3):
                    row_part(S_WO, MIX, 0, j, t, j == 0)
            row_last(S_WO, MIX, 1, False, N3)
            norm_tile(N3, TT - 1)
            pe.wait_ge(S["n_lo"], 2 * (3 * TT + MT))

            def up(i, j):
                n = 4 * i + j
                need(pe, S["up_relu"], n - 1)
                for k in range(KT):
                    dense_k(S_UP + n, j, B[j % 2], k)

            for j in range(4):
                up(0, j)
            with pe.Fori(1, FT // 4) as i:
                for j in range(4):
                    up(i, j)
            pe.wait_ge(S["up_relu"], FT)

            def down(i, first):
                for j in range(4):
                    for t in range(TT):
                        row_part(S_DOWN, MIX + KT, i, j, t, first and j == 0)

            down(0, True)
            with pe.Fori(1, FT // 4 - 1) as i:
                down(i, False)
            row_last(S_DOWN, MIX + KT, FT // 4 - 1, False, None)

        @block.scalar
        def _(act):
            A = nc.scalar.activation

            def norm_sq(batch, i, src, dump):
                g = batch[1] + i
                for f in range(2):
                    need(act, S["n_sq"], 2 * g + f)
                    A(dump, src[:, f * HALF:(f + 1) * HALF], ACT.Square,
                      accum_out=stat[:, f, g:g + 1]).then_inc(S["n_sq"], 1)

            def norm_root(batch, i):
                g = batch[1] + i
                act.wait_ge(S["n_mean"], g + 1)
                A(stat[:, 4, g:g + 1], stat[:, 3, g:g + 1], ACT.Sqrt).then_inc(S["n_root"], 1)

            def norm_hi(batch, i, dst):
                g = batch[1] + i
                for f in range(2):
                    act.wait_ge(S["n_tr"], 2 * g + f + 1)
                    A(dst[:, 4 * f:4 * f + 4, i * P:(i + 1) * P], B[2 * (i + batch[3]) + f][:].rearrange("p (q t) -> p q t", q=4),
                      ACT.Copy).then_inc(S["n_hi"], 1)

            def tile_hi(s0, i, j, src, scale=None):
                k = 4 * i + j
                if not (isinstance(i, int) and i == 0):
                    w_cut(s0 // 4 + i, j)
                if scale is None:
                    A(a_hi[:, j, :], src(k), ACT.Copy).then_inc(S["cut_hi"], 1)
                else:
                    A(a_hi[:, j, :], src(k), ACT.Copy, scale=scale).then_inc(S["cut_hi"], 1)

            def product_norm(batch, seg, nxt, dst):
                for i in range(TT):
                    g0 = 8 * seg + 2 * i
                    if i == TT - 1:
                        w_cut(nxt // 4, 0)
                        w_cut(nxt // 4, 1)
                    act.wait_ge(S["x_add"], g0 + 2)
                    norm_sq(batch, i, x_res[:, i, :], sq_out[:])
                    if i:
                        norm_hi(batch, i - 1, dst)
                    norm_root(batch, i)
                w_cut(nxt // 4, 2)
                w_cut(nxt // 4, 3)

            def w_cut(i, j):
                if isinstance(i, int) and 4 * i + j >= N_SLABS:
                    return
                act.wait_ge(raw_in[j % RAW_SLOTS], 16 * (2 * i + j // 2 + 1))
                need(act, S["slab_used"], 4 * i + j - SLOTS + 1)
                A(w_hi[:, j, :], raw[:, j % RAW_SLOTS, :], ACT.Copy).then_inc(S["slab_hi"], 1)

            def load_row(w, tiles_before):
                act.wait_ge(S["n_xn"], tiles_before)
                act.dma_start(nrow[:], row(w)).then_inc(S["n_row"], 16)

            act.dma_start(nrow[:], row(a["norm1_w"])).then_inc(S["n_row"], 16)
            act.dma_start(cst[:], a["const"]).then_inc(S["cst_in"], 16)
            for i in range(TT):
                act.wait_ge(x_in[i], 16)
                norm_sq(N1, i, x0[:, i, :], B[7][:])
                norm_root(N1, i)
                if i:
                    norm_hi(N1, i - 1, h_hi)
            w_cut(0, 0)
            act.wait_ge(S["par_in"], PAR_DMAS * 16)
            A(wsm_hi[:], wsm[:], ACT.Copy).then_inc(S["wsm_hi_ok"], 1)
            norm_hi(N1, TT - 1, h_hi)
            w_cut(0, 1)
            load_row(a["mem_norm_w"], TT)
            act.wait_ge(S["mem_in"], 16)
            act.wait_ge(S["n_lo"], 2 * TT)
            for i in range(MT):
                norm_sq(NM, i, mx[:, i, :], B[7][:])
                norm_root(NM, i)
            w_cut(0, 2)
            w_cut(0, 3)

            act.wait_ge(S["gate_raw"], 1)
            A(gt[:, 2], gt[:, 1], ACT.Exp, scale=-1.0)
            A(gt[:, 3, :, 0:HG], gr[:, :, 0:HG], ACT.Exp, scale=-1.0)
            A(arow[:], arow[:], ACT.Exp).then_inc(S["gate_act"], 1)

            def gate_exp():
                act.wait_ge(S["gate_raw"], 2)
                A(gt[:, 1], gt[:, 0], ACT.Exp)
                A(gt[:, 2], gt[:, 8], ACT.Exp)
                A(gt[:, 3], gt[:, 9], ACT.Exp).then_inc(S["gate_act"], 1)

            def gdn_iter(h, a_, b, par, dense, inv, chain):
                pa, pb = 1 - par, par

                def eg_():
                    act.wait_ge(S["pe_g"], a_ + 1)
                    need(act, S["d_qd"], a_)
                    A(eg[:], B[7][:], ACT.Exp).then_inc(S["a_eg"], 1)

                def dt():
                    act.wait_ge(S["pe_gm"], a_ + 1)
                    act.wait_ge(S["d_cols"], a_ + 1)
                    need(act, S["d_u"], a_)
                    need(act, S["d_at"], a_)
                    for c in range(TT):
                        m = A(chunk(dt_, c), chunk(B[7], c), ACT.Exp, bias=colB[:, pa, G_NEG, c:c + 1])
                    m.then_inc(S["a_dt"], 1)

                def q2():
                    act.wait_ge(S["a_silu"], 3 * a_ + 1)
                    need(act, S["pe_f"], a_ - 1)
                    A(q_sqB[:, pa, :], qA[:], ACT.Square).then_inc(S["a_q2"], 1)

                def rinv():
                    act.wait_ge(S["d_sse"], a_ + 1)
                    need(act, S["d_v"], a_)
                    A(ssA[:, 1, :], ssA[:, 0, :], ACT.Sqrt).then_inc(S["a_rinv"], 1)

                def v(c):
                    act.wait_ge(S["pe_v"], 4 * b + c + 1)
                    A(vN[:], B[5][:, 0:P], ACT.Copy, scale=br2B[:, pb, 0, c:c + 1]).then_inc(S["a_v"], 1)

                def m_(l):
                    act.wait_ge(S["pe_mt"], 6 * a_ + l + 1)
                    A(mW[:], B[4][:], ACT.Copy).then_inc(S["a_m"], 1)

                def x_(l):
                    act.wait_ge(S["pe_x"], 6 * a_ + l)
                    A(xW[:], B[2][:], ACT.Copy).then_inc(S["a_x"], 1)

                def o2():
                    act.wait_ge(S["pe_o"], b + 1)
                    A(sqW[:], B[6][:], ACT.Square).then_inc(S["a_o2"], 1)

                def rf():
                    act.wait_ge(S["d_fe"], b + 1)
                    A(fW[:, 1, :], fW[:, 0, :], ACT.Sqrt).then_inc(S["a_rf"], 1)

                def tap(t):
                    act.wait_ge(S["slab_used"], 4 * h + t + 1)
                    act.wait_ge(S["d_cw"], h + 1)
                    need(act, S["a_silu"], 3 * h + t - 1)
                    A(cacc[:, t % 2, :], B[t % 2][:], ACT.Copy, scale=cwB[:, par, 9 + t:10 + t]).then_inc(S["a_tap"], 1)

                def silu(t):
                    act.wait_ge(S["d_tap"], 9 * h + 3 * t + 3)
                    if inv:
                        act.wait_ge(S[("pe_kq", "pe_kt", "pe_vt")[t]], a_ + 1)
                        if t < 2:
                            act.wait_ge(S[("d_qd", "d_kb")[t]], a_ + 1)
                        if t == 0:
                            act.wait_ge(S["a_q2"], a_ + 1)
                    A((qA, kA, vA)[t][:], cacc[:, t % 2, :], ACT.Silu).then_inc(S["a_silu"], 1)

                def k2():
                    act.wait_ge(S["a_silu"], 3 * h + 2)
                    if chain:
                        act.wait_ge(S["pe_f"], b + 1)
                    if inv:
                        act.wait_ge(S["pe_ss"], a_ + 1)
                    A(sqW[:], kA[:], ACT.Square).then_inc(S["a_k2"], 1)

                def z():
                    act.wait_ge(S["slab_used"], 4 * h + 4)
                    A(mix[:, bass.ds(h, 1), :].rearrange("p o t -> p (o t)"), B[1][:], ACT.Silu).then_inc(S["z_done"], 1)

                I = lambda f, *x: f(*x) if inv else None
                C = lambda f, *x: f(*x) if chain else None
                H = lambda f, *x: f(*x) if dense == "head" else None

                def tap_(t):
                    if dense == "head":
                        tap(t)
                    elif dense == "bc":
                        conv_tap(t)

                def silu_(t):
                    if dense == "head":
                        silu(t)
                    elif dense == "bc":
                        bc_silu(t)

                def W(j):
                    if dense == "head":
                        w_cut(S_GDN // 4 + h + 1, j)
                    elif dense == "bc":
                        w_cut(S_XZ // 4, j)

                I(eg_); C(v, 0); I(dt); I(q2); I(rinv)
                C(v, 1); I(m_, 0)
                I(x_, 1); C(v, 2); tap_(0); I(m_, 1); W(0)
                if not inv and not chain:
                    for i in range(MT):
                        norm_hi(NM, i, m_hi)
                I(x_, 2); C(v, 3); I(m_, 2); C(o2)
                I(x_, 3); C(rf); tap_(1); I(m_, 3); W(1)
                silu_(0)
                I(x_, 4); silu_(1); H(k2); I(m_, 4)
                I(x_, 5); tap_(2); I(m_, 5); W(2)
                I(x_, 6); silu_(2); H(z)
                if not inv and not chain:
                    gate_exp()
                if dense == "bc":
                    tap_(3)
                    silu_(3)
                W(3)

            def conv_tap(n):
                act.wait_ge(S["slab_used"], S_BC + n + 1)
                need(act, S["as_silu"], n - 1)
                A(cacc[:, n % 2, :], B[n % 2][:], ACT.Copy, scale=cw_s[:, 3 * 12 + 8 + n:3 * 12 + 9 + n]).then_inc(S["as_tap"], 1)

            def bc_silu(n):
                act.wait_ge(S["ds_tap"], 3 * n + 3)
                A(bcA[:, n, :], cacc[:, n % 2, :], ACT.Silu, bias=vec[:, V_CB + 8 + n:V_CB + 9 + n]).then_inc(S["as_silu"], 1)

            gdn_iter(0, None, None, 0, "head", False, False)
            gdn_iter(1, 0, None, 1, "head", True, False)
            gdn_iter(2, 1, 0, 0, "head", True, True)
            gdn_iter(3, 2, 1, 1, "head", True, True)
            with act.Fori(2, HG // 2) as i:
                gdn_iter(2 * i, 2 * i - 1, 2 * i - 2, 0, "head", True, True)
                gdn_iter(2 * i + 1, 2 * i, 2 * i - 1, 1, "head", True, True)
            gdn_iter(None, HG - 1, HG - 2, 0, "bc", True, True)
            gdn_iter(None, None, HG - 1, 1, "xz", False, True)

            act.wait_ge(S["mix_done"], HG)
            def out_hi(i, j):
                k = 4 * i + j
                tile_hi(S_OUT, i, j, lambda k: mix[:, k, :], None if k < HG else vec[:, V_NW + k - HG:V_NW + k - HG + 1])

            def ssd_iter(j, i, par, dense, ssd_, ring=None):
                def eg_(hh):
                    act.wait_ge(S["ps_g"], 2 * i + hh + 1)
                    need(act, S["ds_cd"], 2 * i)
                    A(egS[:, hh, :], (B[7], B[2])[hh][:], ACT.Exp).then_inc(S["as_eg"], 1)

                def dt(hh):
                    act.wait_ge(S["ps_m"], 2 * i + hh + 1)
                    act.wait_ge(S["ds_cols"], i + 1)
                    need(act, S["ds_sc"], 2 * i)
                    for c in range(TT):
                        m = A(chunk(dtS[:, hh, :], c), chunk((B[7], B[2])[hh], c), ACT.Exp, bias=colS[:, hh, G_NEG, c:c + 1])
                    m.then_inc(S["as_dt"], 1)

                def x():
                    act.wait_ge(S["slab_used"], S_XZ + 2 * j + 1)
                    act.wait_ge(S["ds_cw"], j + 1)
                    act.wait_ge(S["as_silu"], 3 + j)
                    A(cacc[:, par, :], B[0][:], ACT.Copy, scale=cwS[:, par, 3:4]).then_inc(S["as_tap"], 1)

                def silu():
                    act.wait_ge(S["ds_tap"], 3 * (4 + j) + 3)
                    need(act, S["ps_x"], j - 1)
                    need(act, S["ds_y1"], j - 1)
                    A(xA[:, par, :], cacc[:, par, :], ACT.Silu, bias=cwS[:, par, 4:5]).then_inc(S["as_silu"], 1)

                def z():
                    act.wait_ge(S["slab_used"], S_XZ + 2 * j + 2)
                    A(mix[:, bass.ds(HG + j, 1), :].rearrange("p o t -> p (o t)"), B[1][:], ACT.Silu).then_inc(S["zs_done"], 1)

                def square(k):
                    act.wait_ge(S["ds_mix"], k + 1)
                    need(act, S["ps_sq"], k)
                    A(y_sq, mix[:, bass.ds(HG + k, 1), :].rearrange("p o t -> p (o t)"), ACT.Square).then_inc(S["as_sq"], 1)

                if ssd_ and dense:
                    eg_(0); eg_(1); dt(0); dt(1)
                    if not (isinstance(i, int) and i == 0):
                        square(i - 1)
                elif ssd_:
                    out_hi(0, 0); eg_(0); out_hi(0, 1); eg_(1); out_hi(0, 2); dt(0); dt(1); out_hi(0, 3)
                    square(i - 1)
                    square(i)
                if dense:
                    x(); w_cut(ring + 1, 2 * par); silu(); z(); w_cut(ring + 1, 2 * par + 1)

            ssd_iter(0, None, 0, True, False, S_XZ // 4)
            for g in range(GROUPS):
                act.wait_ge(S["pb_tr"], g + 1)
                A(b_tok[:, g, :], B[2 + g][:], ACT.Copy).then_inc(S["ab_tok"], 1)
            ssd_iter(1, 0, 1, True, True, S_XZ // 4)
            with act.Fori(1, XT // 2) as q:
                ssd_iter(2 * q, 2 * q - 1, 0, True, True, S_XZ // 4 + q)
                ssd_iter(2 * q + 1, 2 * q, 1, True, True, S_XZ // 4 + q)
            ssd_iter(None, XT - 1, 0, False, True)
            act.wait_ge(S["gn_mean"], 1)
            A(gnS[:, 2], gnS[:, 1], ACT.Sqrt).then_inc(S["gn_root"], 1)
            act.wait_ge(S["ds_mix"], XT)
            for i in range(1, MIX // 4):
                for j in range(4):
                    out_hi(i, j)
            load_row(a["norm2_w"], TT + MT)

            product_norm(N2, 2, S_WK, h_hi)

            def km(n):
                act.wait_ge(S["slab_used"], S_WK + n + 1)
                A(kmT[:, n, :], B[n % 2][:, 0:M], ACT.Copy).then_inc(S["km_ok"], 1)
                w_cut(S_WK // 4 + 1 + n // 4, n % 4)

            km(0)
            km(1)
            norm_hi(N2, TT - 1, h_hi)
            for n in range(2, KT):
                km(n)
            load_row(a["norm3_w"], 2 * TT + MT)
            for k in range(KT):
                w_cut(S_WV // 4 + 1 + k // 4, k % 4)
            act.wait_ge(S["slab_used"], S_WV + KT)
            for q, bank in enumerate(B[4:]):
                A(v_m[:, q // 2, (q % 2) * HALF:(q % 2 + 1) * HALF], bank[:], ACT.Copy).then_inc(S["vm_ok"], 1)

            def qm(n):
                act.wait_ge(S["slab_used"], S_WQ + n + 1)
                A(qmT[:, n, :], B[n % 2][:], ACT.Copy).then_inc(S["qm_ok"], 1)
                w_cut(S_WQ // 4 + 1 + n // 4, n % 4)

            qm(0)
            qm(1)
            for hd in range(AH):
                act.wait_ge(S["at_neg"], hd + 1)
                need(act, S["at_tr"], MT * (hd - 1))
                need(act, S["at_rec"], hd - 1)
                for t in range(TT):
                    A(pr[:, hd % 2, t, :], B[2 + t // 2][:, (t % 2) * M:(t % 2 + 1) * M], ACT.Exp,
                      bias=sm[:, hd % 2, 1, t:t + 1], scale=float(HD) ** -0.5,
                      accum_out=sm[:, hd % 2, 2, t:t + 1]).then_inc(S["at_exp"], 1)
                if hd + 1 < AH:
                    qm(2 * hd + 2)
                    qm(2 * hd + 3)
                if hd == 2:
                    act.wait_ge(S["at_o"], 4)
                    for j in range(4):
                        tile_hi(S_WO, 0, j, lambda k: oT[:, k, :])
                for u in range(2):
                    act.wait_ge(S["at_pv"], 2 * hd + u + 1)
                    A(oT[:, 2 * hd + u, :], B[6 + u][:], ACT.Copy).then_inc(S["at_o"], 1)

            act.wait_ge(S["at_o"], 2 * AH)
            for j in range(4):
                tile_hi(S_WO, 1, j, lambda k: oT[:, k, :])
            product_norm(N3, 3, S_UP, h_hi)
            norm_hi(N3, TT - 1, h_hi)
            load_row(a["final_norm_w"], 3 * TT + MT)

            def relu(i, j):
                n = 4 * i + j
                act.wait_ge(S["slab_used"], S_UP + n + 1)
                need(act, S["up_sq"], n - 1)
                A(ur[:, j % 2, :], B[j % 2][:], ACT.Relu).then_inc(S["up_relu"], 1)
                w_cut(S_UP // 4 + i + 1, j)

            for j in range(4):
                relu(0, j)
            with act.Fori(1, FT // 4 - 1) as i:
                for j in range(4):
                    relu(i, j)
            act.wait_ge(S["up_sq"], 4)
            for j in range(4):
                relu(FT // 4 - 1, j)
                tile_hi(S_DOWN, 0, j, lambda k: uT[:, k, :])
            act.wait_ge(S["up_sq"], FT)
            with act.Fori(1, FT // 4) as i:
                for j in range(4):
                    tile_hi(S_DOWN, i, j, lambda k: uT[:, bass.ds(k, 1), :].rearrange("p o t -> p (o t)"))
            for i in range(TT):
                act.wait_ge(S["x_add"], 8 * 4 + 2 * i + 2)
                norm_sq(NF, i, x_res[:, i, :], sq_out[:])
                norm_root(NF, i)

        @block.vector
        def _(dve):
            V = nc.vector
            TTn = V.tensor_tensor

            def norm_stat(batch, i):
                g = batch[1] + i
                st = lambda r: stat[:, r, g:g + 1]
                dve.wait_ge(S["n_sq"], 2 * g + 2)
                TTn(st(2), st(0), st(1), ALU.add).then_inc(S["n_add"], 1)
                dve.wait_ge(S["n_add"], g + 1)
                V.tensor_scalar(st(3), st(2), 1.0 / D, EPS, ALU.mult, ALU.add).then_inc(S["n_mean"], 1)
                dve.wait_ge(S["n_root"], g + 1)
                V.reciprocal(st(5), st(4)).then_inc(S["n_rstd"], 1)

            def norm_xn(batch, i, src, out_=None, done="n_xn"):
                g = batch[1] + i
                if batch is not NM:
                    norm_stat(batch, i)
                dve.wait_ge(S["n_rstd"], g + 1)
                dve.wait_ge(S["n_row"], 16 * (batch[0] + 1))
                if done == "n_xn":
                    need(dve, S["n_tr"], 2 * g)
                V.scalar_tensor_tensor(out=xn[:] if out_ is None else out_, in0=src, scalar=stat[:, 5, g:g + 1], in1=nrow[:],
                                       op0=ALU.mult, op1=ALU.mult).then_inc(S[done], 1)

            def norm_lo(batch, i, d_hi, d_lo):
                g = batch[1] + i
                for f in range(2):
                    dve.wait_ge(S["n_hi"], 2 * g + f + 1)
                    fs, ts = slice(4 * f, 4 * f + 4), slice(i * P, (i + 1) * P)
                    TTn(d_lo[:, fs, ts], B[2 * (i + batch[3]) + f][:].rearrange("p (q t) -> p q t", q=4),
                        d_hi[:, fs, ts].bitcast(F32), ALU.subtract).then_inc(S["n_lo"], 1)

            def tile_lo(c0, i, j, src, scale=None):
                k = 4 * i + j
                dve.wait_ge(S["cut_hi"], c0 + k + 1)
                hi = a_hi[:, j, :].bitcast(F32)
                if scale is None:
                    TTn(a_lo[:, j, :], src(k), hi, ALU.subtract).then_inc(S["cut_lo"], 1)
                else:
                    V.scalar_tensor_tensor(out=a_lo[:, j, :], in0=src(k), scalar=scale, in1=hi,
                                           op0=ALU.mult, op1=ALU.subtract).then_inc(S["cut_lo"], 1)

            def add_residual(seg, s_end, t, scale=None):
                if t < TT - 1:
                    dve.wait_ge(S["row_done"], (TT - 1) * seg + t + 1)
                else:
                    dve.wait_ge(S["slab_used"], s_end)
                for f in range(2):
                    x = x_res[:, t, f * HALF:(f + 1) * HALF]
                    need(dve, S["x_add"], 8 * (seg - 1) + 2 * t + f + 1)
                    if scale is None:
                        TTn(x, x, B[2 * t + f][:], ALU.add).then_inc(S["x_add"], 1)
                    else:
                        V.scalar_tensor_tensor(out=x, in0=B[2 * t + f][:], scalar=scale, in1=x,
                                               op0=ALU.mult, op1=ALU.add).then_inc(S["x_add"], 1)

            def product_norm(batch, seg, s_end, scale=lambda t: None):
                for i in range(TT):
                    add_residual(seg, s_end, i, scale(i))
                    if i:
                        norm_lo(batch, i - 1, h_hi, h_lo)
                    norm_xn(batch, i, x_res[:, i, :])
                norm_lo(batch, TT - 1, h_hi, h_lo)

            for i in range(TT):
                norm_xn(N1, i, x0[:, i, :])
                if i:
                    norm_lo(N1, i - 1, h_hi, h_lo)
            dve.wait_ge(S["wsm_hi_ok"], 1)
            TTn(wsm_lo[:], wsm[:], wsm_hi[:].bitcast(F32), ALU.subtract).then_inc(S["wsm_lo_ok"], 1)
            norm_lo(N1, TT - 1, h_hi, h_lo)
            dve.wait_ge(S["rows_tr"], 1)
            V.tensor_copy(cw_g[:], B[2][:, 0:96])
            V.tensor_copy(cw_s[:], B[2][:, 96:144])
            V.tensor_copy(vec[:], B[2][:, 144:144 + VROWS]).then_inc(S["rows_cp"], 1)
            for i in range(MT):
                norm_stat(NM, i)
            norm_xn(NM, 0, mx[:, 0, :])

            step = [0]

            def link(ins):
                step[0] += 1
                ins.then_inc(S["gate_dve"], 1)
                dve.wait_ge(S["gate_dve"], step[0])

            def heads(ap):
                return ap.unsqueeze(1).to_broadcast([P, TT, HEADS])

            def kind(k, lo=0, hi=HEADS):
                return gates[:, lo:hi, k, :].rearrange("p h c -> p c h")

            dve.wait_ge(S["gate_mm"], 1)
            V.tensor_copy(graw[:], B[6][0:32, :]).then_inc(S["gate_cp"], 1)
            dve.wait_ge(S["gate_mm"], 2)
            link(V.tensor_copy(gr[:], B[7][:, 0:TT * 32].rearrange("p (c n) -> p c n", c=TT)))
            link(TTn(gt[:, 0], gr[:, :, HG:], heads(brow[:]), ALU.add))
            V.scalar_tensor_tensor(out=gt[:, 1], in0=gt[:, 0], scalar=-1.0, in1=gt[:, 0], op0=ALU.mult, op1=ALU.max).then_inc(S["gate_raw"], 1)
            dve.wait_ge(S["gate_act"], 1)
            link(V.tensor_scalar(gt[:, 3, :, 0:HG], gt[:, 3, :, 0:HG], 1.0, None, ALU.add))
            link(V.reciprocal(kind(G_BETA, 0, HG), gt[:, 3, :, 0:HG]))
            link(V.tensor_scalar(gt[:, 4], gt[:, 2], 2.0, None, ALU.add))
            link(V.reciprocal(gt[:, 4], gt[:, 4]))
            link(TTn(gt[:, 4], gt[:, 4], gt[:, 2], ALU.mult))
            link(TTn(gt[:, 5], gt[:, 4], gt[:, 4], ALU.mult))
            link(V.tensor_scalar(gt[:, 6], gt[:, 5], 1.0 / 15, None, ALU.mult))
            for n in (13, 11, 9, 7, 5, 3):
                link(V.scalar_tensor_tensor(out=gt[:, 6], in0=gt[:, 6], scalar=1.0 / n, in1=gt[:, 5], op0=ALU.add, op1=ALU.mult))
            link(V.scalar_tensor_tensor(out=gt[:, 6], in0=gt[:, 6], scalar=1.0, in1=gt[:, 4], op0=ALU.add, op1=ALU.mult))
            link(V.tensor_scalar(gt[:, 6], gt[:, 6], 2.0, None, ALU.mult))
            link(V.scalar_tensor_tensor(out=gt[:, 7], in0=gt[:, 0], scalar=0.0, in1=gt[:, 6], op0=ALU.max, op1=ALU.add))
            V.tensor_copy(kind(G_BETA, HG), gt[:, 7, :, HG:])
            link(V.scalar_tensor_tensor(out=gt[:, 5], in0=gt[:, 7], scalar=-1.0, in1=heads(arow[:]), op0=ALU.mult, op1=ALU.mult))
            V.tensor_copy(kind(G_G), gt[:, 5]).then_inc(S["gate_cs"], 1)
            def gate_tail():
                dve.wait_ge(S["gate_mm"], 3)
                link(V.tensor_copy(gt[:, 8].rearrange("p c h -> p (c h)"), B[7][:, P:P + TT * HEADS]))
                link(V.tensor_copy(gt[:, 9].rearrange("p c h -> p (c h)"), B[7][:, 2 * P:2 * P + TT * HEADS]))
                TTn(gt[:, 0], gt[:, 9], gt[:, 8], ALU.subtract).then_inc(S["gate_raw"], 1)
                dve.wait_ge(S["gate_act"], 2)
                V.tensor_scalar(kind(G_NEG), gt[:, 8], -1.0, None, ALU.mult)
                V.tensor_scalar(kind(G_NEXP), gt[:, 2], -1.0, None, ALU.mult)
                V.tensor_copy(kind(G_DEC), gt[:, 1])
                V.tensor_copy(kind(G_CD), gt[:, 3]).then_inc(S["gates_ok"], 1)
                dve.wait_ge(S["gates_ok"], 1)

            def tap(acc, bank, w, sem_, n0, d):
                if d > 1:
                    dve.wait_ge(sem_, n0 + d - 1)
                V.scalar_tensor_tensor(out=acc[:, d:], in0=bank[:, 0:T - d], scalar=w(TAPS - 1 - d), in1=acc[:, d:],
                                       op0=ALU.mult, op1=ALU.add).then_inc(sem_, 1)

            def gdn_iter(h, a_, b, par, dense, inv, chain):
                pa, pb = 1 - par, par

                def cw():
                    V.tensor_copy(cwB[:, par, :], cw_g[:].rearrange("p (x h) -> p x h", h=HG)[:, :, bass.ds(h, 1)]
                                  .rearrange("p x o -> p (x o)")).then_inc(S["d_cw"], 1)

                def cols():
                    V.tensor_copy(colB[:, pa, :, :].rearrange("p k c -> p (k c)"),
                                  gates[:, bass.ds(a_, 1), :, :].rearrange("p o k c -> p (o k c)")).then_inc(S["d_cols"], 1)

                def ss():
                    dve.wait_ge(S["pe_ss"], a_ + 1)
                    need(dve, S["a_rinv"], a_)
                    V.tensor_scalar(ssA[:, 0, :], B[5][:, 0:TT], EPS, None, ALU.add).then_inc(S["d_sse"], 1)
                    dve.wait_ge(S["d_sse"], a_ + 1)
                    V.reciprocal(ssA[:, 2, :], ssA[:, 0, :]).then_inc(S["d_rec"], 1)
                    dve.wait_ge(S["d_rec"], a_ + 1)
                    dve.wait_ge(S["d_cols"], a_ + 1)
                    need(dve, S["a_v"], 4 * (a_ - 1))
                    TTn(br2B[:, pa, 0, :], ssA[:, 2, :], colB[:, pa, G_BETA, :], ALU.mult).then_inc(S["d_br"], 1)
                    dve.wait_ge(S["d_br"], a_ + 1)
                    V.tensor_scalar(br2B[:, pa, 1, :], br2B[:, pa, 0, :], -1.0, None, ALU.mult).then_inc(S["d_nb"], 1)

                def kb():
                    dve.wait_ge(S["a_silu"], 3 * a_ + 2)
                    need(dve, S["pe_o"], a_ - 1)
                    V.tensor_copy(kB[:, pa, :], kA[:]).then_inc(S["d_kb"], 1)

                def qd():
                    dve.wait_ge(S["a_eg"], a_ + 1)
                    TTn(qdB[:, pa, :], qA[:], eg[:], ALU.mult).then_inc(S["d_qd"], 1)

                def kd():
                    dve.wait_ge(S["pe_kt"], a_ + 1)
                    TTn(kdB[:, pa, :].rearrange("p (c d) -> p c d", c=TT), B[4][:].rearrange("p (c d) -> p c d", c=TT),
                        bcast(colB[:, pa, G_DEC, :], P), ALU.mult).then_inc(S["d_kd"], 1)

                def u():
                    dve.wait_ge(S["pe_kk"], a_ + 1)
                    dve.wait_ge(S["a_dt"], a_ + 1)
                    dve.wait_ge(S["d_nb"], a_ + 1)
                    for c in range(TT):
                        m = V.scalar_tensor_tensor(out=chunk(u_neg, c), in0=chunk(B[2], c), scalar=br2B[:, pa, 1, c:c + 1],
                                                   in1=chunk(dt_, c), op0=ALU.mult, op1=ALU.mult)
                    m.then_inc(S["d_u"], 1)

                def off(l):
                    dve.wait_ge(S["d_u"], a_ + 1)
                    need(dve, S["pe_x"], 6 * a_ + max(l - 2, 0))
                    TTn(u_off[:, l % 2, :].rearrange("p (c t) -> p c t", c=TT), u_neg[:].rearrange("p (c t) -> p c t", c=TT),
                        cst[:, C_MASK + l, :].unsqueeze(1).to_broadcast([P, TT, P]), ALU.mult).then_inc(S["d_off"], 1)

                def n1():
                    dve.wait_ge(S["d_off"], 7 * a_ + 1)
                    need(dve, S["pe_n"], 6 * a_)
                    TTn(nW[:].rearrange("p (c t) -> p c t", c=TT), u_off[:, 0, :].rearrange("p (c t) -> p c t", c=TT),
                        ident.unsqueeze(1).to_broadcast([P, TT, P]), ALU.add).then_inc(S["d_n"], 1)

                def at():
                    dve.wait_ge(S["pe_kq"], a_ + 1)
                    TTn(atB[:, pa, :], B[3][:], dt_[:], ALU.mult).then_inc(S["d_at"], 1)

                def vb():
                    dve.wait_ge(S["pe_vt"], a_ + 1)
                    dve.wait_ge(S["a_rinv"], a_ + 1)
                    TTn(vB[:, pa, :].rearrange("p (c d) -> p c d", c=TT), B[7][:].rearrange("p (c d) -> p c d", c=TT),
                        bcast(ssA[:, 1, :], P), ALU.mult).then_inc(S["d_v"], 1)

                def nn(l):
                    dve.wait_ge(S["pe_n"], 6 * a_ + l)
                    dve.wait_ge(S["d_n"], 7 * a_ + l)
                    dst = nB[:, pa, :] if l == LEVELS - 1 else nW[:]
                    TTn(dst, nW[:], B[3][:], ALU.add).then_inc(S["d_n"], 1)

                def r(c):
                    dve.wait_ge(S["pe_ks"], 3 * b + c)
                    V.scalar_tensor_tensor(out=rR[:], in0=B[5][:, 0:P], scalar=colB[:, pb, G_NEXP, c:c + 1],
                                           in1=chunk(vB[:, pb, :], c), op0=ALU.mult, op1=ALU.add).then_inc(S["d_r"], 1)

                def s(c):
                    dve.wait_ge(S["pe_s"], 3 * b + c + 1)
                    if c == 0:
                        V.tensor_copy(stS[:], B[5][:, 0:P]).then_inc(S["d_s"], 1)
                    else:
                        dve.wait_ge(S["d_s"], 3 * b + c)
                        V.scalar_tensor_tensor(out=stS[:], in0=stS[:], scalar=colB[:, pb, G_CD, c:c + 1], in1=B[5][:, 0:P],
                                               op0=ALU.mult, op1=ALU.add).then_inc(S["d_s"], 1)

                def mixb():
                    return mix[:, bass.ds(b, 1), :].rearrange("p o t -> p (o t)")

                def oz_():
                    dve.wait_ge(S["a_o2"], b + 1)
                    dve.wait_ge(S["z_done"], b + 1)
                    need(dve, S["mix_done"], b)
                    V.scalar_tensor_tensor(out=oz[:], in0=B[6][:], scalar=vec[:, V_GN:V_GN + 1], in1=mixb(),
                                           op0=ALU.mult, op1=ALU.mult).then_inc(S["d_oz"], 1)

                def fe():
                    dve.wait_ge(S["pe_f"], b + 1)
                    V.tensor_scalar(fW[:, 0, :], B[5][:, 0:TT], EPS * EPS * P, None, ALU.add).then_inc(S["d_fe"], 1)

                def fr():
                    dve.wait_ge(S["a_rf"], b + 1)
                    V.reciprocal(fW[:, 2, :], fW[:, 1, :]).then_inc(S["d_fr"], 1)

                def mx_():
                    dve.wait_ge(S["pe_fb"], b + 1)
                    dve.wait_ge(S["d_oz"], b + 1)
                    TTn(mixb(), oz[:], B[5][:], ALU.mult).then_inc(S["mix_done"], 1)

                def conv(t, d):
                    if dense == "head":
                        if d == 1:
                            dve.wait_ge(S["a_tap"], 3 * h + t + 1)
                        tap(cacc[:, t % 2, :], B[t % 2], lambda x: cwB[:, par, 3 * x + t:3 * x + t + 1], S["d_tap"], 9 * h + 3 * t, d)
                    elif dense == "bc":
                        if d == 1:
                            dve.wait_ge(S["as_tap"], t + 1)
                        tap(cacc[:, t % 2, :], B[t % 2], lambda x: cw_s[:, 12 * x + 8 + t:12 * x + 9 + t], S["ds_tap"], 3 * t, d)

                I = lambda f, *x: f(*x) if inv else None
                C = lambda f, *x: f(*x) if chain else None
                H = lambda f, *x: f(*x) if dense == "head" else None
                I(cols); H(cw); I(ss); I(kb); I(qd); I(kd)
                C(s, 0); C(r, 1)
                I(u); I(off, 0); I(n1); I(at); I(off, 1)
                C(s, 1); I(vb); C(r, 2)
                I(nn, 1); C(s, 2); I(off, 2); C(r, 3)
                conv(0, 1); I(nn, 2); conv(0, 2); I(off, 3); conv(0, 3)
                if not inv and not chain:
                    norm_xn(NM, 1, mx[:, 1, :])
                    for i in range(MT):
                        norm_lo(NM, i, m_hi, m_lo)
                C(oz_); C(fe); C(fr); I(nn, 3); I(off, 4)
                conv(1, 1); C(mx_); conv(1, 2); I(nn, 4); conv(1, 3); I(off, 5)
                I(nn, 5); conv(2, 1); I(off, 6); conv(2, 2); conv(2, 3)
                I(nn, 6)
                if dense == "bc":
                    for d in range(1, TAPS):
                        conv(3, d)

            gdn_iter(0, None, None, 0, "head", False, False)
            gate_tail()
            gdn_iter(1, 0, None, 1, "head", True, False)
            gdn_iter(2, 1, 0, 0, "head", True, True)
            gdn_iter(3, 2, 1, 1, "head", True, True)
            with dve.Fori(2, HG // 2) as i:
                gdn_iter(2 * i, 2 * i - 1, 2 * i - 2, 0, "head", True, True)
                gdn_iter(2 * i + 1, 2 * i, 2 * i - 1, 1, "head", True, True)
            gdn_iter(None, HG - 1, HG - 2, 0, "bc", True, True)
            gdn_iter(None, None, HG - 1, 1, "xz", False, True)

            def out_lo(i, j):
                k = 4 * i + j
                tile_lo(0, i, j, lambda k: mix[:, k, :], None if k < HG else vec[:, V_NW + k - HG:V_NW + k - HG + 1])

            def ssd_iter(j, i, par, dense, ssd_):
                pi = 1 - par

                def v3(ap):
                    return ap.rearrange("p (c u d) -> p c u d", c=TT, u=2)

                def hcol(k):
                    x = colS[:, :, k, :].rearrange("p u c -> p c u")
                    return x.unsqueeze(3).to_broadcast([P, TT, 2, HP])

                if dense:
                    V.tensor_copy(cwS[:, par, 0:TAPS], cw_s[:].rearrange("p (x n) -> p x n", n=12)[:, :, bass.ds(j, 1)]
                                  .rearrange("p x o -> p (x o)"))
                    V.tensor_copy(cwS[:, par, 5:6], dcol[:, bass.ds(j, 1)])
                    V.tensor_copy(cwS[:, par, 4:5], vec[:, bass.ds(V_CB + j, 1)]).then_inc(S["ds_cw"], 1)
                def out_lo_(j):
                    if not dense:
                        out_lo(0, j)

                def square_sum(k):
                    dve.wait_ge(S["ps_sq"], k + 1)
                    V.tensor_copy(ssq[:, bass.ds(k, 1), :].rearrange("p o c -> p (o c)"), B[5][:, 0:TT]).then_inc(S["ds_sq"], 1)

                if ssd_:
                    out_lo_(0)
                    g = i // 4
                    need(dve, S["ps_g"], 2 * i)
                    need(dve, S["as_dt"], 2 * i)
                    V.tensor_copy(colS[:].rearrange("p u k c -> p (u k c)"),
                                  gates[:, bass.ds(HG + 2 * i, 2), :, :].rearrange("p u k c -> p (u k c)")).then_inc(S["ds_cols"], 1)
                    need(dve, S["ps_st"], i)
                    V.tensor_copy(b_cur[:], b_tok[:, bass.ds(g, 1), :].rearrange("p o t -> p (o t)")).then_inc(S["ds_bcur"], 1)
                    dve.wait_ge(S["ps_x"], i + 1)
                    dve.wait_ge(S["ds_cols"], i + 1)
                    need(dve, S["ps_y"], i)
                    TTn(v3(xdt[:]), v3(B[3][:]), hcol(G_BETA), ALU.mult).then_inc(S["ds_xdt"], 1)
                    dve.wait_ge(S["ds_xdt"], i + 1)
                    TTn(v3(xdd[:]), v3(xdt[:]), hcol(G_DEC), ALU.mult).then_inc(S["ds_xdd"], 1)
                    out_lo_(1)
                    for hh in range(2):
                        dve.wait_ge(S["as_eg"], 2 * i + hh + 1)
                        TTn(cdS[:, hh, :], bcA[:, bass.ds(GROUPS + g, 1), :].rearrange("p o t -> p (o t)"), egS[:, hh, :],
                            ALU.mult).then_inc(S["ds_cd"], 1)
                    out_lo_(2)
                    for hh in range(2):
                        dve.wait_ge(S["as_dt"], 2 * i + hh + 1)
                        TTn(scS[:, hh, :], cb[:, bass.ds(g, 1), :].rearrange("p o t -> p (o t)"), dtS[:, hh, :],
                            ALU.mult).then_inc(S["ds_sc"], 1)
                    out_lo_(3)
                    if not (isinstance(i, int) and i == 0):
                        square_sum(i - 1)
                if dense:
                    dve.wait_ge(S["as_tap"], 5 + j)
                    for d in range(1, TAPS):
                        tap(cacc[:, par, :], B[0], lambda x: cwS[:, par, x:x + 1], S["ds_tap"], 3 * (4 + j), d)
                if ssd_:
                    dve.wait_ge(S["ps_st"], i + 1)
                    V.tensor_copy(hst[:, 0, :], B[4][:, 0:P]).then_inc(S["ds_h"], 1)
                    for c in (1, 2):
                        dve.wait_ge(S["ds_h"], 3 * i + c)
                        for hh in range(2):
                            hs = slice(hh * HP, (hh + 1) * HP)
                            m = V.scalar_tensor_tensor(out=hst[:, c, hs], in0=hst[:, c - 1, hs], scalar=colS[:, hh, G_CD, c:c + 1],
                                                       in1=B[4][:, c * P + hh * HP:c * P + (hh + 1) * HP],
                                                       op0=ALU.mult, op1=ALU.add)
                        m.then_inc(S["ds_h"], 1)
                    dve.wait_ge(S["ps_y"], i + 1)
                    V.scalar_tensor_tensor(out=y1, in0=xA[:, pi, :], scalar=cwS[:, pi, 5:6], in1=B[6][:],
                                           op0=ALU.mult, op1=ALU.add).then_inc(S["ds_y1"], 1)
                    dve.wait_ge(S["ds_y1"], i + 1)
                    dve.wait_ge(S["zs_done"], i + 1)
                    mi = mix[:, bass.ds(HG + i, 1), :].rearrange("p o t -> p (o t)")
                    TTn(mi, y1, mi, ALU.mult).then_inc(S["ds_mix"], 1)

            ssd_iter(0, None, 0, True, False)
            for g in range(GROUPS):
                dve.wait_ge(S["pb_cb"], g + 1)
                V.tensor_copy(cb[:, g, :], B[4 + g][:]).then_inc(S["db_cb"], 1)
            dve.wait_ge(S["db_cb"], GROUPS)
            dve.wait_ge(S["ab_tok"], GROUPS)
            ssd_iter(1, 0, 1, True, True)
            with dve.Fori(1, XT // 2) as q:
                ssd_iter(2 * q, 2 * q - 1, 0, True, True)
                ssd_iter(2 * q + 1, 2 * q, 1, True, True)
            ssd_iter(None, XT - 1, 0, False, True)
            dve.wait_ge(S["ps_sq"], XT)
            V.tensor_copy(ssq[:, XT - 1, :], B[5][:, 0:TT]).then_inc(S["ds_sq"], 1)
            dve.wait_ge(S["ds_sq"], XT)
            V.tensor_reduce(gnS[:, 0], ssq[:].rearrange("p (g q) c -> p g c q", g=GROUPS), AX.X, ALU.add).then_inc(S["gn_sum"], 1)
            dve.wait_ge(S["gn_sum"], 1)
            V.tensor_scalar(gnS[:, 1], gnS[:, 0], 1.0 / (4 * P), EPS, ALU.mult, ALU.add).then_inc(S["gn_mean"], 1)
            dve.wait_ge(S["gn_root"], 1)
            V.reciprocal(gnS[:, 3], gnS[:, 2]).then_inc(S["gn_rec"], 1)
            dve.wait_ge(S["gn_rec"], 1)

            for j in range(4):
                out_lo(1, j)
            for j in range(4):
                out_lo(2, j)
                if j == 3:
                    dve.wait_ge(S["xr_in"], 16 * TT)
            for t in range(TT):
                add_residual(0, S_OUT + 8, t)
            for j in range(4):
                out_lo(3, j)
            for t in range(TT):
                add_residual(1, S_OUT + 12, t, gnS[:, 3, 0, t:t + 1])
            product_norm(N2, 2, S_OUT + MIX, lambda t: gnS[:, 3, 1, t:t + 1])

            for hd in range(AH):
                e = hd % 2
                need(dve, S["at_exp"], TT * (hd - 1))
                for u in range(2):
                    dve.wait_ge(S["at_s"], 2 * hd + u + 1)
                    m = V.tensor_reduce(sm[:, e, 0, 2 * u:2 * u + 2], B[2 + u][:].rearrange("p (t m) -> p t m", t=2), AX.X, ALU.max)
                m.then_inc(S["at_max"], 1)
                dve.wait_ge(S["at_max"], hd + 1)
                V.tensor_scalar(sm[:, e, 1, :], sm[:, e, 0, :], -float(HD) ** -0.5, None, ALU.mult).then_inc(S["at_neg"], 1)
                dve.wait_ge(S["at_exp"], TT * (hd + 1))
                V.reciprocal(sm[:, e, 3, :], sm[:, e, 2, :]).then_inc(S["at_rec"], 1)
                dve.wait_ge(S["at_rec"], hd + 1)
                TTn(pr[:, e], pr[:, e], bcast(sm[:, e, 3, :], M), ALU.mult).then_inc(S["at_pn"], 1)
                for mt_ in range(MT):
                    dve.wait_ge(S["at_tr"], MT * hd + mt_ + 1)
                    need(dve, S["at_pv"], 2 * (hd - 1))
                    V.tensor_copy(prT[:, e, mt_, :], B[4 + mt_][:]).then_inc(S["at_prt"], 1)
                if hd == 2:
                    for j in range(4):
                        tile_lo(MIX, 0, j, lambda k: oT[:, k, :])

            for j in range(4):
                tile_lo(MIX, 1, j, lambda k: oT[:, k, :])
            product_norm(N3, 3, S_WO + KT)

            def square(i, j):
                n = 4 * i + j
                dve.wait_ge(S["up_relu"], n + 1)
                TTn(uT[:, bass.ds(n, 1), :].rearrange("p o t -> p (o t)"), ur[:, j % 2, :], ur[:, j % 2, :],
                    ALU.mult).then_inc(S["up_sq"], 1)

            for j in range(4):
                square(0, j)
            with dve.Fori(1, FT // 4 - 1) as i:
                for j in range(4):
                    square(i, j)
            for j in range(4):
                square(FT // 4 - 1, j)
                tile_lo(MIX + KT, 0, j, lambda k: uT[:, k, :])
            with dve.Fori(1, FT // 4) as i:
                for j in range(4):
                    tile_lo(MIX + KT, i, j, lambda k: uT[:, bass.ds(k, 1), :].rearrange("p o t -> p (o t)"))
            for t in range(TT):
                add_residual(4, S_DOWN + FT, t)
                norm_xn(NF, t, x_res[:, t, :], x_res[:, t, :], "fin_y")


PAR_DMAS = 14
N_SLABS = S_END

INPUTS = ["x", "mem", "norm1_w", "w_in", "gdn_conv_w", "gdn_a_log", "gdn_dt_bias", "gdn_norm_w", "ssm_conv_w",
          "ssm_conv_b", "ssm_a_log", "ssm_dt_bias", "ssm_d", "ssm_norm_w", "w_out", "norm2_w", "mem_norm_w",
          "wq_mem", "wk_mem", "wv_mem", "wo_mem", "norm3_w", "w_up", "w_down", "final_norm_w"]


def kernel(**inputs):
    import ml_dtypes
    import concourse.bacc as bacc
    from concourse.bass_utils import run_bass_kernel_spmd

    nc = bacc.Bacc("TRN2", target_bir_lowering=False, num_devices=1)
    arrays, aps = {}, {}
    host = {n: np.ascontiguousarray(inputs[n]) for n in INPUTS}
    host["const"] = constants()
    host["negm"] = neg_mask().astype(ml_dtypes.bfloat16)
    for name, arr in host.items():
        arrays[f"in_{name}"] = arr
        aps[name] = nc.dram_tensor(f"in_{name}", arr.shape, mybir.dt.from_np(arr.dtype), kind="ExternalInput").ap()
    out = nc.dram_tensor("out_0", (1, T, D), F32, kind="ExternalOutput").ap()
    layer(nc, aps, out)
    r = run_bass_kernel_spmd(nc, [arrays], core_ids=[0])
    return r.results[0]["out_0"]
```

```python
from contextlib import ExitStack

import concourse.bass as bass
import numpy as np
from concourse import mybir

F32 = mybir.dt.float32
F32R = mybir.dt.float32r
BF16 = mybir.dt.bfloat16
ALU = mybir.AluOpType
ACT = mybir.ActivationFunctionType
AX = mybir.AxisListType

P = 128
D = 1024
T = 512
M = 256
KT = D // P
TT = T // P
MT = M // P
HALF = 512
EPS = 1e-6
TAPS = 4
HG = 8
GDN = HG * P
GDN_COLS = 4 * GDN + 2 * HG
HS = 16
HP = 64
XT = D // P
GROUPS = 2
BC = GROUPS * P
HEADS = HG + HS
MIX = (GDN + D) // P
FF = 4 * D
FT = FF // P
AH = 4
HD = D // AH
LEVELS = 7
SLOTS = 4
RAW_SLOTS = 2
SLAB = 1024

S_GDN = 0
S_BC = S_GDN + 4 * HG
S_XZ = S_BC + 4
S_OUT = S_XZ + 2 * XT
S_MEM = S_OUT + MIX
S_WO = S_MEM + 3 * KT
S_UP = S_WO + KT
S_DOWN = S_UP + FT
S_END = S_DOWN + FT

MEM_ORDER = ([("k", 0), ("k", 1), ("k", 2), ("k", 3), ("q", 0), ("k", 4), ("k", 5), ("q", 1), ("k", 6), ("k", 7)]
             + [("v", 0), ("v", 1), ("v", 2), ("q", 2), ("v", 3), ("v", 4), ("v", 5), ("q", 3), ("v", 6), ("v", 7)]
             + [("q", 4), ("q", 5), ("q", 6), ("q", 7)])
MEM_FIRST = 20
MEM_FILL = [[20], [21], [22, 23], []]


def mem_made(pos):
    return sum(w != "v" for w, _ in MEM_ORDER[:pos])


C_ID, C_TRI, C_ONES, C_VEC, C_MASK = 0, 1, 2, 3, 4
NCONST = C_MASK + LEVELS
V_CB, V_NW, V_GN, VROWS = 0, 12, 20, 21
G_NEG, G_NEXP, G_DEC, G_CD, G_BETA, KINDS = 0, 1, 2, 3, 4, 5
NORM_TILES = 4 * TT + MT


def constants():
    c = np.zeros((P, NCONST, P), np.float32)
    s, t = np.arange(P)[:, None], np.arange(P)[None, :]
    c[:, C_ID] = s == t
    c[:, C_TRI] = s <= t
    c[:, C_ONES] = 1.0
    c[:, C_VEC, 0] = 1.0 / P
    for l in range(LEVELS):
        c[:, C_MASK + l] = ((s >> (l + 1)) == (t >> (l + 1))) & ((s >> l) + 1 == (t >> l))
    return c


def neg_mask():
    m = np.zeros((P, 1 + TT, P), np.float32)
    s, t = np.arange(P)[:, None], np.arange(P)[None, :]
    m[:, 0] = s == t
    m[:, 1:] = np.where(s > t, -1e30, 0.0)[:, None, :]
    return m


def need(eng, sem, n):
    if isinstance(n, int) and n <= 0:
        return
    eng.wait_ge(sem, n)


def layer(nc, a, out):
    with ExitStack() as ctx:
        def sb(name, shape, dt=F32):
            return ctx.enter_context(nc.sbuf_tensor(name, shape, dt))

        def sem(name):
            return ctx.enter_context(nc.semaphore(name))

        B = [ctx.enter_context(nc.psum_tensor(f"bank{i}", [P, HALF], F32)) for i in range(8)]

        raw = sb("raw", [P, RAW_SLOTS, SLAB])
        w_hi = sb("w_hi", [P, SLOTS, SLAB], F32R)
        w_lo = sb("w_lo", [P, SLOTS, SLAB], F32R)
        h_hi = sb("h_hi", [P, KT, T], F32R)
        h_lo = sb("h_lo", [P, KT, T], F32R)
        cst = sb("cst", [P, NCONST, P])
        negm = sb("negm", [P, 1 + TT, P], BF16)
        x0_scope = ExitStack()
        x0 = x0_scope.enter_context(nc.sbuf_tensor("x0", [P, TT, D], F32))
        x0_scope.close()
        m_hi = sb("m_hi", [P, KT, M], F32R)
        m_lo = sb("m_lo", [P, KT, M], F32R)
        nrow = sb("nrow", [P, D])
        gT_scope = ExitStack()
        gT_hi = gT_scope.enter_context(nc.sbuf_tensor("gT_hi", [HEADS, T], F32R))
        gT_lo = gT_scope.enter_context(nc.sbuf_tensor("gT_lo", [HEADS, T], F32R))
        gT_scope.close()
        xn = sb("xn", [P, D])
        stat = sb("stat", [P, 6, NORM_TILES])
        ident, tri, ones = cst[:, C_ID, :], cst[:, C_TRI, :], cst[:, C_ONES, :]

        def mb(name, shape, dt=F32, where=ctx):
            return where.enter_context(nc.sbuf_tensor(name, shape, dt))

        mixing = ExitStack()
        mix = mb("mix", [P, MIX, T], where=mixing)
        vec = mb("vec", [P, VROWS], where=mixing)
        inner = ExitStack()
        cw_g = mb("cw_g", [P, TAPS * 24], where=inner)
        cw_s = mb("cw_s", [P, TAPS * 12], where=inner)
        dcol = mb("dcol", [P, XT], where=inner)
        gates = mb("gates", [P, HEADS, KINDS, TT], where=inner)
        cacc = mb("cacc", [P, 2, T], where=inner)

        bcA = mb("bcA", [P, 4, T], where=inner)

        gdn = ExitStack()
        qA = mb("qA", [P, T], where=gdn)
        kA = mb("kA", [P, T], where=gdn)
        vA = mb("vA", [P, T], where=gdn)
        cwB = mb("cwB", [P, 2, 12], where=gdn)
        colB = mb("colB", [P, 2, KINDS, TT], where=gdn)
        selB = mb("selB", [HEADS, 2], F32R, gdn)
        br2B = mb("br2B", [P, 2, 2, TT], where=gdn)
        ssA = mb("ssA", [P, 4, TT], where=gdn)
        k_sq = mb("k_sq", [P, P], where=gdn)
        sqW = mb("sqW", [P, T], where=gdn)

        start = ExitStack()
        rows_g = mb("rows_g", [96, P], where=start)
        rows_s = mb("rows_s", [48, P], where=start)
        rows_v = mb("rows_v", [VROWS, P], where=start)
        wsm = mb("wsm", [P, KT, 32], where=start)
        wsm_hi = mb("wsm_hi", [P, KT, 32], F32R, start)
        wsm_lo = mb("wsm_lo", [P, KT, 32], F32R, start)
        brow = mb("brow", [P, HEADS], where=start)
        arow = mb("arow", [P, HEADS], where=start)
        graw = mb("graw", [32, T], where=start)
        gr = mb("gr", [P, TT, 32], where=start)
        gt = mb("gt", [P, 10, TT, HEADS], where=start)
        mx = mb("mx", [P, MT, D], where=start)
        xn_b = mb("xn_b", [P, D], where=start)
        start.close()

        kB = mb("kB", [P, 2, T], where=gdn)
        qdB = mb("qdB", [P, 2, T], where=gdn)
        q_sqB = mb("q_sqB", [P, 2, T], where=gdn)
        vB = mb("vB", [P, 2, T], where=gdn)
        kdB = mb("kdB", [P, 2, T], where=gdn)
        atB = mb("atB", [P, 2, T], where=gdn)
        nB = mb("nB", [P, 2, T], where=gdn)
        eg = mb("eg", [P, T], where=gdn)
        dt_ = mb("dt_", [P, T], where=gdn)
        u_neg = mb("u_neg", [P, T], where=gdn)
        u_off = mb("u_off", [P, 2, T], where=gdn)
        nW = mb("nW", [P, T], where=gdn)
        mW = mb("mW", [P, T], where=gdn)
        xW = mb("xW", [P, TT * HP], where=gdn)
        stS = mb("stS", [P, P], where=gdn)
        rR = mb("rR", [P, P], where=gdn)
        vN = mb("vN", [P, P], where=gdn)
        oz = mb("oz", [P, T], where=gdn)
        fW = mb("fW", [P, 3, TT], where=gdn)
        gdn.close()

        ssd = ExitStack()
        b_tok = mb("b_tok", [P, GROUPS, T], where=ssd)
        cb = mb("cb", [P, GROUPS, T], where=ssd)
        b_cur = mb("b_cur", [P, T], where=ssd)
        colS = mb("colS", [P, 2, 2, KINDS, TT], where=ssd)
        selS = mb("selS", [HEADS, 2, 2], F32R, ssd)
        cwS = mb("cwS", [P, 2, 6], where=ssd)
        gsq = mb("gsq", [P, GROUPS, T], where=ssd)
        gnS = mb("gnS", [P, 3, GROUPS, TT], where=ssd)
        xA = mb("xA", [P, 2, T], where=ssd)
        egS = mb("egS", [P, 2, T], where=ssd)
        dtS = mb("dtS", [P, 2, T], where=ssd)
        scS = mb("scS", [P, 2, T], where=ssd)
        xdt = mb("xdt", [P, T], where=ssd)
        xdd = mb("xdd", [P, T], where=ssd)
        hst = mb("hst", [P, 3, P], where=ssd)
        y1, y_sq = bcA[:, 0, :], bcA[:, 1, :]
        ssd.close()
        inner.close()
        mixing.close()

        att = ExitStack()
        kmT = mb("kmT", [P, KT, M], where=att)
        v_m = mb("v_m", [P, MT, D], where=att)
        pr = mb("pr", [P, 2, TT, M], where=att)
        prT = mb("prT", [P, 2, MT, T], where=att)
        qmT = mb("qmT", [P, KT, T], where=att)
        oT = mb("oT", [P, KT, T], where=att)
        att.close()

        uT = mb("uT", [P, FT, T])
        ur = mb("ur", [P, 2, T])
        x_res = mb("x_res", [P, TT, D])
        a_hi = mb("a_hi", [P, 4, T], F32R)
        a_lo = mb("a_lo", [P, 4, T], F32R)
        sq_out = mb("sq_out", [P, HALF])
        sm = mb("sm", [P, 2, 4, TT])

        names = """
        par_in id_in cst_in n_row mem_in xr_in out_done
        slab_hi slab_ready slab_used
        n_sq n_add n_mean n_root n_rstd n_xn n_tr n_hi n_lo
        rows_tr rows_cp wsm_hi_ok wsm_lo_ok gate_mm gate_cp gate_raw gate_dve gate_act gate_cs gates_ok
        gT_tr gT_hi_ok gT_lo_ok
        d_cols d_cw d_sse d_rec d_br d_nb d_kb d_qd d_kd d_u d_at d_v d_off d_n1 d_m d_inv d_r d_s d_o2q d_oz d_fe d_fr mix_done
        d_tap a_tap a_silu z_done
        pe_g pe_gm pe_kk pe_kq pe_kt pe_vt pe_mt pe_x pe_n pe_ks pe_v pe_s pe_o pe_f pe_fb
        a_eg a_dt a_q2 a_rinv a_x a_m a_v a_o2 a_ss a_rf
        as_tap ds_tap as_silu zs_done pb_tr pb_cb ab_tok db_cb
        ds_cw ds_cols ds_bcur ds_xdt ds_xdd ds_cd ds_sc ds_h ds_y1 ds_mix
        ps_g ps_m ps_x ps_st ps_y as_eg as_dt as_sq ds_sq
        gn_sum gn_mean gn_root gn_rec
        cut_hi cut_lo row_done x_add kq_ok vm_ok
        at_s at_max at_neg at_exp at_rec at_pn at_tr at_prt at_pv at_o
        up_relu up_sq fin_y
        """.split()
        S = {n: sem(n) for n in names}
        x_in = [sem(f"x_in{t}") for t in range(TT)]
        raw_in = [sem(f"raw_in{j}") for j in range(RAW_SLOTS)]
        block = ctx.enter_context(nc.Block())

        def row(w):
            return w.rearrange("(o n) -> o n", o=1).partition_broadcast(P)

        N1, NM, N2, N3, NF = (0, 0, TT, 0), (1, TT, MT, 1), (2, TT + MT, TT, 0), (3, 2 * TT + MT, TT, 0), (4, 3 * TT + MT, TT, 0)

        def even_blocks(ap, l):
            return ap.rearrange("p (b u w) -> p b u w", u=2, w=1 << l)[:, :, 0, :]

        def chunk(ap, c):
            return ap[:, c * P:(c + 1) * P]

        def bcast(ap, n):
            return ap.unsqueeze(2).to_broadcast([P, ap.shape[1], n])

        @block.sync
        def _(sp):
            w_in_v = a["w_in"].rearrange("(k p) n -> p k n", p=P)

            def slab(s, j, src):
                need(sp, S["slab_ready"], s - RAW_SLOTS + 1)
                dst = raw[:, j % RAW_SLOTS, :]
                if len(src.shape) == 3:
                    dst = dst.rearrange("p (k n) -> p k n", k=KT)
                sp.dma_start(dst, src).then_inc(raw_in[j % RAW_SLOTS], 16)

            def cols(w, c0):
                return w[:, :, bass.ds(c0, P)]

            def rows(w, r0):
                return w[bass.ds(r0, P), :]

            def gdn_slabs(h):
                for j in range(4):
                    slab(S_GDN + 4 * h + j, j, cols(w_in_v, j * GDN + h * P))

            for t in range(TT):
                sp.dma_start(x0[:, t, :], a["x"][0, t * P:(t + 1) * P, :]).then_inc(x_in[t], 16)
            slab(0, 0, cols(w_in_v, 0))
            slab(1, 1, cols(w_in_v, GDN))
            par = [
                (wsm[:, :, 0:16], w_in_v[:, :, 4 * GDN:4 * GDN + 16]),
                (wsm[:, :, 16:32], w_in_v[:, :, GDN_COLS + 2 * D + 2 * BC:]),
                (rows_g[:], a["gdn_conv_w"].rearrange("k (j p) -> (k j) p", p=P)),
                (rows_s[:], a["ssm_conv_w"].rearrange("k (j p) -> (k j) p", p=P)),
                (rows_v[V_CB:V_NW, :], a["ssm_conv_b"].rearrange("(j p) -> j p", p=P)),
                (rows_v[V_NW:V_GN, :], a["ssm_norm_w"].rearrange("(j p) -> j p", p=P)),
                (rows_v[V_GN:VROWS, :], a["gdn_norm_w"].rearrange("(j p) -> j p", p=P)),
                (brow[:, 0:HG], row(a["gdn_dt_bias"])), (brow[:, HG:], row(a["ssm_dt_bias"])),
                (arow[:, 0:HG], row(a["gdn_a_log"])), (arow[:, HG:], row(a["ssm_a_log"])),
                (negm[:], a["negm"]),
            ]
            for hh in range(2):
                d = a["ssm_d"].rearrange("(o j u) -> o j u", o=1, u=2)[:, :, hh]
                par.append((dcol[hh * HP:(hh + 1) * HP, :], d.partition_broadcast(HP)))
            assert len(par) == PAR_DMAS
            with nc.allow_non_contiguous_dma(reason="a few short rows and per-head scalars"):
                for dst, src in par:
                    sp.dma_start(dst, src).then_inc(S["par_in"], 16)
            sp.dma_start(mx[:], a["mem"].rearrange("b (t p) d -> p (b t) d", p=P)).then_inc(S["mem_in"], 16)
            slab(2, 2, cols(w_in_v, 2 * GDN))
            slab(3, 3, cols(w_in_v, 3 * GDN))
            with sp.Fori(1, HG) as h:
                gdn_slabs(h)
            for n in range(4):
                slab(S_BC + n, n, cols(w_in_v, GDN_COLS + 2 * D + n * P))

            def xz_slabs(i):
                for u in range(2):
                    slab(S_XZ + 4 * i + 2 * u, 2 * u, cols(w_in_v, GDN_COLS + D + (2 * i + u) * P))
                    slab(S_XZ + 4 * i + 2 * u + 1, 2 * u + 1, cols(w_in_v, GDN_COLS + (2 * i + u) * P))

            with sp.Fori(0, XT // 2) as i:
                xz_slabs(i)

            def row_slabs(w, s0, n):
                with sp.Fori(0, n // 4) as i:
                    for j in range(4):
                        slab(s0 + 4 * i + j, j, rows(w, (4 * i + j) * P))

            def col_slabs(w, s0, n):
                wv = w.rearrange("(k p) n -> p k n", p=P)
                with sp.Fori(0, n // 4) as i:
                    for j in range(4):
                        slab(s0 + 4 * i + j, j, cols(wv, (4 * i + j) * P))

            for k in range(6):
                slab(S_OUT + k, k % 4, rows(a["w_out"], k * P))
            sp.wait_ge(S["ds_mix"], XT)
            sp.wait_ge(S["ps_y"], XT)
            for t in range(TT):
                sp.dma_start(x_res[:, t, :], a["x"][0, t * P:(t + 1) * P, :]).then_inc(S["xr_in"], 16)
            for k in range(6, MIX):
                slab(S_OUT + k, k % 4, rows(a["w_out"], k * P))
            mem_w = {"k": a["wk_mem"].rearrange("(k p) n -> p k n", p=P), "q": a["wq_mem"].rearrange("(k p) n -> p k n", p=P)}
            for pos, (w, i) in enumerate(MEM_ORDER):
                slab(S_MEM + pos, pos % 4, rows(a["wv_mem"], i * P) if w == "v" else cols(mem_w[w], i * P))
            row_slabs(a["wo_mem"], S_WO, KT)
            col_slabs(a["w_up"], S_UP, FT)
            row_slabs(a["w_down"], S_DOWN, FT)
            for t in range(TT):
                sp.wait_ge(S["fin_y"], t + 1)
                sp.dma_start(out[0, t * P:(t + 1) * P, :], x_res[:, t, :]).then_inc(S["out_done"], 16)
            sp.wait_ge(S["out_done"], 16 * TT)

        @block.gpsimd
        def _(pool):
            def cut(i, j):
                s = 4 * i + j
                pool.wait_ge(S["slab_hi"], s + 1)
                nc.gpsimd.tensor_tensor(w_lo[:, j, :], raw[:, j % RAW_SLOTS, :], w_hi[:, j, :].bitcast(F32),
                                        ALU.subtract).then_inc(S["slab_ready"], 1)

            for j in range(SLOTS):
                cut(0, j)
            with pool.Fori(1, N_SLABS // SLOTS) as i:
                for j in range(SLOTS):
                    cut(i, j)

        @block.tensor
        def _(pe):
            mm = nc.tensor.matmul

            def dense_k(s, j, bank, k, r_hi=h_hi, r_lo=h_lo, n=T):
                if k == 0:
                    pe.wait_ge(S["slab_ready"], s + 1)
                wh, wl = w_hi[:, j, k * P:(k + 1) * P], w_lo[:, j, k * P:(k + 1) * P]
                mm(bank[:, 0:n], wh, r_hi[:, k, :], start=(k == 0), stop=False)
                mm(bank[:, 0:n], wh, r_lo[:, k, :], start=False, stop=False)
                m = mm(bank[:, 0:n], wl, r_hi[:, k, :], start=False, stop=(k == KT - 1))
                if k == KT - 1:
                    m.then_inc(S["slab_used"], 1)

            def norm_tile(batch, i, src=xn):
                g = batch[1] + i
                pe.wait_ge(S["n_xn"], g + 1)
                for f in range(2):
                    bank = B[2 * (i + batch[3]) + f]
                    for q in range(4):
                        m = nc.tensor.transpose(chunk(bank, q), src[:, (4 * f + q) * P:(4 * f + q + 1) * P], ident)
                    m.then_inc(S["n_tr"], 1)

            def row_tile(j, t, lh, ll, first, last, banks):
                for f in range(2):
                    fs = slice(f * HALF, (f + 1) * HALF)
                    mm(banks[2 * t + f][:], lh, w_hi[:, j, fs], start=first, stop=False)
                    mm(banks[2 * t + f][:], lh, w_lo[:, j, fs], start=False, stop=False)
                for f in range(2):
                    fs = slice(f * HALF, (f + 1) * HALF)
                    m = mm(banks[2 * t + f][:], ll, w_hi[:, j, fs], start=False, stop=last)
                return m

            def row_part(s0, c0, i, j, t, first=False, last=False):
                k = 4 * i + j
                pe.wait_ge(S["slab_ready"], s0 + k + 1)
                pe.wait_ge(S["cut_lo"], c0 + k + 1)
                m = row_tile(j, t, chunk(a_hi[:, j, :], t), chunk(a_lo[:, j, :], t), first, last, B)
                if t == TT - 1:
                    m.then_inc(S["slab_used"], 1)
                elif last:
                    m.then_inc(S["row_done"], 1)

            def row_last(s0, c0, i, first, norm_batch):
                for t in range(TT):
                    if first:
                        pe.wait_ge(S["x_add"], 2 * TT + 2 * t + 2)
                    for j in range(4):
                        if j == 1 and t > 1 and norm_batch:
                            norm_tile(norm_batch, t - 2)
                        row_part(s0, c0, i, j, t, first and j == 0, j == 3)
                if norm_batch:
                    norm_tile(norm_batch, TT - 2)

            pe.wait_ge(S["id_in"], 16)
            for i in range(TT):
                norm_tile(N1, i, (xn, xn_b)[i % 2])
            pe.wait_ge(S["par_in"], PAR_DMAS * 16)
            pe.wait_ge(S["n_lo"], 4)
            nc.tensor.transpose(B[2][:, 0:96], rows_g[:], cst[0:96, C_ID, 0:96])
            nc.tensor.transpose(B[2][:, 96:144], rows_s[:], cst[0:48, C_ID, 0:48])
            nc.tensor.transpose(B[2][:, 144:144 + VROWS], rows_v[:],
                                cst[0:VROWS, C_ID, 0:VROWS]).then_inc(S["rows_tr"], 1)
            pe.wait_ge(S["n_lo"], 2 * TT)
            pe.wait_ge(S["wsm_lo_ok"], 1)
            for k in range(KT):
                mm(B[6][0:32, :], wsm_hi[:, k, :], h_hi[:, k, :], start=(k == 0), stop=False)
                mm(B[6][0:32, :], wsm_hi[:, k, :], h_lo[:, k, :], start=False, stop=False)
                m = mm(B[6][0:32, :], wsm_lo[:, k, :], h_hi[:, k, :], start=False, stop=(k == KT - 1))
            m.then_inc(S["gate_mm"], 1)

            def gate_tokens():
                pe.wait_ge(S["gate_cp"], 1)
                pe.wait_ge(S["n_sq"], 2 * (TT + MT))
                for t in range(TT):
                    m = nc.tensor.transpose(B[7][:, t * 32:(t + 1) * 32], graw[:, t * P:(t + 1) * P], cst[0:32, C_ID, 0:32])
                m.then_inc(S["gate_mm"], 1)

            def gate_sums():
                pe.wait_ge(S["gate_cs"], 1)
                pe.wait_ge(S["cst_in"], 16)
                gsrc = gt[:, 5].rearrange("p c h -> p (c h)")
                mm(B[7][:, P:P + TT * HEADS], tri, gsrc, start=True, stop=True)
                mm(B[7][:, 2 * P:2 * P + TT * HEADS], ones, gsrc, start=True, stop=True).then_inc(S["gate_mm"], 1)

            for x in range(32):
                if x == 4:
                    gate_tokens()
                if x == 2:
                    pe.wait_ge(S["rows_cp"], 1)
                    norm_tile(NM, 0)
                if x == 6:
                    norm_tile(NM, 1)
                if x == 24:
                    pe.wait_ge(S["gates_ok"], 1)
                    for t in range(TT):
                        m = nc.tensor.transpose(B[7][0:HEADS, t * P:(t + 1) * P], gt[:, 8, t, :], ident)
                    m.then_inc(S["gT_tr"], 1)
                if x == 16:
                    gate_sums()
                if x in (16, 24):
                    pe.wait_ge(S["d_tap"], 3 * (x // 8 - 1))
                dense_k(x // 8, x // 8, B[(x // 8) % 2], x % 8)

            def gdn_iter(h, a_, b, par, dense, inv, chain):
                pa, pb = 1 - par, par
                steps = iter(range({"head": 32, "bc": 32, "xz": 16, None: 0}[dense]))

                def D(n):
                    for _ in range(n):
                        x = next(steps, None)
                        if x is None:
                            return
                        j, k = x // 8, x % 8
                        if dense == "head":
                            if k == 0:
                                if j == 1:
                                    need(pe, S["z_done"], h)
                                else:
                                    need(pe, S["d_tap"], 9 * h + 3 * max(j - 1, 0))
                            dense_k(4 * h + j, j, B[j % 2], k)
                        elif dense == "bc":
                            if k == 0:
                                if j == 0:
                                    pe.wait_ge(S["d_tap"], 9 * HG)
                                elif j == 1:
                                    pe.wait_ge(S["z_done"], HG)
                                else:
                                    pe.wait_ge(S["ds_tap"], 3 * (j - 1))
                            dense_k(S_BC + j, j, B[j % 2], k)
                        else:
                            if k == 0:
                                pe.wait_ge(S["ds_tap"], 3 * (3 + j))
                            dense_k(S_XZ + j, j, B[j], k)

                def gsum():
                    pe.wait_ge(S["d_cols"], a_ + 1)
                    need(pe, S["d_v"], a_)
                    if isinstance(a_, int) and a_ == 0:
                        pe.wait_ge(S["gT_hi_ok"], 1)
                        pe.wait_ge(S["gT_lo_ok"], 1)
                    sel = selB[:, pa:pa + 1].to_broadcast([HEADS, P])
                    mm(B[7][:], sel, gT_hi[:], start=True, stop=False, skip_group_check=True)
                    mm(B[7][:], sel, gT_lo[:], start=False, stop=False, skip_group_check=True).then_inc(S["pe_g"], 1)

                def mask():
                    pe.wait_ge(S["a_eg"], a_ + 1)
                    mm(B[7][:], negm[:, 0, :], negm[:, 1:, :].rearrange("p c t -> p (c t)"), start=False,
                       stop=True, skip_group_check=True).then_inc(S["pe_gm"], 1)

                def kk():
                    need(pe, S["a_x"], 6 * a_)
                    pe.wait_ge(S["a_silu"], 3 * a_ + 2)
                    for c in range(TT):
                        m = mm(chunk(B[2], c), chunk(kA, c), chunk(kA, c), start=True, stop=True)
                    m.then_inc(S["pe_kk"], 1)

                def kq():
                    need(pe, S["d_m"], 6 * a_)
                    for c in range(TT):
                        m = mm(chunk(B[3], c), chunk(kA, c), chunk(qA, c), start=True, stop=True)
                    m.then_inc(S["pe_kq"], 1)

                def kt():
                    need(pe, S["d_inv"], a_)
                    for c in range(TT):
                        m = nc.tensor.transpose(chunk(B[4], c), chunk(kA, c), ident)
                    m.then_inc(S["pe_kt"], 1)

                def vt():
                    pe.wait_ge(S["a_dt"], a_ + 1)
                    pe.wait_ge(S["a_silu"], 3 * a_ + 3)
                    for c in range(TT):
                        m = nc.tensor.transpose(chunk(B[7], c), chunk(vA, c), ident)
                    m.then_inc(S["pe_vt"], 1)

                def mt(l):
                    if l == 0:
                        pe.wait_ge(S["d_n1"], a_ + 1)
                        pe.wait_ge(S["d_kd"], a_ + 1)
                    else:
                        pe.wait_ge(S["d_m"], 6 * a_ + l)
                        pe.wait_ge(S["a_m"], 6 * a_ + l)
                    for c in range(TT):
                        m = nc.tensor.transpose(chunk(B[4], c), chunk(nW if l == 0 else mW, c), ident)
                    m.then_inc(S["pe_mt"], 1)

                def xm(l):
                    pe.wait_ge(S["d_off"], 7 * a_ + l + 1)
                    if l == 1:
                        pe.wait_ge(S["a_m"], 6 * a_ + 1)
                        pe.wait_ge(S["d_u"], a_ + 1)
                    else:
                        pe.wait_ge(S["d_m"], 6 * a_ + l - 1)
                        pe.wait_ge(S["a_x"], 6 * a_ + l - 1)
                    for c in range(TT):
                        m = mm(B[2][:, c * HP:(c + 1) * HP], chunk(u_off[:, l % 2, :], c), even_blocks(chunk(mW, c), l),
                               start=True, stop=True)
                    m.then_inc(S["pe_x"], 1)

                def nn(l):
                    pe.wait_ge(S["a_x"], 6 * a_ + l)
                    if l == 1:
                        pe.wait_ge(S["d_at"], a_ + 1)
                    else:
                        pe.wait_ge(S["a_m"], 6 * a_ + l)
                        pe.wait_ge(S["d_m"], 6 * a_ + l - 1)
                    for c in range(TT):
                        half = slice(c * HP, (c + 1) * HP)
                        m = mm(B[3][:, half], chunk(nW, c), xW[:, half], start=True, stop=True)
                    m.then_inc(S["pe_n"], 1)

                def ks(c):
                    pe.wait_ge(S["d_s"], 3 * b + c)
                    mm(B[5][:, 0:P], chunk(kB[:, pb, :], c), stS[:], start=True, stop=True).then_inc(S["pe_ks"], 1)

                def vv(c):
                    if c == 0:
                        pe.wait_ge(S["d_inv"], b + 1)
                        pe.wait_ge(S["d_v"], b + 1)
                        need(pe, S["mix_done"], b)
                        rhs = chunk(vB[:, pb, :], 0)
                    else:
                        pe.wait_ge(S["d_r"], 3 * b + c)
                        rhs = rR[:]
                    mm(B[5][:, 0:P], chunk(nB[:, pb, :], c), rhs, start=True, stop=True).then_inc(S["pe_v"], 1)

                def oo(c):
                    if c == 0:
                        need(pe, S["d_oz"], b)
                        pe.wait_ge(S["d_at"], b + 1)
                    else:
                        mm(chunk(B[6], c), stS[:], chunk(qdB[:, pb, :], c), start=True, stop=False)
                    pe.wait_ge(S["a_v"], 4 * b + c + 1)
                    m = mm(chunk(B[6], c), vN[:], chunk(atB[:, pb, :], c), start=(c == 0), stop=True)
                    if c < TT - 1:
                        mm(B[5][:, 0:P], chunk(kdB[:, pb, :], c), vN[:], start=True, stop=True).then_inc(S["pe_s"], 1)
                    else:
                        m.then_inc(S["pe_o"], 1)

                def fsum():
                    pe.wait_ge(S["d_o2q"], b + 1)
                    for c in range(TT):
                        m = mm(B[5][:, c:c + 1], chunk(sqW, c), cst[:, C_VEC, 0:1], start=True, stop=True)
                    m.then_inc(S["pe_f"], 1)

                def fb():
                    pe.wait_ge(S["d_fr"], b + 1)
                    for c in range(TT):
                        m = mm(chunk(B[5], c), fW[:, 2, c:c + 1].to_broadcast([P, P]), ident, start=True, stop=True)
                    m.then_inc(S["pe_fb"], 1)

                def b_tr():
                    pe.wait_ge(S["a_x"], 6 * HG)
                    pe.wait_ge(S["d_m"], 6 * HG)
                    pe.wait_ge(S["as_silu"], 2)
                    for g in range(GROUPS):
                        for c in range(TT):
                            m = nc.tensor.transpose(chunk(B[2 + g], c), chunk(bcA[:, g, :], c), ident)
                        m.then_inc(S["pb_tr"], 1)

                def cb_mm():
                    pe.wait_ge(S["d_inv"], HG)
                    pe.wait_ge(S["ab_tok"], 1)
                    pe.wait_ge(S["as_silu"], 4)
                    for g in range(GROUPS):
                        for c in range(TT):
                            m = mm(chunk(B[4 - 2 * g], c), chunk(bcA[:, g, :], c), chunk(bcA[:, 2 + g, :], c), start=True, stop=True)
                        m.then_inc(S["pb_cb"], 1)

                I = lambda f, *x: f(*x) if inv else None
                C = lambda f, *x: f(*x) if chain else None
                E = lambda f: f() if dense == "xz" else None
                I(gsum); I(kk); D(1)
                I(kt); I(kq); C(vv, 0); E(b_tr); D(2)
                I(mask); D(1); C(oo, 0); D(1)
                C(ks, 1); D(1)
                I(vt); C(vv, 1); D(2)
                I(mt, 0); C(oo, 1); D(1)
                I(xm, 1); C(ks, 2); D(2)
                I(nn, 1); C(vv, 2); D(1)
                I(xm, 2); I(mt, 1); C(oo, 2); D(2)
                I(nn, 2); C(ks, 3); E(cb_mm); D(2)
                I(xm, 3); I(mt, 2); C(vv, 3); D(2)
                I(nn, 3); C(oo, 3); D(2)
                I(xm, 4); I(mt, 3); D(2)
                I(nn, 4); C(fsum); D(2)
                I(xm, 5); I(mt, 4); D(3)
                I(nn, 5); C(fb); D(1)
                I(xm, 6); I(mt, 5); D(2)
                I(nn, 6); D(2)
                I(mt, 6)

            gdn_iter(1, 0, None, 1, "head", True, False)
            gdn_iter(2, 1, 0, 0, "head", True, True)
            gdn_iter(3, 2, 1, 1, "head", True, True)
            with pe.Fori(2, HG // 2) as i:
                gdn_iter(2 * i, 2 * i - 1, 2 * i - 2, 0, "head", True, True)
                gdn_iter(2 * i + 1, 2 * i, 2 * i - 1, 1, "head", True, True)
            gdn_iter(None, HG - 1, HG - 2, 0, "bc", True, True)
            gdn_iter(None, None, HG - 1, 1, "xz", False, True)

            def ssd_iter(j, i, par, dense, ssd_):
                pi = 1 - par
                steps = iter(range(16))

                def D(n):
                    if not dense:
                        return
                    for _ in range(n):
                        x = next(steps)
                        u, k = x // 8, x % 8
                        if k == 0 and u == 0:
                            pe.wait_ge(S["ds_tap"], 3 * (3 + j))
                        elif k == 0:
                            pe.wait_ge(S["zs_done"], j)
                        dense_k(S_XZ + 2 * j + u, (2 * par + u), B[u], k)

                def gsum(hh):
                    bank = B[7] if hh == 0 else B[2]
                    if hh == 0:
                        pe.wait_ge(S["ds_cols"], i + 1)
                    elif isinstance(i, int) and i == 0:
                        pe.wait_ge(S["db_cb"], GROUPS)
                    need(pe, S["as_dt"], 2 * i - 1 + hh)
                    sel = selS[:, pi, hh:hh + 1].to_broadcast([HEADS, P])
                    mm(bank[:], sel, gT_hi[:], start=True, stop=False, skip_group_check=True)
                    mm(bank[:], sel, gT_lo[:], start=False, stop=False, skip_group_check=True).then_inc(S["ps_g"], 1)

                def mask(hh):
                    bank = B[7] if hh == 0 else B[2]
                    pe.wait_ge(S["as_eg"], 2 * i + 1 + hh)
                    mm(bank[:], negm[:, 0, :], negm[:, 1:, :].rearrange("p c t -> p (c t)"), start=False,
                       stop=True, skip_group_check=True).then_inc(S["ps_m"], 1)

                def xt():
                    pe.wait_ge(S["as_silu"], i + 5)
                    if isinstance(i, int) and i == 0:
                        pe.wait_ge(S["ab_tok"], GROUPS)
                    need(pe, S["ds_xdt"], i)
                    for c in range(TT):
                        m = nc.tensor.transpose(chunk(B[3], c), chunk(xA[:, pi, :], c), ident)
                    m.then_inc(S["ps_x"], 1)

                def st():
                    pe.wait_ge(S["ds_xdd"], i + 1)
                    pe.wait_ge(S["ds_bcur"], i + 1)
                    need(pe, S["ds_h"], 3 * i)
                    for c in range(TT - 1):
                        m = mm(chunk(B[4], c), chunk(b_cur, c), chunk(xdd, c), start=True, stop=True)
                    m.then_inc(S["ps_st"], 1)

                def yy():
                    pe.wait_ge(S["ds_sc"], 2 * i + 2)
                    pe.wait_ge(S["ds_cd"], 2 * i + 2)
                    pe.wait_ge(S["ds_h"], 3 * i + 3)
                    need(pe, S["ds_y1"], i)
                    for c in range(TT):
                        for hh in range(2):
                            o = B[6][hh * HP:(hh + 1) * HP, c * P:(c + 1) * P]
                            hs = slice(c * P + hh * HP, c * P + (hh + 1) * HP)
                            m = mm(o, xdt[:, hs], chunk(scS[:, hh, :], c), start=True, stop=(c == 0))
                            if c:
                                m = mm(o, hst[:, c - 1, hh * HP:(hh + 1) * HP], chunk(egS[:, hh, :], c),
                                       start=False, stop=True)
                    m.then_inc(S["ps_y"], 1)

                def out_part(j):
                    if not dense:
                        row_part(S_OUT, 0, 0, j, 0, j == 0)

                gsum(0); xt(); D(2)
                out_part(0)
                gsum(1); D(2)
                mask(0); D(2)
                out_part(1)
                mask(1); D(2)
                out_part(2)
                st(); D(6)
                out_part(3)
                yy(); D(2)

            ssd_iter(1, 0, 1, True, True)
            with pe.Fori(1, XT // 2) as q:
                ssd_iter(2 * q, 2 * q - 1, 0, True, True)
                ssd_iter(2 * q + 1, 2 * q, 1, True, True)
            pe.wait_ge(S["zs_done"], XT)
            pe.wait_ge(S["ds_tap"], 3 * (4 + XT))
            ssd_iter(None, XT - 1, 0, False, True)

            pe.wait_ge(S["as_dt"], 2 * XT)
            pe.wait_ge(S["ds_xdt"], XT)
            for j in range(4):
                row_part(S_OUT, 0, 0, j, 1, j == 0)
            pe.wait_ge(S["ds_sq"], XT + 1)
            for g in range(GROUPS):
                for c in range(TT):
                    n = g * TT + c
                    m = mm(B[5][:, n:n + 1], chunk(gsq[:, g, :], c), ones[:, 0:1], start=True, stop=True)
            m.then_inc(S["gn_sum"], 1)
            pe.wait_ge(S["ds_h"], 3 * XT)
            pe.wait_ge(S["gn_mean"], 1)
            pe.wait_ge(S["ds_y1"], XT)
            for j in range(4):
                for t in (2, 3):
                    row_part(S_OUT, 0, 0, j, t, j == 0)
            for i in (1, 2):
                for j in range(4):
                    for t in range(TT):
                        if i == 2 and j == 0:
                            pe.wait_ge(S["x_add"], 2 * t + 2)
                        row_part(S_OUT, 0, i, j, t, i == 2 and j == 0, j == 3)
            row_last(S_OUT, 0, 3, True, N2)

            def mem_product(pos):
                w, i = MEM_ORDER[pos]
                d = mem_made(pos)
                if w == "v":
                    pe.wait_ge(S["slab_ready"], S_MEM + pos + 1)
                    if i == 0:
                        pe.wait_ge(S["n_lo"], 2 * (2 * TT + MT))
                    for t in range(MT):
                        m = row_tile(pos % 4, t, chunk(m_hi[:, i, :], t), chunk(m_lo[:, i, :], t), i == 0, i == KT - 1, B[4:])
                    m.then_inc(S["slab_used"], 1)
                    return
                if d < 2:
                    pe.wait_ge(S["n_lo"], 2 * (TT + MT + 1))
                else:
                    pe.wait_ge(S["kq_ok"], d - 1)
                if w == "q" and i == 0:
                    pe.wait_ge(S["n_lo"], 2 * (2 * TT + MT))
                r_hi, r_lo, n = (m_hi, m_lo, M) if w == "k" else (h_hi, h_lo, T)
                for k in range(KT):
                    dense_k(S_MEM + pos, pos % 4, B[d % 2], k, r_hi, r_lo, n)

            for pos in range(MEM_FIRST):
                mem_product(pos)
                if pos == 1:
                    norm_tile(N2, TT - 1)

            def scores(hd):
                pe.wait_ge(S["kq_ok"], mem_made(MEM_ORDER.index(("q", 2 * hd + 1)) + 1))
                need(pe, S["at_exp"], TT * hd)
                for t in range(TT):
                    o = B[2 + t // 2][:, (t % 2) * M:(t % 2 + 1) * M]
                    for u in range(2):
                        m = mm(o, chunk(qmT[:, 2 * hd + u, :], t), kmT[:, 2 * hd + u, :], start=(u == 0), stop=(u == 1))
                    if t % 2:
                        m.then_inc(S["at_s"], 1)

            def probs_tr(hd):
                pe.wait_ge(S["at_pn"], hd + 1)
                if hd:
                    pe.wait_ge(S["at_prt"], MT * hd)
                else:
                    pe.wait_ge(S["vm_ok"], 2 * MT)
                for mt_ in range(MT):
                    for t in range(TT):
                        m = nc.tensor.transpose(chunk(B[4 + mt_], t), pr[:, hd % 2, t, mt_ * P:(mt_ + 1) * P], ident)
                    m.then_inc(S["at_tr"], 1)

            def values(hd):
                pe.wait_ge(S["at_prt"], MT * (hd + 1))
                need(pe, S["at_o"], 2 * hd)
                for u in range(2):
                    for mt_ in range(MT):
                        d0 = hd * HD + u * P
                        m = mm(B[6 + u][:], v_m[:, mt_, d0:d0 + P], prT[:, hd % 2, mt_, :], start=(mt_ == 0), stop=(mt_ == 1))
                    m.then_inc(S["at_pv"], 1)

            scores(0)
            for hd in range(AH - 1):
                for pos in MEM_FILL[hd]:
                    mem_product(pos)
                probs_tr(hd)
                scores(hd + 1)
                values(hd)
            for j in range(4):
                if j == 0:
                    pe.wait_ge(S["kq_ok"], 2 * KT)
                row_part(S_WO, MIX, 0, j, 0, j == 0)
            probs_tr(AH - 1)
            pe.wait_ge(S["at_exp"], TT * AH)
            for j in range(4):
                row_part(S_WO, MIX, 0, j, 1, j == 0)
            values(AH - 1)
            pe.wait_ge(S["at_prt"], MT * AH)
            pe.wait_ge(S["at_o"], 2 * AH)
            for j in range(4):
                for t in (2, 3):
                    row_part(S_WO, MIX, 0, j, t, j == 0)
            row_last(S_WO, MIX, 1, False, N3)

            def up_tokens(j, lo, hi):
                pe.wait_ge(S["slab_ready"], S_UP + j + 1)
                for k in range(KT):
                    if (j, lo, k) == (1, 0, KT // 2):
                        norm_tile(N3, TT - 1)
                    wh, wl = w_hi[:, j, k * P:(k + 1) * P], w_lo[:, j, k * P:(k + 1) * P]
                    mm(B[j][:, lo:hi], wh, h_hi[:, k, lo:hi], start=(k == 0), stop=False)
                    mm(B[j][:, lo:hi], wh, h_lo[:, k, lo:hi], start=False, stop=False)
                    m = mm(B[j][:, lo:hi], wl, h_hi[:, k, lo:hi], start=False, stop=(k == KT - 1))
                if hi == T:
                    m.then_inc(S["slab_used"], 1)

            pe.wait_ge(S["n_lo"], 2 * (3 * TT + MT) - 4)
            up_tokens(0, 0, T // 2)
            up_tokens(1, 0, T // 2)
            pe.wait_ge(S["n_lo"], 2 * (3 * TT + MT))
            up_tokens(0, T // 2, T)
            up_tokens(1, T // 2, T)

            def up(i, j):
                n = 4 * i + j
                need(pe, S["up_relu"], n - 1)
                for k in range(KT):
                    dense_k(S_UP + n, j, B[j % 2], k)

            for j in (2, 3):
                up(0, j)
            with pe.Fori(1, FT // 4) as i:
                for j in range(4):
                    up(i, j)
            pe.wait_ge(S["up_relu"], FT)

            def down(i, first):
                for j in range(4):
                    for t in range(TT):
                        row_part(S_DOWN, MIX + KT, i, j, t, first and j == 0)

            down(0, True)
            with pe.Fori(1, FT // 4 - 1) as i:
                down(i, False)
            row_last(S_DOWN, MIX + KT, FT // 4 - 1, False, None)

        @block.scalar
        def _(act):
            A = nc.scalar.activation

            def norm_sq(batch, i, src, dump):
                g = batch[1] + i
                for f in range(2):
                    need(act, S["n_sq"], 2 * g + f)
                    A(dump, src[:, f * HALF:(f + 1) * HALF], ACT.Square,
                      accum_out=stat[:, f, g:g + 1]).then_inc(S["n_sq"], 1)

            def norm_root(batch, i):
                g = batch[1] + i
                act.wait_ge(S["n_mean"], g + 1)
                A(stat[:, 4, g:g + 1], stat[:, 3, g:g + 1], ACT.Sqrt).then_inc(S["n_root"], 1)

            def norm_hi(batch, i, dst):
                g = batch[1] + i
                for f in range(2):
                    act.wait_ge(S["n_tr"], 2 * g + f + 1)
                    A(dst[:, 4 * f:4 * f + 4, i * P:(i + 1) * P], B[2 * (i + batch[3]) + f][:].rearrange("p (q t) -> p q t", q=4),
                      ACT.Copy).then_inc(S["n_hi"], 1)

            def tile_hi(s0, i, j, src, scale=None):
                k = 4 * i + j
                if not (isinstance(i, int) and i == 0):
                    w_cut(s0 // 4 + i, j)
                if scale is None:
                    A(a_hi[:, j, :], src(k), ACT.Copy).then_inc(S["cut_hi"], 1)
                else:
                    A(a_hi[:, j, :], src(k), ACT.Copy, scale=scale).then_inc(S["cut_hi"], 1)

            def product_norm(batch, seg, nxt, dst):
                for i in range(TT):
                    g0 = 8 * seg + 2 * i
                    if i == TT - 1:
                        w_cut(nxt // 4, 1)
                        norm_hi(batch, i - 1, dst)
                    act.wait_ge(S["x_add"], g0 + 2)
                    norm_sq(batch, i, x_res[:, i, :], sq_out[:])
                    norm_root(batch, i)
                    if i == TT - 2:
                        w_cut(nxt // 4, 0)
                    if 0 < i < TT - 1:
                        norm_hi(batch, i - 1, dst)
                w_cut(nxt // 4, 2)

            def w_cut(i, j):
                if isinstance(i, int) and 4 * i + j >= N_SLABS:
                    return
                act.wait_ge(raw_in[j % RAW_SLOTS], 16 * (2 * i + j // 2 + 1))
                need(act, S["slab_used"], 4 * i + j - SLOTS + 1)
                A(w_hi[:, j, :], raw[:, j % RAW_SLOTS, :], ACT.Copy).then_inc(S["slab_hi"], 1)

            def load_row(w, tiles_before):
                act.wait_ge(S["n_xn"], tiles_before)
                act.dma_start(nrow[:], row(w)).then_inc(S["n_row"], 16)

            act.dma_start(cst[:, C_ID, :], a["const"][:, C_ID, :]).then_inc(S["id_in"], 16)
            act.dma_start(nrow[:], row(a["norm1_w"])).then_inc(S["n_row"], 16)
            act.dma_start(cst[:, C_TRI:, :], a["const"][:, C_TRI:, :]).then_inc(S["cst_in"], 16)
            for i in range(TT):
                act.wait_ge(x_in[i], 16)
                norm_sq(N1, i, x0[:, i, :], B[7][:])
                norm_root(N1, i)
                if i > 1:
                    norm_hi(N1, i - 2, h_hi)
            norm_hi(N1, TT - 2, h_hi)
            w_cut(0, 0)
            act.wait_ge(S["par_in"], PAR_DMAS * 16)
            A(wsm_hi[:], wsm[:], ACT.Copy).then_inc(S["wsm_hi_ok"], 1)
            norm_hi(N1, TT - 1, h_hi)
            w_cut(0, 1)
            load_row(a["mem_norm_w"], TT)
            act.wait_ge(S["mem_in"], 16)
            act.wait_ge(S["n_lo"], 2 * TT)
            for i in range(MT):
                norm_sq(NM, i, mx[:, i, :], B[7][:])
                norm_root(NM, i)
            w_cut(0, 2)
            w_cut(0, 3)

            act.wait_ge(S["gate_raw"], 1)
            A(gt[:, 2], gt[:, 1], ACT.Exp, scale=-1.0)
            A(gt[:, 3, :, 0:HG], gr[:, :, 0:HG], ACT.Exp, scale=-1.0)
            A(arow[:], arow[:], ACT.Exp).then_inc(S["gate_act"], 1)
            for i in range(MT):
                norm_hi(NM, i, m_hi)

            def gate_exp():
                act.wait_ge(S["gate_raw"], 2)
                A(gt[:, 1], gt[:, 0], ACT.Exp)
                A(gt[:, 2], gt[:, 8], ACT.Exp)
                A(gt[:, 3], gt[:, 9], ACT.Exp).then_inc(S["gate_act"], 1)

            def gdn_iter(h, a_, b, par, dense, inv, chain):
                pa, pb = 1 - par, par

                def eg_():
                    act.wait_ge(S["pe_g"], a_ + 1)
                    need(act, S["d_qd"], a_)
                    A(eg[:], B[7][:], ACT.Exp).then_inc(S["a_eg"], 1)

                def dt():
                    act.wait_ge(S["pe_gm"], a_ + 1)
                    act.wait_ge(S["d_cols"], a_ + 1)
                    need(act, S["d_u"], a_)
                    need(act, S["d_at"], a_)
                    for c in range(TT):
                        m = A(chunk(dt_, c), chunk(B[7], c), ACT.Exp, bias=colB[:, pa, G_NEG, c:c + 1])
                    m.then_inc(S["a_dt"], 1)

                def q2():
                    act.wait_ge(S["a_silu"], 3 * a_ + 1)
                    need(act, S["d_o2q"], a_ - 1)
                    A(q_sqB[:, pa, :], qA[:], ACT.Square, scale=float(np.sqrt(EPS) * P)).then_inc(S["a_q2"], 1)

                def rinv():
                    act.wait_ge(S["d_sse"], a_ + 1)
                    need(act, S["d_v"], a_)
                    A(ssA[:, 1, :], ssA[:, 0, :], ACT.Sqrt).then_inc(S["a_rinv"], 1)

                def v(c):
                    act.wait_ge(S["pe_v"], 4 * b + c + 1)
                    A(vN[:], B[5][:, 0:P], ACT.Copy, scale=br2B[:, pb, 0, c:c + 1]).then_inc(S["a_v"], 1)

                def m_(l):
                    act.wait_ge(S["pe_mt"], 7 * a_ + l + 1)
                    A((nW if l else mW)[:], B[4][:], ACT.Copy).then_inc(S["a_m"], 1)

                def x_(l):
                    act.wait_ge(S["pe_x"], 6 * a_ + l)
                    A(xW[:], B[2][:, 0:TT * HP], ACT.Copy).then_inc(S["a_x"], 1)

                def ss():
                    act.wait_ge(S["pe_kt"], a_ + 1)
                    need(act, S["d_sse"], a_)
                    for c in range(TT):
                        need(act, S["a_ss"], 4 * a_ + c)
                        A(k_sq[:], chunk(B[4], c), ACT.Square, accum_out=ssA[:, 3, c:c + 1]).then_inc(S["a_ss"], 1)

                def o2():
                    act.wait_ge(S["pe_o"], b + 1)
                    need(act, S["pe_f"], b)
                    A(sqW[:], B[6][:], ACT.Square).then_inc(S["a_o2"], 1)

                def rf():
                    act.wait_ge(S["d_fe"], b + 1)
                    A(fW[:, 1, :], fW[:, 0, :], ACT.Sqrt).then_inc(S["a_rf"], 1)

                def tap(t):
                    act.wait_ge(S["slab_used"], 4 * h + t + 1)
                    act.wait_ge(S["d_cw"], h + 1)
                    need(act, S["a_silu"], 3 * h + t - 1)
                    A(cacc[:, t % 2, :], B[t % 2][:], ACT.Copy, scale=cwB[:, par, 9 + t:10 + t]).then_inc(S["a_tap"], 1)

                def silu(t):
                    act.wait_ge(S["d_tap"], 9 * h + 3 * t + 3)
                    if inv:
                        act.wait_ge(S[("pe_kq", "pe_kt", "pe_vt")[t]], a_ + 1)
                        if t < 2:
                            act.wait_ge(S[("d_qd", "d_kb")[t]], a_ + 1)
                        if t == 0:
                            act.wait_ge(S["a_q2"], a_ + 1)
                    A((qA, kA, vA)[t][:], cacc[:, t % 2, :], ACT.Silu).then_inc(S["a_silu"], 1)

                def z():
                    act.wait_ge(S["slab_used"], 4 * h + 4)
                    A(mix[:, bass.ds(h, 1), :].rearrange("p o t -> p (o t)"), B[1][:], ACT.Silu).then_inc(S["z_done"], 1)

                I = lambda f, *x: f(*x) if inv else None
                C = lambda f, *x: f(*x) if chain else None
                H = lambda f, *x: f(*x) if dense == "head" else None

                def tap_(t):
                    if dense == "head":
                        tap(t)
                    elif dense == "bc":
                        conv_tap(t)

                def silu_(t):
                    if dense == "head":
                        silu(t)
                    elif dense == "bc":
                        bc_silu(t)

                def W(j):
                    if dense == "head":
                        w_cut(S_GDN // 4 + h + 1, j)
                    elif dense == "bc":
                        w_cut(S_XZ // 4, j)

                I(eg_); I(ss); C(v, 0); I(dt); I(q2); I(rinv)
                if dense == "xz":
                    conv_tap(3)
                    w_cut(S_XZ // 4, 3)
                C(v, 1); I(m_, 0)
                if dense == "xz":
                    bc_silu(3)
                    b_copy()
                I(x_, 1); C(v, 2); tap_(0)
                if not inv and not chain:
                    gate_exp()
                I(x_, 2); I(m_, 1); W(0)
                I(x_, 3); I(m_, 2); C(v, 3); tap_(1); C(o2)
                if dense == "xz":
                    x0_tap()
                I(x_, 4); I(m_, 3); W(1); C(rf); silu_(0)
                I(x_, 5); I(m_, 4); silu_(1)
                if not inv and not chain:
                    act.wait_ge(S["gT_tr"], 1)
                    A(gT_hi[:], B[7][0:HEADS, :], ACT.Copy).then_inc(S["gT_hi_ok"], 1)
                tap_(2); W(2)
                I(x_, 6); I(m_, 5); silu_(2); H(z)
                if dense == "head":
                    W(3)

            def b_copy():
                act.wait_ge(S["d_qd"], HG)
                act.wait_ge(S["d_kb"], HG)
                for g in range(GROUPS):
                    act.wait_ge(S["pb_tr"], g + 1)
                    A(b_tok[:, g, :], B[2 + g][:], ACT.Copy).then_inc(S["ab_tok"], 1)

            def x0_tap():
                act.wait_ge(S["slab_used"], S_XZ + 1)
                act.wait_ge(S["as_silu"], 3)
                A(cacc[:, 0, :], B[0][:], ACT.Copy, scale=cw_s[:, 3 * 12:3 * 12 + 1]).then_inc(S["as_tap"], 1)

            def conv_tap(n):
                act.wait_ge(S["slab_used"], S_BC + n + 1)
                need(act, S["as_silu"], n - 1)
                A(cacc[:, n % 2, :], B[n % 2][:], ACT.Copy, scale=cw_s[:, 3 * 12 + 8 + n:3 * 12 + 9 + n]).then_inc(S["as_tap"], 1)

            def bc_silu(n):
                act.wait_ge(S["ds_tap"], 3 * n + 3)
                A(bcA[:, n, :], cacc[:, n % 2, :], ACT.Silu, bias=vec[:, V_CB + 8 + n:V_CB + 9 + n]).then_inc(S["as_silu"], 1)

            gdn_iter(0, None, None, 0, "head", False, False)
            gdn_iter(1, 0, None, 1, "head", True, False)
            gdn_iter(2, 1, 0, 0, "head", True, True)
            gdn_iter(3, 2, 1, 1, "head", True, True)
            with act.Fori(2, HG // 2) as i:
                gdn_iter(2 * i, 2 * i - 1, 2 * i - 2, 0, "head", True, True)
                gdn_iter(2 * i + 1, 2 * i, 2 * i - 1, 1, "head", True, True)
            gdn_iter(None, HG - 1, HG - 2, 0, "bc", True, True)
            gdn_iter(None, None, HG - 1, 1, "xz", False, True)

            act.wait_ge(S["mix_done"], HG)
            def out_hi(i, j):
                k = 4 * i + j
                tile_hi(S_OUT, i, j, lambda k: mix[:, k, :], None if k < HG else vec[:, V_NW + k - HG:V_NW + k - HG + 1])

            def ssd_iter(j, i, par, dense, ssd_, ring=None):
                pi = 1 - par

                def eg_(hh):
                    act.wait_ge(S["ps_g"], 2 * i + hh + 1)
                    need(act, S["ps_y"], i)
                    A(egS[:, hh, :], (B[7], B[2])[hh][:], ACT.Exp).then_inc(S["as_eg"], 1)

                def dt(hh):
                    act.wait_ge(S["ps_m"], 2 * i + hh + 1)
                    act.wait_ge(S["ds_cols"], i + 1)
                    need(act, S["ds_sc"], 2 * i)
                    for c in range(TT):
                        m = A(chunk(dtS[:, hh, :], c), chunk((B[7], B[2])[hh], c), ACT.Exp, bias=colS[:, pi, hh, G_NEG, c:c + 1])
                    m.then_inc(S["as_dt"], 1)

                def x():
                    act.wait_ge(S["slab_used"], S_XZ + 2 * j + 1)
                    act.wait_ge(S["ds_cw"], j + 1)
                    act.wait_ge(S["as_silu"], 3 + j)
                    A(cacc[:, par, :], B[0][:], ACT.Copy, scale=cwS[:, par, 3:4]).then_inc(S["as_tap"], 1)

                def silu():
                    act.wait_ge(S["ds_tap"], 3 * (4 + j) + 3)
                    act.wait_ge(S["ds_cw"], j + 1)
                    need(act, S["ps_x"], j - 1)
                    need(act, S["ds_y1"], j - 1)
                    A(xA[:, par, :], cacc[:, par, :], ACT.Silu, bias=cwS[:, par, 4:5]).then_inc(S["as_silu"], 1)

                def z():
                    act.wait_ge(S["slab_used"], S_XZ + 2 * j + 2)
                    A(mix[:, bass.ds(HG + j, 1), :].rearrange("p o t -> p (o t)"), B[1][:], ACT.Silu).then_inc(S["zs_done"], 1)

                def square(k):
                    act.wait_ge(S["ds_mix"], k + 1)
                    need(act, S["ds_sq"], k + 1)
                    A(y_sq, mix[:, bass.ds(HG + k, 1), :].rearrange("p o t -> p (o t)"), ACT.Square).then_inc(S["as_sq"], 1)

                if ssd_ and dense:
                    eg_(0); eg_(1); dt(0); dt(1)
                    if not (isinstance(i, int) and i == 0):
                        square(i - 1)
                elif ssd_:
                    out_hi(0, 0); eg_(0); out_hi(0, 1); eg_(1); out_hi(0, 2); dt(0); dt(1); out_hi(0, 3)
                    square(i - 1)
                    square(i)
                if dense and ssd_:
                    x()
                if dense:
                    w_cut(ring + 1, 2 * par); silu(); z(); w_cut(ring + 1, 2 * par + 1)

            ssd_iter(0, None, 0, True, False, S_XZ // 4)
            ssd_iter(1, 0, 1, True, True, S_XZ // 4)
            with act.Fori(1, XT // 2) as q:
                ssd_iter(2 * q, 2 * q - 1, 0, True, True, S_XZ // 4 + q)
                ssd_iter(2 * q + 1, 2 * q, 1, True, True, S_XZ // 4 + q)
            ssd_iter(None, XT - 1, 0, False, True)
            act.wait_ge(S["gn_mean"], 1)
            A(gnS[:, 1], gnS[:, 0], ACT.Sqrt).then_inc(S["gn_root"], 1)
            act.wait_ge(S["ds_mix"], XT)
            for i in range(1, MIX // 4):
                for j in range(4):
                    out_hi(i, j)
            load_row(a["norm2_w"], TT + MT)

            product_norm(N2, 2, S_MEM, h_hi)
            w_cut(S_MEM // 4, 3)

            def mem_item(pos):
                w, i = MEM_ORDER[pos]
                d = mem_made(pos)
                if w != "v":
                    act.wait_ge(S["slab_used"], S_MEM + pos + 1)
                    dst, n = (kmT, M) if w == "k" else (qmT, T)
                    A(dst[:, i, :], B[d % 2][:, 0:n], ACT.Copy).then_inc(S["kq_ok"], 1)
                w_cut(S_MEM // 4 + 1 + pos // 4, pos % 4)

            for pos in range(MEM_FIRST - 2):
                mem_item(pos)
                if pos == 1:
                    norm_hi(N2, TT - 1, h_hi)
                    load_row(a["norm3_w"], 2 * TT + MT)

            def values_out():
                act.wait_ge(S["slab_used"], S_MEM + MEM_FIRST)
                for q, bank in enumerate(B[4:]):
                    A(v_m[:, q // 2, (q % 2) * HALF:(q % 2 + 1) * HALF], bank[:], ACT.Copy).then_inc(S["vm_ok"], 1)

            for hd in range(AH):
                act.wait_ge(S["at_neg"], hd + 1)
                need(act, S["at_tr"], MT * (hd - 1))
                need(act, S["at_rec"], hd - 1)
                for t in range(TT):
                    A(pr[:, hd % 2, t, :], B[2 + t // 2][:, (t % 2) * M:(t % 2 + 1) * M], ACT.Exp,
                      bias=sm[:, hd % 2, 1, t:t + 1], scale=float(HD) ** -0.5,
                      accum_out=sm[:, hd % 2, 2, t:t + 1]).then_inc(S["at_exp"], 1)
                if hd == 0:
                    values_out()
                    mem_item(MEM_FIRST - 2)
                    mem_item(MEM_FIRST - 1)
                for pos in MEM_FILL[hd]:
                    mem_item(pos)
                if hd == 2:
                    act.wait_ge(S["at_o"], 4)
                    for j in range(4):
                        tile_hi(S_WO, 0, j, lambda k: oT[:, k, :])
                for u in range(2):
                    act.wait_ge(S["at_pv"], 2 * hd + u + 1)
                    A(oT[:, 2 * hd + u, :], B[6 + u][:], ACT.Copy).then_inc(S["at_o"], 1)

            act.wait_ge(S["at_o"], 2 * AH)
            for j in range(4):
                tile_hi(S_WO, 1, j, lambda k: oT[:, k, :])
            product_norm(N3, 3, S_UP, h_hi)
            norm_hi(N3, TT - 1, h_hi)
            w_cut(S_UP // 4, 3)
            load_row(a["final_norm_w"], 3 * TT + MT)

            def relu(i, j):
                n = 4 * i + j
                act.wait_ge(S["slab_used"], S_UP + n + 1)
                need(act, S["up_sq"], n - 1)
                A(ur[:, j % 2, :], B[j % 2][:], ACT.Relu).then_inc(S["up_relu"], 1)
                w_cut(S_UP // 4 + i + 1, j)

            for j in range(4):
                relu(0, j)
            with act.Fori(1, FT // 4 - 1) as i:
                for j in range(4):
                    relu(i, j)
            act.wait_ge(S["up_sq"], 4)
            for j in range(4):
                relu(FT // 4 - 1, j)
                tile_hi(S_DOWN, 0, j, lambda k: uT[:, k, :])
            act.wait_ge(S["up_sq"], FT)
            with act.Fori(1, FT // 4) as i:
                for j in range(4):
                    tile_hi(S_DOWN, i, j, lambda k: uT[:, bass.ds(k, 1), :].rearrange("p o t -> p (o t)"))
            for i in range(TT):
                act.wait_ge(S["x_add"], 8 * 4 + 2 * i + 2)
                norm_sq(NF, i, x_res[:, i, :], sq_out[:])
                norm_root(NF, i)

        @block.vector
        def _(dve):
            V = nc.vector
            TTn = V.tensor_tensor

            def norm_mean(batch, i):
                g = batch[1] + i
                st = lambda r: stat[:, r, g:g + 1]
                dve.wait_ge(S["n_sq"], 2 * g + 2)
                TTn(st(2), st(0), st(1), ALU.add).then_inc(S["n_add"], 1)
                dve.wait_ge(S["n_add"], g + 1)
                V.tensor_scalar(st(3), st(2), 1.0 / D, EPS, ALU.mult, ALU.add).then_inc(S["n_mean"], 1)

            def norm_rstd(batch, i):
                g = batch[1] + i
                st = lambda r: stat[:, r, g:g + 1]
                dve.wait_ge(S["n_root"], g + 1)
                V.reciprocal(st(5), st(4)).then_inc(S["n_rstd"], 1)

            def norm_xn(batch, i, src, out_=None, done="n_xn"):
                g = batch[1] + i
                if batch in (N2, N3, NF):
                    norm_mean(batch, i)
                    norm_rstd(batch, i)
                dve.wait_ge(S["n_rstd"], g + 1)
                dve.wait_ge(S["n_row"], 16 * (batch[0] + 1))
                if done == "n_xn":
                    need(dve, S["n_tr"], 2 * g if batch is not N1 else 2 * g - 2)
                V.scalar_tensor_tensor(out=xn[:] if out_ is None else out_, in0=src, scalar=stat[:, 5, g:g + 1], in1=nrow[:],
                                       op0=ALU.mult, op1=ALU.mult).then_inc(S[done], 1)

            def norm_lo(batch, i, d_hi, d_lo):
                g = batch[1] + i
                for f in range(2):
                    dve.wait_ge(S["n_hi"], 2 * g + f + 1)
                    fs, ts = slice(4 * f, 4 * f + 4), slice(i * P, (i + 1) * P)
                    TTn(d_lo[:, fs, ts], B[2 * (i + batch[3]) + f][:].rearrange("p (q t) -> p q t", q=4),
                        d_hi[:, fs, ts].bitcast(F32), ALU.subtract).then_inc(S["n_lo"], 1)

            def tile_lo(c0, i, j, src, scale=None):
                k = 4 * i + j
                dve.wait_ge(S["cut_hi"], c0 + k + 1)
                hi = a_hi[:, j, :].bitcast(F32)
                if scale is None:
                    TTn(a_lo[:, j, :], src(k), hi, ALU.subtract).then_inc(S["cut_lo"], 1)
                else:
                    V.scalar_tensor_tensor(out=a_lo[:, j, :], in0=src(k), scalar=scale, in1=hi,
                                           op0=ALU.mult, op1=ALU.subtract).then_inc(S["cut_lo"], 1)

            def add_residual(seg, s_end, t, scale=None):
                if t < TT - 1:
                    dve.wait_ge(S["row_done"], (TT - 1) * seg + t + 1)
                else:
                    dve.wait_ge(S["slab_used"], s_end)
                for f in range(2):
                    x = x_res[:, t, f * HALF:(f + 1) * HALF]
                    need(dve, S["x_add"], 8 * (seg - 1) + 2 * t + f + 1)
                    if scale is None:
                        TTn(x, x, B[2 * t + f][:], ALU.add).then_inc(S["x_add"], 1)
                    else:
                        V.scalar_tensor_tensor(out=x, in0=B[2 * t + f][:], scalar=scale, in1=x,
                                               op0=ALU.mult, op1=ALU.add).then_inc(S["x_add"], 1)

            def product_norm(batch, seg, s_end, scale=lambda t: None):
                for i in range(TT):
                    add_residual(seg, s_end, i, scale(i))
                    if i == TT - 1:
                        norm_lo(batch, i - 1, h_hi, h_lo)
                    norm_xn(batch, i, x_res[:, i, :])
                    if 0 < i < TT - 1:
                        norm_lo(batch, i - 1, h_hi, h_lo)
                norm_lo(batch, TT - 1, h_hi, h_lo)

            norm_mean(N1, 0)
            for i in range(TT):
                norm_rstd(N1, i)
                norm_xn(N1, i, x0[:, i, :], (xn, xn_b)[i % 2][:])
                if i < TT - 1:
                    norm_mean(N1, i + 1)
                if i:
                    norm_lo(N1, i - 1, h_hi, h_lo)
            dve.wait_ge(S["wsm_hi_ok"], 1)
            TTn(wsm_lo[:], wsm[:], wsm_hi[:].bitcast(F32), ALU.subtract).then_inc(S["wsm_lo_ok"], 1)
            norm_lo(N1, TT - 1, h_hi, h_lo)
            dve.wait_ge(S["rows_tr"], 1)
            V.tensor_copy(cw_g[:], B[2][:, 0:96])
            V.tensor_copy(cw_s[:], B[2][:, 96:144])
            V.tensor_copy(vec[:], B[2][:, 144:144 + VROWS]).then_inc(S["rows_cp"], 1)
            for i in range(MT):
                norm_mean(NM, i)
                norm_rstd(NM, i)
            norm_xn(NM, 0, mx[:, 0, :])

            step = [0]

            def link(ins):
                step[0] += 1
                ins.then_inc(S["gate_dve"], 1)
                dve.wait_ge(S["gate_dve"], step[0])

            def heads(ap):
                return ap.unsqueeze(1).to_broadcast([P, TT, HEADS])

            def kind(k, lo=0, hi=HEADS):
                return gates[:, lo:hi, k, :].rearrange("p h c -> p c h")

            dve.wait_ge(S["gate_mm"], 1)
            V.tensor_copy(graw[:], B[6][0:32, :]).then_inc(S["gate_cp"], 1)
            norm_xn(NM, 1, mx[:, 1, :])
            dve.wait_ge(S["gate_mm"], 2)
            link(V.tensor_copy(gr[:], B[7][:, 0:TT * 32].rearrange("p (c n) -> p c n", c=TT)))
            link(TTn(gt[:, 0], gr[:, :, HG:], heads(brow[:]), ALU.add))
            V.scalar_tensor_tensor(out=gt[:, 1], in0=gt[:, 0], scalar=-1.0, in1=gt[:, 0], op0=ALU.mult, op1=ALU.max).then_inc(S["gate_raw"], 1)
            dve.wait_ge(S["gate_act"], 1)
            link(V.tensor_scalar(gt[:, 3, :, 0:HG], gt[:, 3, :, 0:HG], 1.0, None, ALU.add))
            link(V.reciprocal(kind(G_BETA, 0, HG), gt[:, 3, :, 0:HG]))
            link(V.tensor_scalar(gt[:, 4], gt[:, 2], 2.0, None, ALU.add))
            link(V.reciprocal(gt[:, 4], gt[:, 4]))
            link(TTn(gt[:, 4], gt[:, 4], gt[:, 2], ALU.mult))
            link(TTn(gt[:, 5], gt[:, 4], gt[:, 4], ALU.mult))
            link(V.tensor_scalar(gt[:, 6], gt[:, 5], 1.0 / 15, None, ALU.mult))
            for n in (13, 11, 9, 7, 5, 3):
                link(V.scalar_tensor_tensor(out=gt[:, 6], in0=gt[:, 6], scalar=1.0 / n, in1=gt[:, 5], op0=ALU.add, op1=ALU.mult))
            link(V.scalar_tensor_tensor(out=gt[:, 6], in0=gt[:, 6], scalar=1.0, in1=gt[:, 4], op0=ALU.add, op1=ALU.mult))
            link(V.tensor_scalar(gt[:, 6], gt[:, 6], 2.0, None, ALU.mult))
            link(V.scalar_tensor_tensor(out=gt[:, 7], in0=gt[:, 0], scalar=0.0, in1=gt[:, 6], op0=ALU.max, op1=ALU.add))
            V.tensor_copy(kind(G_BETA, HG), gt[:, 7, :, HG:])
            V.scalar_tensor_tensor(out=gt[:, 5], in0=gt[:, 7], scalar=-1.0, in1=heads(arow[:]),
                                   op0=ALU.mult, op1=ALU.mult).then_inc(S["gate_cs"], 1)
            def gate_tail():
                dve.wait_ge(S["gate_mm"], 3)
                link(V.tensor_copy(gt[:, 8].rearrange("p c h -> p (c h)"), B[7][:, P:P + TT * HEADS]))
                link(V.tensor_copy(gt[:, 9].rearrange("p c h -> p (c h)"), B[7][:, 2 * P:2 * P + TT * HEADS]))
                TTn(gt[:, 0], gt[:, 9], gt[:, 8], ALU.subtract).then_inc(S["gate_raw"], 1)
                dve.wait_ge(S["gate_act"], 2)
                V.tensor_scalar(kind(G_NEG), gt[:, 8], -1.0, None, ALU.mult)
                V.tensor_scalar(kind(G_NEXP), gt[:, 2], -1.0, None, ALU.mult)
                V.tensor_copy(kind(G_DEC), gt[:, 1])
                V.tensor_copy(kind(G_CD), gt[:, 3]).then_inc(S["gates_ok"], 1)
                dve.wait_ge(S["gates_ok"], 1)

            def tap(acc, bank, w, sem_, n0, d):
                if d > 1:
                    dve.wait_ge(sem_, n0 + d - 1)
                V.scalar_tensor_tensor(out=acc[:, d:], in0=bank[:, 0:T - d], scalar=w(TAPS - 1 - d), in1=acc[:, d:],
                                       op0=ALU.mult, op1=ALU.add).then_inc(sem_, 1)

            def gdn_iter(h, a_, b, par, dense, inv, chain):
                pa, pb = 1 - par, par

                def cw():
                    V.tensor_copy(cwB[:, par, :], cw_g[:].rearrange("p (x h) -> p x h", h=HG)[:, :, bass.ds(h, 1)]
                                  .rearrange("p x o -> p (x o)")).then_inc(S["d_cw"], 1)

                def cols():
                    if b is not None:
                        dve.wait_ge(S["d_s"], 3 * b + 3)
                        dve.wait_ge(S["d_r"], 3 * b + 3)
                    V.tensor_copy(selB[:, par:par + 1], cst[0:HEADS, C_ID, bass.ds(h, 1)])
                    V.tensor_copy(colB[:, par, :, :].rearrange("p k c -> p (k c)"),
                                  gates[:, bass.ds(h, 1), :, :].rearrange("p o k c -> p (o k c)")).then_inc(S["d_cols"], 1)

                def ss():
                    dve.wait_ge(S["a_ss"], 4 * a_ + 4)
                    need(dve, S["a_rinv"], a_)
                    V.tensor_scalar(ssA[:, 0, :], ssA[:, 3, :], EPS, None, ALU.add).then_inc(S["d_sse"], 1)
                    dve.wait_ge(S["d_sse"], a_ + 1)
                    V.reciprocal(ssA[:, 2, :], ssA[:, 0, :]).then_inc(S["d_rec"], 1)
                    dve.wait_ge(S["d_rec"], a_ + 1)
                    dve.wait_ge(S["d_cols"], a_ + 1)
                    need(dve, S["a_v"], 4 * (a_ - 1))
                    TTn(br2B[:, pa, 0, :], ssA[:, 2, :], colB[:, pa, G_BETA, :], ALU.mult).then_inc(S["d_br"], 1)
                    dve.wait_ge(S["d_br"], a_ + 1)
                    V.tensor_scalar(br2B[:, pa, 1, :], br2B[:, pa, 0, :], -1.0, None, ALU.mult).then_inc(S["d_nb"], 1)

                def kb():
                    dve.wait_ge(S["a_silu"], 3 * a_ + 2)
                    need(dve, S["pe_o"], a_ - 1)
                    V.tensor_copy(kB[:, pa, :], kA[:]).then_inc(S["d_kb"], 1)

                def qd():
                    dve.wait_ge(S["a_eg"], a_ + 1)
                    TTn(qdB[:, pa, :], qA[:], eg[:], ALU.mult).then_inc(S["d_qd"], 1)

                def kd():
                    dve.wait_ge(S["pe_kt"], a_ + 1)
                    dve.wait_ge(S["a_ss"], 4 * a_ + 4)
                    TTn(kdB[:, pa, :].rearrange("p (c d) -> p c d", c=TT), B[4][:].rearrange("p (c d) -> p c d", c=TT),
                        bcast(colB[:, pa, G_DEC, :], P), ALU.mult).then_inc(S["d_kd"], 1)

                def u():
                    dve.wait_ge(S["pe_kk"], a_ + 1)
                    dve.wait_ge(S["a_dt"], a_ + 1)
                    dve.wait_ge(S["d_nb"], a_ + 1)
                    for c in range(TT):
                        m = V.scalar_tensor_tensor(out=chunk(u_neg, c), in0=chunk(B[2], c), scalar=br2B[:, pa, 1, c:c + 1],
                                                   in1=chunk(dt_, c), op0=ALU.mult, op1=ALU.mult)
                    m.then_inc(S["d_u"], 1)

                def off(l):
                    dve.wait_ge(S["d_u"], a_ + 1)
                    need(dve, S["pe_x"], 6 * a_ + max(l - 2, 0))
                    if l == 2:
                        dve.wait_ge(S["d_n1"], a_ + 1)
                    TTn(u_off[:, l % 2, :].rearrange("p (c t) -> p c t", c=TT), u_neg[:].rearrange("p (c t) -> p c t", c=TT),
                        cst[:, C_MASK + l, :].unsqueeze(1).to_broadcast([P, TT, P]), ALU.mult).then_inc(S["d_off"], 1)

                def n1():
                    dve.wait_ge(S["d_off"], 7 * a_ + 1)
                    need(dve, S["pe_n"], 6 * a_)
                    TTn(nW[:].rearrange("p (c t) -> p c t", c=TT), u_off[:, 0, :].rearrange("p (c t) -> p c t", c=TT),
                        ident.unsqueeze(1).to_broadcast([P, TT, P]), ALU.add).then_inc(S["d_n1"], 1)

                def at():
                    dve.wait_ge(S["pe_kq"], a_ + 1)
                    TTn(atB[:, pa, :], B[3][:], dt_[:], ALU.mult).then_inc(S["d_at"], 1)

                def vb():
                    dve.wait_ge(S["pe_vt"], a_ + 1)
                    dve.wait_ge(S["a_rinv"], a_ + 1)
                    TTn(vB[:, pa, :].rearrange("p (c d) -> p c d", c=TT), B[7][:].rearrange("p (c d) -> p c d", c=TT),
                        bcast(ssA[:, 1, :], P), ALU.mult).then_inc(S["d_v"], 1)

                def m_(l):
                    dve.wait_ge(S["pe_n"], 6 * a_ + l)
                    if l == 1:
                        dve.wait_ge(S["a_m"], 6 * a_ + 1)
                    else:
                        dve.wait_ge(S["d_m"], 6 * a_ + l - 1)
                    even = even_blocks(mW[:], l)
                    TTn(even, even, B[3][:, 0:TT * HP].rearrange("p (b w) -> p b w", w=1 << l), ALU.add).then_inc(S["d_m"], 1)

                def inverse():
                    dve.wait_ge(S["pe_mt"], 7 * a_ + 7)
                    V.tensor_copy(nB[:, pa, :], B[4][:]).then_inc(S["d_inv"], 1)

                def r(c):
                    dve.wait_ge(S["pe_ks"], 3 * b + c)
                    V.scalar_tensor_tensor(out=rR[:], in0=B[5][:, 0:P], scalar=colB[:, pb, G_NEXP, c:c + 1],
                                           in1=chunk(vB[:, pb, :], c), op0=ALU.mult, op1=ALU.add).then_inc(S["d_r"], 1)

                def s(c):
                    dve.wait_ge(S["pe_s"], 3 * b + c + 1)
                    if c == 0:
                        V.tensor_copy(stS[:], B[5][:, 0:P]).then_inc(S["d_s"], 1)
                    else:
                        dve.wait_ge(S["d_s"], 3 * b + c)
                        V.scalar_tensor_tensor(out=stS[:], in0=stS[:], scalar=colB[:, pb, G_CD, c:c + 1], in1=B[5][:, 0:P],
                                               op0=ALU.mult, op1=ALU.add).then_inc(S["d_s"], 1)

                def mixb():
                    return mix[:, bass.ds(b, 1), :].rearrange("p o t -> p (o t)")

                def o2q():
                    dve.wait_ge(S["a_o2"], b + 1)
                    dve.wait_ge(S["a_q2"], b + 1)
                    TTn(sqW[:], sqW[:], q_sqB[:, pb, :], ALU.add).then_inc(S["d_o2q"], 1)

                def oz_():
                    dve.wait_ge(S["a_o2"], b + 1)
                    dve.wait_ge(S["z_done"], b + 1)
                    need(dve, S["mix_done"], b)
                    V.scalar_tensor_tensor(out=oz[:], in0=B[6][:], scalar=vec[:, V_GN:V_GN + 1], in1=mixb(),
                                           op0=ALU.mult, op1=ALU.mult).then_inc(S["d_oz"], 1)

                def fe():
                    dve.wait_ge(S["pe_f"], b + 1)
                    V.tensor_scalar(fW[:, 0, :], B[5][:, 0:TT], EPS * EPS * P, None, ALU.add).then_inc(S["d_fe"], 1)

                def fr():
                    dve.wait_ge(S["a_rf"], b + 1)
                    V.reciprocal(fW[:, 2, :], fW[:, 1, :]).then_inc(S["d_fr"], 1)

                def mx_():
                    dve.wait_ge(S["pe_fb"], b + 1)
                    dve.wait_ge(S["d_oz"], b + 1)
                    TTn(mixb(), oz[:], B[5][:], ALU.mult).then_inc(S["mix_done"], 1)

                def conv(t, d):
                    if dense == "head":
                        if d == 1:
                            dve.wait_ge(S["a_tap"], 3 * h + t + 1)
                        tap(cacc[:, t % 2, :], B[t % 2], lambda x: cwB[:, par, 3 * x + t:3 * x + t + 1], S["d_tap"], 9 * h + 3 * t, d)
                    elif dense == "bc":
                        if d == 1:
                            dve.wait_ge(S["as_tap"], t + 1)
                        tap(cacc[:, t % 2, :], B[t % 2], lambda x: cw_s[:, 12 * x + 8 + t:12 * x + 9 + t], S["ds_tap"], 3 * t, d)

                I = lambda f, *x: f(*x) if inv else None
                C = lambda f, *x: f(*x) if chain else None
                H = lambda f, *x: f(*x) if dense == "head" else None
                H(cw); I(kb); I(qd); I(ss); C(s, 0); I(kd); C(r, 1)
                if dense == "xz":
                    dve.wait_ge(S["as_tap"], 4)
                    for d in range(1, TAPS):
                        tap(cacc[:, 1, :], B[1], lambda x: cw_s[:, 12 * x + 11:12 * x + 12], S["ds_tap"], 9, d)
                I(u); I(off, 0); I(n1); I(at); I(off, 1); C(s, 1)
                I(vb); C(r, 2); I(off, 2); I(m_, 1)
                conv(0, 1); C(s, 2); I(off, 3); I(m_, 2)
                conv(0, 2); C(r, 3); conv(0, 3)
                if not inv and not chain:
                    gate_tail()
                    for i in range(MT):
                        norm_lo(NM, i, m_hi, m_lo)
                I(off, 4); I(m_, 3)
                C(o2q); C(oz_); conv(1, 1); conv(1, 2); I(off, 5); I(m_, 4)
                conv(1, 3); C(fe); C(fr); I(off, 6); I(m_, 5)
                if not inv and not chain:
                    dve.wait_ge(S["gT_hi_ok"], 1)
                    TTn(gT_lo[:], B[7][0:HEADS, :], gT_hi[:].bitcast(F32), ALU.subtract).then_inc(S["gT_lo_ok"], 1)
                if dense == "xz":
                    dve.wait_ge(S["as_tap"], 5)
                    for d in range(1, TAPS):
                        tap(cacc[:, 0, :], B[0], lambda x: cw_s[:, 12 * x:12 * x + 1], S["ds_tap"], 12, d)
                C(mx_); conv(2, 1); I(m_, 6)
                conv(2, 2); H(cols); conv(2, 3); I(inverse)

            gdn_iter(0, None, None, 0, "head", False, False)
            gdn_iter(1, 0, None, 1, "head", True, False)
            gdn_iter(2, 1, 0, 0, "head", True, True)
            gdn_iter(3, 2, 1, 1, "head", True, True)
            with dve.Fori(2, HG // 2) as i:
                gdn_iter(2 * i, 2 * i - 1, 2 * i - 2, 0, "head", True, True)
                gdn_iter(2 * i + 1, 2 * i, 2 * i - 1, 1, "head", True, True)
            gdn_iter(None, HG - 1, HG - 2, 0, "bc", True, True)
            gdn_iter(None, None, HG - 1, 1, "xz", False, True)

            def scan_cols(k, p):
                V.tensor_copy(selS[:, p, :], cst[0:HEADS, C_ID, bass.ds(HG + 2 * k, 2)])
                V.tensor_copy(colS[:, p].rearrange("p u k c -> p (u k c)"),
                              gates[:, bass.ds(HG + 2 * k, 2), :, :].rearrange("p u k c -> p (u k c)")).then_inc(S["ds_cols"], 1)

            def square_sum(k):
                dve.wait_ge(S["as_sq"], k + 1)
                acc = gsq[:, bass.ds(k // 4, 1), :].rearrange("p o t -> p (o t)")
                dve.wait_ge(S["ds_sq"], k + 1)
                TTn(acc, acc, y_sq, ALU.add).then_inc(S["ds_sq"], 1)

            def out_lo(i, j):
                k = 4 * i + j
                tile_lo(0, i, j, lambda k: mix[:, k, :], None if k < HG else vec[:, V_NW + k - HG:V_NW + k - HG + 1])

            def ssd_iter(j, i, par, dense, ssd_):
                pi = 1 - par

                def v3(ap):
                    return ap.rearrange("p (c u d) -> p c u d", c=TT, u=2)

                def hcol(k):
                    x = colS[:, pi, :, k, :].rearrange("p u c -> p c u")
                    return x.unsqueeze(3).to_broadcast([P, TT, 2, HP])

                if dense:
                    V.tensor_copy(cwS[:, par, 0:TAPS], cw_s[:].rearrange("p (x n) -> p x n", n=12)[:, :, bass.ds(j, 1)]
                                  .rearrange("p x o -> p (x o)"))
                    V.tensor_copy(cwS[:, par, 5:6], dcol[:, bass.ds(j, 1)])
                    V.tensor_copy(cwS[:, par, 4:5], vec[:, bass.ds(V_CB + j, 1)]).then_inc(S["ds_cw"], 1)
                def out_lo_(j):
                    if not dense:
                        out_lo(0, j)

                if ssd_:
                    out_lo_(0)
                    g = i // 4
                    need(dve, S["ps_st"], i)
                    V.tensor_copy(b_cur[:], b_tok[:, bass.ds(g, 1), :].rearrange("p o t -> p (o t)")).then_inc(S["ds_bcur"], 1)
                    dve.wait_ge(S["ps_x"], i + 1)
                    dve.wait_ge(S["ds_cols"], i + 1)
                    need(dve, S["ps_y"], i)
                    TTn(v3(xdt[:]), v3(B[3][:]), hcol(G_BETA), ALU.mult).then_inc(S["ds_xdt"], 1)
                    dve.wait_ge(S["ds_xdt"], i + 1)
                    TTn(v3(xdd[:]), v3(xdt[:]), hcol(G_DEC), ALU.mult).then_inc(S["ds_xdd"], 1)
                    out_lo_(1)
                    for hh in range(2):
                        dve.wait_ge(S["as_eg"], 2 * i + hh + 1)
                        TTn(egS[:, hh, :], bcA[:, bass.ds(GROUPS + g, 1), :].rearrange("p o t -> p (o t)"), egS[:, hh, :],
                            ALU.mult).then_inc(S["ds_cd"], 1)
                    out_lo_(2)
                    for hh in range(2):
                        dve.wait_ge(S["as_dt"], 2 * i + hh + 1)
                        TTn(scS[:, hh, :], cb[:, bass.ds(g, 1), :].rearrange("p o t -> p (o t)"), dtS[:, hh, :],
                            ALU.mult).then_inc(S["ds_sc"], 1)
                    out_lo_(3)
                    if not (isinstance(i, int) and i == 0):
                        square_sum(i - 1)
                if dense and ssd_:
                    need(dve, S["as_dt"], 2 * i)
                    need(dve, S["ps_g"], 2 * i)
                    scan_cols(j, par)
                if ssd_:
                    dve.wait_ge(S["ps_st"], i + 1)
                    V.tensor_copy(hst[:, 0, :], B[4][:, 0:P]).then_inc(S["ds_h"], 1)
                    for c in (1, 2):
                        dve.wait_ge(S["ds_h"], 3 * i + c)
                        for hh in range(2):
                            hs = slice(hh * HP, (hh + 1) * HP)
                            m = V.scalar_tensor_tensor(out=hst[:, c, hs], in0=hst[:, c - 1, hs], scalar=colS[:, pi, hh, G_CD, c:c + 1],
                                                       in1=B[4][:, c * P + hh * HP:c * P + (hh + 1) * HP],
                                                       op0=ALU.mult, op1=ALU.add)
                        m.then_inc(S["ds_h"], 1)
                if dense and ssd_:
                    dve.wait_ge(S["as_tap"], 5 + j)
                    for d in range(1, TAPS):
                        tap(cacc[:, par, :], B[0], lambda x: cwS[:, par, x:x + 1], S["ds_tap"], 3 * (4 + j), d)
                if ssd_:
                    dve.wait_ge(S["ps_y"], i + 1)
                    V.scalar_tensor_tensor(out=y1, in0=xA[:, pi, :], scalar=cwS[:, pi, 5:6], in1=B[6][:],
                                           op0=ALU.mult, op1=ALU.add).then_inc(S["ds_y1"], 1)
                    dve.wait_ge(S["ds_y1"], i + 1)
                    dve.wait_ge(S["zs_done"], i + 1)
                    mi = mix[:, bass.ds(HG + i, 1), :].rearrange("p o t -> p (o t)")
                    TTn(mi, y1, mi, ALU.mult).then_inc(S["ds_mix"], 1)

            ssd_iter(0, None, 0, True, False)
            scan_cols(0, 0)
            for g in range(GROUPS):
                dve.wait_ge(S["pb_cb"], g + 1)
                V.tensor_copy(cb[:, g, :], B[4 - 2 * g][:]).then_inc(S["db_cb"], 1)
            dve.wait_ge(S["db_cb"], GROUPS)
            dve.wait_ge(S["ab_tok"], GROUPS)
            V.memset(gsq[:], 0.0).then_inc(S["ds_sq"], 1)
            ssd_iter(1, 0, 1, True, True)
            with dve.Fori(1, XT // 2) as q:
                ssd_iter(2 * q, 2 * q - 1, 0, True, True)
                ssd_iter(2 * q + 1, 2 * q, 1, True, True)
            ssd_iter(None, XT - 1, 0, False, True)
            square_sum(XT - 1)
            dve.wait_ge(S["gn_sum"], 1)
            V.tensor_scalar(gnS[:, 0].rearrange("p g c -> p (g c)"), B[5][:, 0:GROUPS * TT], 1.0 / (4 * P), EPS, ALU.mult, ALU.add).then_inc(S["gn_mean"], 1)
            dve.wait_ge(S["gn_root"], 1)
            V.reciprocal(gnS[:, 2], gnS[:, 1]).then_inc(S["gn_rec"], 1)
            dve.wait_ge(S["gn_rec"], 1)

            for j in range(4):
                out_lo(1, j)
            for j in range(3):
                out_lo(2, j)
            dve.wait_ge(S["xr_in"], 16 * TT)
            for t in range(TT):
                add_residual(0, S_OUT + 8, t)
            out_lo(2, 3)
            for j in range(3):
                out_lo(3, j)
            for t in range(TT):
                add_residual(1, S_OUT + 12, t, gnS[:, 2, 0, t:t + 1])
            out_lo(3, 3)
            product_norm(N2, 2, S_OUT + MIX, lambda t: gnS[:, 2, 1, t:t + 1])

            for hd in range(AH):
                e = hd % 2
                need(dve, S["at_exp"], TT * (hd - 1))
                for u in range(2):
                    dve.wait_ge(S["at_s"], 2 * hd + u + 1)
                    m = V.tensor_reduce(sm[:, e, 0, 2 * u:2 * u + 2], B[2 + u][:].rearrange("p (t m) -> p t m", t=2), AX.X, ALU.max)
                m.then_inc(S["at_max"], 1)
                dve.wait_ge(S["at_max"], hd + 1)
                V.tensor_scalar(sm[:, e, 1, :], sm[:, e, 0, :], -float(HD) ** -0.5, None, ALU.mult).then_inc(S["at_neg"], 1)
                dve.wait_ge(S["at_exp"], TT * (hd + 1))
                V.reciprocal(sm[:, e, 3, :], sm[:, e, 2, :]).then_inc(S["at_rec"], 1)
                dve.wait_ge(S["at_rec"], hd + 1)
                TTn(pr[:, e], pr[:, e], bcast(sm[:, e, 3, :], M), ALU.mult).then_inc(S["at_pn"], 1)
                for mt_ in range(MT):
                    dve.wait_ge(S["at_tr"], MT * hd + mt_ + 1)
                    need(dve, S["at_pv"], 2 * (hd - 1))
                    V.tensor_copy(prT[:, e, mt_, :], B[4 + mt_][:]).then_inc(S["at_prt"], 1)
                if hd == 2:
                    for j in range(4):
                        tile_lo(MIX, 0, j, lambda k: oT[:, k, :])

            for j in range(4):
                tile_lo(MIX, 1, j, lambda k: oT[:, k, :])
            product_norm(N3, 3, S_WO + KT)

            def square(i, j):
                n = 4 * i + j
                dve.wait_ge(S["up_relu"], n + 1)
                TTn(uT[:, bass.ds(n, 1), :].rearrange("p o t -> p (o t)"), ur[:, j % 2, :], ur[:, j % 2, :],
                    ALU.mult).then_inc(S["up_sq"], 1)

            for j in range(4):
                square(0, j)
            with dve.Fori(1, FT // 4 - 1) as i:
                for j in range(4):
                    square(i, j)
            for j in range(4):
                square(FT // 4 - 1, j)
                tile_lo(MIX + KT, 0, j, lambda k: uT[:, k, :])
            with dve.Fori(1, FT // 4) as i:
                for j in range(4):
                    tile_lo(MIX + KT, i, j, lambda k: uT[:, bass.ds(k, 1), :].rearrange("p o t -> p (o t)"))
            for t in range(TT):
                add_residual(4, S_DOWN + FT, t)
                norm_xn(NF, t, x_res[:, t, :], x_res[:, t, :], "fin_y")


PAR_DMAS = 14
N_SLABS = S_END

INPUTS = ["x", "mem", "norm1_w", "w_in", "gdn_conv_w", "gdn_a_log", "gdn_dt_bias", "gdn_norm_w", "ssm_conv_w",
          "ssm_conv_b", "ssm_a_log", "ssm_dt_bias", "ssm_d", "ssm_norm_w", "w_out", "norm2_w", "mem_norm_w",
          "wq_mem", "wk_mem", "wv_mem", "wo_mem", "norm3_w", "w_up", "w_down", "final_norm_w"]


def kernel(**inputs):
    import ml_dtypes
    import concourse.bacc as bacc
    from concourse.bass_utils import run_bass_kernel_spmd

    nc = bacc.Bacc("TRN2", target_bir_lowering=False, num_devices=1)
    arrays, aps = {}, {}
    host = {n: np.ascontiguousarray(inputs[n]) for n in INPUTS}
    host["const"] = constants()
    host["negm"] = neg_mask().astype(ml_dtypes.bfloat16)
    for name, arr in host.items():
        arrays[f"in_{name}"] = arr
        aps[name] = nc.dram_tensor(f"in_{name}", arr.shape, mybir.dt.from_np(arr.dtype), kind="ExternalInput").ap()
    out = nc.dram_tensor("out_0", (1, T, D), F32, kind="ExternalOutput").ap()
    layer(nc, aps, out)
    r = run_bass_kernel_spmd(nc, [arrays], core_ids=[0])
    return r.results[0]["out_0"]
```
